# Optimizing a Trainium2 kernel written in Bass

```python
import math
import jax, jax.numpy as jnp
from jax import lax
import numpy as np

D_MODEL = 1024
BATCH = 1
SEQ = 256
DEPTH = 4

N_MIXERS = 3
EPS = 1e-6
SB_HEAD_DIM = 64
SB_HEADS = D_MODEL // SB_HEAD_DIM
Q_BLOCK = 128
CHUNK = 128
SG_WIDTH = D_MODEL
SG_GROUPS = 8
SG_HEAD_DIM = SG_WIDTH // SG_GROUPS
SSM_GROUP = 16
SSM_GROUPS = D_MODEL // SSM_GROUP
SSM_STATE = 64
DT_MIN = 1e-3
DT_MAX = 1e-1
D_FF = 2816
CONV_K = 3
N_A = (DEPTH + 2) // 3
N_B = (DEPTH + 1) // 3
N_C = DEPTH // 3


def rmsnorm(x, g):
    xf = x.astype(jnp.float32)
    y = xf * lax.rsqrt(jnp.mean(xf * xf, axis=-1, keepdims=True) + EPS) * g.astype(jnp.float32)
    return y.astype(x.dtype)

def stick_breaking_attention(xn, w_qkv, w_o):
    B, L, _ = xn.shape
    qkv = (xn @ w_qkv).reshape(B, L, 3, SB_HEADS, SB_HEAD_DIM).astype(jnp.float32)
    q = qkv[:, :, 0] * (SB_HEAD_DIM ** -0.5)
    k = qkv[:, :, 1]
    v = qkv[:, :, 2]
    blocks = []
    for i in range(L // Q_BLOCK):
        t0 = i * Q_BLOCK
        t1 = t0 + Q_BLOCK
        qb, kb, vb = q[:, t0:t1], k[:, :t1], v[:, :t1]
        z = jnp.einsum('bthd,bshd->bhts', qb, kb)
        t_pos = t0 + jnp.arange(Q_BLOCK)
        s_pos = jnp.arange(t1)
        mask = s_pos[None, :] < t_pos[:, None]
        log_1m = jnp.where(mask, jax.nn.log_sigmoid(-z), 0.0)
        log_w = jax.nn.log_sigmoid(z) + lax.cumsum(log_1m, axis=3, reverse=True) - log_1m
        w = jnp.where(mask, jnp.exp(log_w), 0.0)
        blocks.append(jnp.einsum('bhts,bshd->bthd', w, vb))
    o = jnp.concatenate(blocks, axis=1).reshape(B, L, D_MODEL).astype(xn.dtype)
    return o @ w_o

def chunked_spatial_gating(xn, w_in, v_norm_g, w_s, b_s, w_o):
    B, L, _ = xn.shape
    h = jax.nn.gelu(xn @ w_in)
    u, v = jnp.split(h, 2, axis=-1)
    v = rmsnorm(v, v_norm_g)
    v = v.reshape(B, L // CHUNK, CHUNK, SG_GROUPS, SG_HEAD_DIM)
    w_causal = jnp.tril(w_s)
    sv = jnp.einsum('gts,bcsgd->bctgd', w_causal, v) + b_s.T[:, :, None]
    return (u * sv.reshape(B, L, SG_WIDTH)) @ w_o

def _complex_affine_combine(e1, e2):
    a1r, a1i, b1r, b1i = e1
    a2r, a2i, b2r, b2i = e2
    ar = a2r * a1r - a2i * a1i
    ai = a2r * a1i + a2i * a1r
    br = a2r * b1r - a2i * b1i + b2r
    bi = a2r * b1i + a2i * b1r + b2i
    return (ar, ai, br, bi)

def s5_layer(xn, w_in, lam_re, lam_im, log_dt, b_re, b_im, c_re, c_im, d_skip, w_glu):
    B, L, _ = xn.shape
    u = (xn @ w_in).astype(jnp.float32)
    ug = u.reshape(B, L, SSM_GROUPS, SSM_GROUP)
    lr = jnp.minimum(lam_re.astype(jnp.float32), -1e-4)
    li = lam_im.astype(jnp.float32)
    dt = jnp.exp(log_dt.astype(jnp.float32))[:, None]
    mag = jnp.exp(dt * lr)
    ar = mag * jnp.cos(dt * li)
    ai = mag * jnp.sin(dt * li)
    den = lr * lr + li * li
    coef_re = ((ar - 1.0) * lr + ai * li) / den
    coef_im = (ai * lr - (ar - 1.0) * li) / den
    br32, bi32 = b_re.astype(jnp.float32), b_im.astype(jnp.float32)
    bbar_re = coef_re[..., None] * br32 - coef_im[..., None] * bi32
    bbar_im = coef_re[..., None] * bi32 + coef_im[..., None] * br32
    bu_re = jnp.einsum('gph,blgh->blgp', bbar_re, ug)
    bu_im = jnp.einsum('gph,blgh->blgp', bbar_im, ug)
    a_re = jnp.broadcast_to(ar, (1, L, SSM_GROUPS, SSM_STATE))
    a_im = jnp.broadcast_to(ai, (1, L, SSM_GROUPS, SSM_STATE))
    _, _, xr, xi = lax.associative_scan(_complex_affine_combine, (a_re, a_im, bu_re, bu_im), axis=1)
    y = (jnp.einsum('ghp,blgp->blgh', c_re.astype(jnp.float32), xr)
         - jnp.einsum('ghp,blgp->blgh', c_im.astype(jnp.float32), xi))
    y = y.reshape(B, L, D_MODEL) + d_skip.astype(jnp.float32) * u
    hg = jax.nn.gelu(y).astype(xn.dtype) @ w_glu
    a, g = jnp.split(hg, 2, axis=-1)
    return a * jax.nn.sigmoid(g)

def causal_depthwise_conv(h, w, b):
    L = h.shape[1]
    hp = jnp.pad(h, ((0, 0), (CONV_K - 1, 0), (0, 0)))
    y = hp[:, 0:L] * w[0]
    for kk in range(1, CONV_K):
        y = y + hp[:, kk:kk + L] * w[kk]
    return y + b

def conv_gated_ffn(xn, w_up, conv_w, conv_b, w_down):
    h = causal_depthwise_conv(xn @ w_up, conv_w, conv_b)
    a, g = jnp.split(h, 2, axis=-1)
    return (jax.nn.silu(g) * a) @ w_down

def first_inputs(seed: int = 0) -> dict:
    key = jax.random.key(seed)
    ks = jax.random.split(key, 32)
    f32 = jnp.float32

    def nrm(k, shape, scale):
        return jax.random.normal(k, shape, f32) * scale

    x = nrm(ks[0], (BATCH, SEQ, D_MODEL), 1.0)
    norm_g = 1.0 + nrm(ks[1], (DEPTH, 2, D_MODEL), 0.05)
    final_norm_g = 1.0 + nrm(ks[2], (D_MODEL,), 0.05)
    sb_w_qkv = nrm(ks[3], (N_A, D_MODEL, 3 * D_MODEL), D_MODEL ** -0.5)
    sb_w_o = nrm(ks[4], (N_A, D_MODEL, D_MODEL), D_MODEL ** -0.5)
    sg_w_in = nrm(ks[5], (N_B, D_MODEL, 2 * SG_WIDTH), D_MODEL ** -0.5)
    sg_norm_g = 1.0 + nrm(ks[6], (N_B, SG_WIDTH), 0.05)
    sg_w_s = nrm(ks[7], (N_B, SG_GROUPS, CHUNK, CHUNK), CHUNK ** -0.5)
    sg_b = 1.0 + nrm(ks[8], (N_B, SG_GROUPS, CHUNK), 0.1)
    sg_w_o = nrm(ks[9], (N_B, SG_WIDTH, D_MODEL), SG_WIDTH ** -0.5)
    ssm_w_in = nrm(ks[10], (N_C, D_MODEL, D_MODEL), D_MODEL ** -0.5)
    ssm_lam_re = -0.5 + nrm(ks[11], (N_C, SSM_GROUPS, SSM_STATE), 0.01)
    ssm_lam_im = (jnp.pi * jnp.arange(SSM_STATE, dtype=f32)
                  + nrm(ks[12], (N_C, SSM_GROUPS, SSM_STATE), 0.01))
    ssm_log_dt = jax.random.uniform(ks[13], (N_C, SSM_GROUPS), f32,
                                    minval=math.log(DT_MIN), maxval=math.log(DT_MAX))
    ssm_b_re = nrm(ks[14], (N_C, SSM_GROUPS, SSM_STATE, SSM_GROUP), (2 * SSM_GROUP) ** -0.5)
    ssm_b_im = nrm(ks[15], (N_C, SSM_GROUPS, SSM_STATE, SSM_GROUP), (2 * SSM_GROUP) ** -0.5)
    ssm_c_re = nrm(ks[16], (N_C, SSM_GROUPS, SSM_GROUP, SSM_STATE), SSM_STATE ** -0.5)
    ssm_c_im = nrm(ks[17], (N_C, SSM_GROUPS, SSM_GROUP, SSM_STATE), SSM_STATE ** -0.5)
    ssm_d = nrm(ks[18], (N_C, D_MODEL), 1.0)
    ssm_w_glu = nrm(ks[19], (N_C, D_MODEL, 2 * D_MODEL), D_MODEL ** -0.5)
    ffn_w_up = nrm(ks[20], (DEPTH, D_MODEL, 2 * D_FF), D_MODEL ** -0.5)
    ffn_conv_w = nrm(ks[21], (DEPTH, CONV_K, 2 * D_FF), CONV_K ** -0.5)
    ffn_conv_b = nrm(ks[22], (DEPTH, 2 * D_FF), 0.01)
    ffn_w_down = nrm(ks[23], (DEPTH, D_FF, D_MODEL), D_FF ** -0.5)
    return {
        "x": x, "norm_g": norm_g, "final_norm_g": final_norm_g,
        "sb_w_qkv": sb_w_qkv, "sb_w_o": sb_w_o,
        "sg_w_in": sg_w_in, "sg_norm_g": sg_norm_g, "sg_w_s": sg_w_s, "sg_b": sg_b, "sg_w_o": sg_w_o,
        "ssm_w_in": ssm_w_in, "ssm_lam_re": ssm_lam_re, "ssm_lam_im": ssm_lam_im,
        "ssm_log_dt": ssm_log_dt, "ssm_b_re": ssm_b_re, "ssm_b_im": ssm_b_im,
        "ssm_c_re": ssm_c_re, "ssm_c_im": ssm_c_im, "ssm_d": ssm_d, "ssm_w_glu": ssm_w_glu,
        "ffn_w_up": ffn_w_up, "ffn_conv_w": ffn_conv_w, "ffn_conv_b": ffn_conv_b,
        "ffn_w_down": ffn_w_down,
    }

def first_block(x, norm_g, final_norm_g, sb_w_qkv, sb_w_o, sg_w_in, sg_norm_g, sg_w_s, sg_b, sg_w_o,
              ssm_w_in, ssm_lam_re, ssm_lam_im, ssm_log_dt, ssm_b_re, ssm_b_im, ssm_c_re, ssm_c_im,
              ssm_d, ssm_w_glu, ffn_w_up, ffn_conv_w, ffn_conv_b, ffn_w_down):
    for i in range(DEPTH):
        mixer = i % N_MIXERS
        j = i // N_MIXERS
        xn = rmsnorm(x, norm_g[i, 0])
        if mixer == 0:
            m = stick_breaking_attention(xn, sb_w_qkv[j], sb_w_o[j])
        elif mixer == 1:
            m = chunked_spatial_gating(xn, sg_w_in[j], sg_norm_g[j], sg_w_s[j], sg_b[j], sg_w_o[j])
        else:
            m = s5_layer(xn, ssm_w_in[j], ssm_lam_re[j], ssm_lam_im[j], ssm_log_dt[j],
                         ssm_b_re[j], ssm_b_im[j], ssm_c_re[j], ssm_c_im[j], ssm_d[j], ssm_w_glu[j])
        x = x + m.astype(x.dtype)
        f = conv_gated_ffn(rmsnorm(x, norm_g[i, 1]), ffn_w_up[i], ffn_conv_w[i], ffn_conv_b[i],
                           ffn_w_down[i])
        x = x + f.astype(x.dtype)
    return rmsnorm(x, final_norm_g)


DEPTH_2 = 1

GRID_W = 64
CTX_LEN = 256
ROPE_THETA = 10000.0
V_HEAD_DIM = 128
QK_NOPE_DIM = 128
QK_ROPE_DIM = 64
Q_LORA_RANK = 256
KV_LORA_RANK = 256
MLA_HEADS = D_MODEL // (2 * V_HEAD_DIM)
MLA_WIDTH = MLA_HEADS * V_HEAD_DIM
QK_HEAD_DIM = QK_NOPE_DIM + QK_ROPE_DIM
HGRN_KEY_DIM = 128
HGRN_VAL_DIM = 128
HGRN_HEADS = D_MODEL // (2 * HGRN_VAL_DIM)
HGRN_WIDTH = HGRN_HEADS * HGRN_KEY_DIM
CHUNK_2 = 64
MIX_WIDTH = MLA_WIDTH + HGRN_HEADS * HGRN_VAL_DIM
IN_SIZES = (Q_LORA_RANK, KV_LORA_RANK, QK_ROPE_DIM,
            HGRN_WIDTH, HGRN_WIDTH, HGRN_WIDTH, HGRN_WIDTH, HGRN_WIDTH)
IN_COLS = sum(IN_SIZES)
D_FF_2 = -(-8 * D_MODEL // (3 * 256)) * 256


def rmsnorm_2(x, g):
    x32 = x.astype(jnp.float32)
    y = x32 * lax.rsqrt(jnp.mean(x32 * x32, axis=-1, keepdims=True) + EPS)
    return (y * g.astype(jnp.float32)).astype(x.dtype)

def modulate(h, shift, scale):
    return h * (1.0 + scale) + shift

def axial_rope_2d(n):
    rows = n // GRID_W
    row = jnp.broadcast_to(jnp.arange(rows)[:, None], (rows, GRID_W)).reshape(n)
    col = jnp.broadcast_to(jnp.arange(GRID_W)[None, :], (rows, GRID_W)).reshape(n)
    axis_dim = QK_ROPE_DIM // 2
    inv = 1.0 / (ROPE_THETA ** (jnp.arange(0, axis_dim, 2, dtype=jnp.float32) / axis_dim))
    ang = jnp.concatenate([row.astype(jnp.float32)[:, None] * inv,
                           col.astype(jnp.float32)[:, None] * inv], axis=-1)
    return jnp.cos(ang), jnp.sin(ang)

def apply_rope(x, cos, sin):
    if x.ndim == 4:
        cos, sin = cos[:, None, :], sin[:, None, :]
    nf = QK_ROPE_DIM // 4
    x32 = x.astype(jnp.float32)
    outs = []
    for a in range(2):
        xa = x32[..., a * 2 * nf:(a + 1) * 2 * nf]
        c, s = cos[..., a * nf:(a + 1) * nf], sin[..., a * nf:(a + 1) * nf]
        x1, x2 = xa[..., :nf], xa[..., nf:]
        outs.append(jnp.concatenate([x1 * c - x2 * s, x2 * c + x1 * s], axis=-1))
    return jnp.concatenate(outs, axis=-1).astype(x.dtype)

def attend_blocks(q, k, v):
    B, N, H, dq = q.shape
    nb = N // Q_BLOCK
    scale = 1.0 / float(np.sqrt(dq))
    qb = jnp.moveaxis(q.reshape(B, nb, Q_BLOCK, H, dq), 1, 0)

    def one(qblk):
        s = jnp.einsum('bqhd,bkhd->bhqk', qblk, k).astype(jnp.float32) * scale
        p = jax.nn.softmax(s, axis=-1).astype(v.dtype)
        return jnp.einsum('bhqk,bkhd->bqhd', p, v)

    o = lax.map(one, qb)
    return jnp.moveaxis(o, 0, 1).reshape(B, N, H, v.shape[-1])

def gla_chunked(q, k, v, log_f, s0):
    B, T, H, dk = q.shape
    dv = v.shape[-1]
    nc = T // CHUNK_2

    def to_chunks(t):
        return jnp.moveaxis(t.reshape(B, nc, CHUNK_2, H, t.shape[-1]), 1, 0)

    mask = jnp.tril(jnp.ones((CHUNK_2, CHUNK_2), dtype=bool))

    def step(S, inp):
        qc, kc, vc, gc = inp
        b = jnp.cumsum(gc, axis=1)
        b_ref = b[:, CHUNK_2 // 2 - 1][:, None]
        b_last = b[:, -1]
        o_inter = jnp.einsum('bchk,bhkv->bchv', qc * jnp.exp(b), S)
        A = jnp.einsum('bthk,bshk->bhts', qc * jnp.exp(b - b_ref), kc * jnp.exp(b_ref - b))
        A = jnp.where(mask, A, 0.0)
        o_intra = jnp.einsum('bhts,bshv->bthv', A, vc)
        S_new = jnp.exp(b_last)[..., None] * S + jnp.einsum(
            'bshk,bshv->bhkv', kc * jnp.exp(b_last[:, None] - b), vc)
        return S_new, o_inter + o_intra

    s_fin, o = lax.scan(step, s0, (to_chunks(q), to_chunks(k), to_chunks(v), to_chunks(log_f)))
    return s_fin, jnp.moveaxis(o, 0, 1).reshape(B, T, H, dv)

def scan_direction(q, k, v, log_f, s0, reverse):
    if reverse:
        q, k, v, log_f = (jnp.flip(t, axis=1) for t in (q, k, v, log_f))
    s_fin, o = gla_chunked(q, k, v, log_f, s0)
    if reverse:
        o = jnp.flip(o, axis=1)
    return s_fin, o

def token_mixer(h_lat, h_ctx, cos, sin, layer, w_in, g_qn, w_uq, g_kvn, w_ukv,
                lb_fwd, lb_bwd, g_on, w_out, with_ctx_out):
    B, N, _ = h_lat.shape
    L = h_ctx.shape[1]
    offs = [int(v) for v in np.cumsum(IN_SIZES)[:-1]]
    cq_l, ckv_l, kpe_l, hq_l, hi_l, hg_l, ff_l, fb_l = jnp.split(h_lat @ w_in, offs, axis=-1)
    cq_c, ckv_c, kpe_c, hq_c, hi_c, hg_c, ff_c, fb_c = jnp.split(h_ctx @ w_in, offs, axis=-1)

    def mla_q(cq, n):
        q = (rmsnorm_2(cq, g_qn) @ w_uq).reshape(B, n, MLA_HEADS, QK_HEAD_DIM)
        return q[..., :QK_NOPE_DIM], q[..., QK_NOPE_DIM:]

    def mla_kv(ckv, n):
        kv = (rmsnorm_2(ckv, g_kvn) @ w_ukv).reshape(B, n, MLA_HEADS, QK_NOPE_DIM + V_HEAD_DIM)
        return kv[..., :QK_NOPE_DIM], kv[..., QK_NOPE_DIM:]

    def full_k(k_nope, k_pe, n):
        k_pe = jnp.broadcast_to(k_pe[:, :, None, :], (B, n, MLA_HEADS, QK_ROPE_DIM))
        return jnp.concatenate([k_nope, k_pe], axis=-1)

    qn_l, qr_l = mla_q(cq_l, N)
    q_lat = jnp.concatenate([qn_l, apply_rope(qr_l, cos, sin)], axis=-1)
    kn_l, v_l = mla_kv(ckv_l, N)
    k_lat = full_k(kn_l, apply_rope(kpe_l, cos, sin), N)
    kn_c, v_c = mla_kv(ckv_c, L)
    k_ctx = full_k(kn_c, kpe_c, L)
    K = jnp.concatenate([k_ctx, k_lat], axis=1)
    V = jnp.concatenate([v_c, v_l], axis=1)
    o_mla_lat = attend_blocks(q_lat, K, V).reshape(B, N, MLA_WIDTH)

    def heads(t, n):
        return t.astype(jnp.float32).reshape(B, n, HGRN_HEADS, HGRN_KEY_DIM)

    def gates(fraw, lb_tab, n):
        lb = jnp.cumsum(jax.nn.softmax(lb_tab.astype(jnp.float32), axis=0), axis=0)[layer]
        f = lb + (1.0 - lb) * jax.nn.sigmoid(fraw.astype(jnp.float32))
        return heads(1.0 - f, n), heads(jnp.log(f), n)

    s0 = jnp.zeros((B, HGRN_HEADS, HGRN_KEY_DIM, HGRN_VAL_DIM), jnp.float32)
    q_hl, v_hl = heads(hq_l, N), heads(hi_l, N)
    q_hc, v_hc = heads(hq_c, L), heads(hi_c, L)
    o_h_lat = 0.0
    o_h_ctx = 0.0
    for fr_l, fr_c, lb_tab, rev in ((ff_l, ff_c, lb_fwd, False), (fb_l, fb_c, lb_bwd, True)):
        k_c, lf_c = gates(fr_c, lb_tab, L)
        s_ctx, o_c = scan_direction(q_hc, k_c, v_hc, lf_c, s0, rev)
        k_l, lf_l = gates(fr_l, lb_tab, N)
        _, o_l = scan_direction(q_hl, k_l, v_hl, lf_l, s_ctx, rev)
        o_h_lat = o_h_lat + o_l
        o_h_ctx = o_h_ctx + o_c

    def hgrn_out(o, hg, n):
        o = rmsnorm_2(o, g_on).astype(hg.dtype).reshape(B, n, HGRN_HEADS * HGRN_VAL_DIM)
        return o * jax.nn.silu(hg)

    lat_out = jnp.concatenate([o_mla_lat, hgrn_out(o_h_lat, hg_l, N)], axis=-1) @ w_out
    if not with_ctx_out:
        return lat_out, None
    qn_c, qr_c = mla_q(cq_c, L)
    q_ctx = jnp.concatenate([qn_c, qr_c], axis=-1)
    o_mla_ctx = attend_blocks(q_ctx, k_ctx, v_c).reshape(B, L, MLA_WIDTH)
    ctx_out = jnp.concatenate([o_mla_ctx, hgrn_out(o_h_ctx, hg_c, L)], axis=-1) @ w_out
    return lat_out, ctx_out

def swiglu(h, w_gate, w_up, w_down):
    return (jax.nn.silu(h @ w_gate) * (h @ w_up)) @ w_down

def second_inputs(seed: int = 0) -> dict:
    key = jax.random.key(seed)
    ks = jax.random.split(key, 24)

    def nrm(k, shape, scale):
        return jax.random.normal(k, shape, jnp.float32) * scale

    def gain(k, shape):
        return 1.0 + nrm(k, shape, 0.05)

    return {
        "x": nrm(ks[0], (BATCH, SEQ, D_MODEL), 1.0),
        "c": nrm(ks[1], (BATCH, D_MODEL), 1.0),
        "ctx": nrm(ks[2], (BATCH, CTX_LEN, D_MODEL), 1.0),
        "c_ctx": nrm(ks[3], (D_MODEL,), 1.0),
        "w_mod": nrm(ks[4], (DEPTH_2, D_MODEL, 6 * D_MODEL), 0.5 * D_MODEL ** -0.5),
        "b_mod": nrm(ks[5], (DEPTH_2, 6 * D_MODEL), 0.02),
        "g_norm_mix": gain(ks[6], (DEPTH_2, D_MODEL)),
        "g_norm_ffn": gain(ks[7], (DEPTH_2, D_MODEL)),
        "w_in": nrm(ks[8], (DEPTH_2, D_MODEL, IN_COLS), D_MODEL ** -0.5),
        "g_q_norm": gain(ks[9], (DEPTH_2, Q_LORA_RANK)),
        "w_uq": nrm(ks[10], (DEPTH_2, Q_LORA_RANK, MLA_HEADS * QK_HEAD_DIM), Q_LORA_RANK ** -0.5),
        "g_kv_norm": gain(ks[11], (DEPTH_2, KV_LORA_RANK)),
        "w_ukv": nrm(ks[12], (DEPTH_2, KV_LORA_RANK, MLA_HEADS * (QK_NOPE_DIM + V_HEAD_DIM)), KV_LORA_RANK ** -0.5),
        "lb_fwd": nrm(ks[13], (DEPTH_2 + 1, HGRN_WIDTH), 0.1),
        "lb_bwd": nrm(ks[14], (DEPTH_2 + 1, HGRN_WIDTH), 0.1),
        "g_hgrn_norm": gain(ks[15], (DEPTH_2, HGRN_VAL_DIM)),
        "w_out": nrm(ks[16], (DEPTH_2, MIX_WIDTH, D_MODEL), MIX_WIDTH ** -0.5),
        "w_gate": nrm(ks[17], (DEPTH_2, D_MODEL, D_FF_2), D_MODEL ** -0.5),
        "w_up": nrm(ks[18], (DEPTH_2, D_MODEL, D_FF_2), D_MODEL ** -0.5),
        "w_down": nrm(ks[19], (DEPTH_2, D_FF_2, D_MODEL), D_FF_2 ** -0.5),
        "g_final": gain(ks[20], (D_MODEL,)),
    }

def second_block(x, c, ctx, c_ctx, w_mod, b_mod, g_norm_mix, g_norm_ffn, w_in, g_q_norm, w_uq,
              g_kv_norm, w_ukv, lb_fwd, lb_bwd, g_hgrn_norm, w_out, w_gate, w_up, w_down, g_final):
    N = x.shape[1]
    cos, sin = axial_rope_2d(N)
    for layer in range(DEPTH_2):
        mod = jax.nn.silu(c) @ w_mod[layer] + b_mod[layer]
        sh1, sc1, gt1, sh2, sc2, gt2 = jnp.split(mod[:, None, :], 6, axis=-1)
        mod_c = jax.nn.silu(c_ctx) @ w_mod[layer] + b_mod[layer]
        csh1, csc1, cgt1, csh2, csc2, cgt2 = jnp.split(mod_c, 6, axis=-1)
        update_ctx = layer < DEPTH_2 - 1

        h = modulate(rmsnorm_2(x, g_norm_mix[layer]), sh1, sc1)
        hc = modulate(rmsnorm_2(ctx, g_norm_mix[layer]), csh1, csc1)
        mix_lat, mix_ctx = token_mixer(h, hc, cos, sin, layer, w_in[layer], g_q_norm[layer],
                                       w_uq[layer], g_kv_norm[layer], w_ukv[layer],
                                       lb_fwd, lb_bwd, g_hgrn_norm[layer], w_out[layer], update_ctx)
        x = x + gt1 * mix_lat
        h2 = modulate(rmsnorm_2(x, g_norm_ffn[layer]), sh2, sc2)
        x = x + gt2 * swiglu(h2, w_gate[layer], w_up[layer], w_down[layer])
        if update_ctx:
            ctx = ctx + cgt1 * mix_ctx
            hc2 = modulate(rmsnorm_2(ctx, g_norm_ffn[layer]), csh2, csc2)
            ctx = ctx + cgt2 * swiglu(hc2, w_gate[layer], w_up[layer], w_down[layer])
    return rmsnorm_2(x, g_final)


def setup_inputs(seed=0):
    out = dict(first_inputs(seed))
    for name, value in second_inputs(seed + 1).items():
        if name != "x":
            out[name + "_2"] = value
    return out


def reference(
    x, norm_g, final_norm_g, sb_w_qkv, sb_w_o, sg_w_in, sg_norm_g, sg_w_s, sg_b, sg_w_o,
    ssm_w_in, ssm_lam_re, ssm_lam_im, ssm_log_dt, ssm_b_re, ssm_b_im, ssm_c_re, ssm_c_im, ssm_d,
    ssm_w_glu, ffn_w_up, ffn_conv_w, ffn_conv_b, ffn_w_down, c_2, ctx_2, c_ctx_2, w_mod_2,
    b_mod_2, g_norm_mix_2, g_norm_ffn_2, w_in_2, g_q_norm_2, w_uq_2, g_kv_norm_2, w_ukv_2,
    lb_fwd_2, lb_bwd_2, g_hgrn_norm_2, w_out_2, w_gate_2, w_up_2, w_down_2, g_final_2,
):
    x = first_block(
        x, norm_g, final_norm_g, sb_w_qkv, sb_w_o, sg_w_in, sg_norm_g, sg_w_s, sg_b, sg_w_o,
        ssm_w_in, ssm_lam_re, ssm_lam_im, ssm_log_dt, ssm_b_re, ssm_b_im, ssm_c_re, ssm_c_im,
        ssm_d, ssm_w_glu, ffn_w_up, ffn_conv_w, ffn_conv_b, ffn_w_down,
    )
    return second_block(
        x, c_2, ctx_2, c_ctx_2, w_mod_2, b_mod_2, g_norm_mix_2, g_norm_ffn_2, w_in_2,
        g_q_norm_2, w_uq_2, g_kv_norm_2, w_ukv_2, lb_fwd_2, lb_bwd_2, g_hgrn_norm_2, w_out_2,
        w_gate_2, w_up_2, w_down_2, g_final_2,
    )


_drawn_inputs = setup_inputs


def setup_inputs(seed=0):
    import zlib

    import numpy as np

    out = dict(_drawn_inputs(seed))
    spreads = {}
    factors = {'sg_norm_g': 2.915,
     'ssm_lam_re': 8.0,
     'ssm_log_dt': 2.725,
     'ssm_b_re': 3.581,
     'ssm_b_im': 3.573,
     'ssm_c_re': 3.613,
     'ssm_c_im': 3.474,
     'ffn_conv_b': 4.426,
     'ctx_2': 4.007,
     'g_norm_mix_2': 3.686,
     'g_norm_ffn_2': 3.736,
     'g_q_norm_2': 8.0,
     'w_uq_2': 2.977,
     'g_kv_norm_2': 8.0,
     'lb_fwd_2': 7.446,
     'lb_bwd_2': 8.0,
     'g_hgrn_norm_2': 8.0}
    for name, (base, spread) in spreads.items():
        noise = np.random.default_rng([zlib.crc32(name.encode()), seed]).standard_normal(out[name].shape)
        drawn = base * np.exp(spread * noise) if base else spread * noise
        out[name] = __import__('jax').numpy.asarray(drawn.astype(out[name].dtype))
    for name, factor in factors.items():
        out[name] = (out[name] * factor).astype(out[name].dtype)
    return out
```

```python
from contextlib import ExitStack

import numpy as np

import concourse.bass as bass
from concourse import mybir

F32 = mybir.dt.float32
R32 = mybir.dt.float32r
BF16 = mybir.dt.bfloat16
ALU = mybir.AluOpType
ACT = mybir.ActivationFunctionType
AX = mybir.AxisListType

P = 128
T = 256
D = 1024
KT = D // P
EPS = 1e-6
UNIT = 2048
RING = 3
FF = 2816
FT = FF // P
HEADS = 16

PLAN = [("qkv", 12), ("wo", 4), ("ffn", 33), ("sg", 8), ("wo", 4), ("ffn", 33), ("ssm", 4),
        ("mod", 24), ("glu", 8), ("ffn", 33), ("qkv", 12), ("wo", 4), ("ffn", 33),
        ("in2", 14), ("wo", 4), ("ffn", 33)]
STARTS = [sum(n for _, n in PLAN[:i]) for i in range(len(PLAN) + 1)]
UNITS = STARTS[-1]
MOD0, MODN = STARTS[7], 24


def split_index(u):
    return u if u < MOD0 else u - MODN


def unit_of(s):
    return s if s < MOD0 else s + MODN


def quarters(d):
    first, second, whole = slice(0, CH // 2), slice(CH // 2, CH), slice(0, CH)
    return ((first, whole), (second, second)) if d == 0 else ((first, first), (second, whole))


def vector_columns():
    at, n = {}, 0
    for name, k in (("norm_g", 4 * 2 * KT), ("final_norm_g", KT), ("sg_norm_g", KT), ("ssm_d", KT),
                    ("conv", 4 * 2 * FT * 4), ("b_mod", 6 * KT), ("g_mix", KT), ("g_ffn", KT),
                    ("g_q", 2), ("g_kv", 2), ("lb_fwd", 8), ("lb_bwd", 8), ("g_on", 1),
                    ("g_final", KT), ("c", 2 * KT), ("eps", 1),
                    ("lam_re", 32), ("lam_im", 32), ("log_dt", 32)):
        at[name] = n
        n += k
    return at, n


VC, NVEC = vector_columns()
CI, CNU, CNO, CON, CMK, CTR, CRT, CTB, CRO = 0, 128, 256, 384, 512, 640, 768, 832, 896
NCST = 960
QHEADS = 4
NOPE, ROPE = 128, 64
CH = 64
IN0 = STARTS[13]
RAW_USED = (IN0 + 4, IN0 + 5)


class Tally:

    def __init__(self):
        self.u = 0
        self.s = 0
        self.pp = 0
        self.norm = 0
        self.op = 0
        self.up = 0
        self.hid = 0
        self.conv = 0
        self.acc = 0
        self.att = 0
        self.xn = 0
        self.normed = 0
        self.wide = 0


def program(nc, wst, vec, cst, xin, sgw, sgb, sbc, ctxin, ropes, out):
    with ExitStack() as ctx:
        def sb(name, shape, dt=F32):
            return ctx.enter_context(nc.sbuf_tensor(name, shape, dt))

        def sem(name):
            return ctx.enter_context(nc.semaphore(name))

        raw = sb("raw", [P, RING, UNIT])
        whi = sb("whi", [P, RING, UNIT], R32)
        wlo = sb("wlo", [P, RING, UNIT], R32)
        XH = sb("XH", [P, KT, 2 * T], R32)
        XL = sb("XL", [P, KT, 2 * T], R32)
        HH = sb("HH", [P, 2, T], R32)
        HL = sb("HL", [P, 2, T], R32)
        XT = sb("XT", [P, KT, T])
        AR = sb("AR", [P, 20480])
        VEC = sb("VEC", [P, NVEC])
        CST = sb("CST", [P, NCST])
        MKB = sb("MKB", [P, P], BF16)
        IDB = sb("IDB", [P, P], BF16)
        ZB = sb("ZB", [P, 512], BF16)
        SCV = sb("SCV", [P, 2 * KT])
        MODV = sb("MODV", [P, 6 * KT, 2])
        MODG = sb("MODG", [P, 2, KT, 2])
        SM = sb("SM", [P, 512])
        PS = ctx.enter_context(nc.psum_tensor("PS", [P, 8, 512], F32))

        def ar(off, *shape):
            n = int(np.prod(shape))
            v = AR[:, off:off + n]
            if len(shape) == 2:
                return v.rearrange("p (a b) -> p a b", b=shape[1])
            if len(shape) == 3:
                return v.rearrange("p (a b c) -> p a b c", b=shape[1], c=shape[2])
            return v

        ident, negU, negones, ones = (CST[:, o:o + P] for o in (CI, CNU, CNO, CON))
        tril = CST[:, CTR:CTR + P]
        rt = CST[:, CRT:CRT + 64]

        def vcol(name, i):
            return VEC[:, VC[name] + i:VC[name] + i + 1]

        XN = ar(0, KT, T)
        SQ = ar(2048, KT, T)
        CA = ar(4096, 2, 2, T)
        SG = ar(5120, 2, T)
        HID = ar(5632, 2, T)
        RMS = SM[:, 0:T]
        RSTD = SM[:, T:2 * T]
        B0 = 6144
        QK = ar(B0, 2 * KT, T)
        V = ar(B0 + 4096, 2, D)
        ZC = ar(B0 + 6144, 2, 768)
        EX = ar(B0 + 7680, 2, 768)
        LN = ar(B0 + 9216, 2, 768)
        SP = ar(B0 + 10752, 2, 768)
        WB = ar(B0 + 12288, 2, 768)
        GV = ar(B0, 2, D)
        GU = ar(B0 + 2048, KT, T)
        GS = ar(B0 + 4096, KT, T)
        GW = ar(B0 + 6144, 8, P)
        GB = ar(B0 + 7168, 8, P)
        GJ = ar(B0 + 8192, 2, D)

        TC = ar(B0, 32, 64)
        TS = ar(B0 + 2048, 32, 64)
        MG = ar(B0 + 4096, 32, 64)
        U5 = ar(B0 + 6144, KT, T)
        CRE = ar(B0 + 8192, 32, 32)
        CIM = ar(B0 + 9216, 32, 32)
        BRE = ar(B0 + 10240, KT, 2, P)
        BIM = ar(B0 + 12288, KT, 2, P)
        SBC = ar(B0 + 12288, 32, 64)
        PHT = ar(0, 32, 64)
        PHN = ar(2048, 32, 64)
        XBR, XBI = ar(0, 32, 32), ar(1024, 32, 32)
        BT = [ar(2048 + 512 * i, 32, 16) for i in range(4)]
        W5 = [[AR[:, 2560 * a + 512 * i:2560 * a + 512 * i + 512] for i in range(5)] for a in range(2)]

        def s5(i):
            return SM[:, 32 * i:32 * i + 32]
        LR, DT, Z5, E5, MAG, PH, NN, ARE, AIM, DEN, CFR, CFI, T0, T1, JRE, JIM = (s5(i) for i in range(16))

        V2 = ar(0, 4, 512)
        KN = ar(2048, QHEADS, 512)
        CKV = ar(4096, 2, 512)
        CQ = ar(5120, 2, T)
        KPE = ar(5632, 512)
        QN = ar(6144, QHEADS, T)
        QR = ar(7168, QHEADS, T)
        GK = [ar(8192 + 4096 * d, 2, 4, T) for d in range(2)]
        GL = [ar(10240 + 4096 * d, 2, 4, T) for d in range(2)]
        HV = ar(16384, 4, 512)
        HQ = ar(18432, 4, T)
        HG = ar(19456, 4, T)
        CT = ar(8192, KT, T)
        MW = 12288
        CSQ = ar(MW, 2, 512)
        RC = ar(MW + 1024, 512)
        RQ = ar(MW + 1536, T)
        PB = ar(MW, 2, 512)
        PT = ar(MW + 1024, 2, 512)
        RP = ar(MW + 2048, 2, T)
        RT = [AR[0:64, MW + 2560:MW + 3584], AR[0:64, 4096:5120]]
        EQ = [ar(1024 * d, 4, T) for d in range(2)]
        W1, W2, W3 = (AR[:, 2048 + 1024 * i:3072 + 1024 * i] for i in range(3))
        M64 = ar(5120, 1024)
        ST = ar(7168, 2, 4, P)
        ATS = ar(2048, 2, 2, 256)
        KDS = ar(3072, 2, 512)
        QA = [GL[d][:, 1] for d in range(2)]
        KA = [GL[d][:, 0] for d in range(2)]
        MX, NMX, PSM, PRS = (SM[:, 8 * i:8 * i + 8] for i in range(4))
        LBD = SM[:, 32:48].rearrange("p (d h r) -> p d h r", d=2, h=4)
        LBM, LBS, LBV, OML = (SM[:, 48 + 8 * i:56 + 8 * i].rearrange("p (d h) -> p d h", d=2) for i in range(4))
        EL = [SM[:, 80 + 16 * d:96 + 16 * d].rearrange("p (h c) -> p h c", c=4) for d in range(2)]

        names = ["const_in", "x_in", "sg_in", "s5_in", "w_hi", "w_lo", "w_used", "pp_taken", "sq_ready",
                 "norm_sum", "rms_ready", "rstd_ready", "xn_ready", "op_hi", "op_lo", "conv0", "conv1",
                 "silu_ready", "hid_ready", "hh_ready", "hl_ready", "acc_taken", "setup", "zc_ready",
                 "ex_ready", "ln_ready", "sp_ready", "wb_ready", "sc_ready", "c_ready", "o_ready",
                 "qkv_ready", "gv_ready", "gss_ready", "grms_ready", "grstd_ready", "gvn_ready", "mix_ready",
                 "gs_ready", "gu_ready", "gtril", "gy_ready", "glu_sig", "glu_mul", "s5_link", "s5_dt",
                 "s5_angle", "s5_table", "s5_xb", "s5_turned", "s5_b", "bu_ready", "bu_mult", "v_ready", "scan_ready",
                 "rot_ready", "x5_ready", "y5_ready", "y5_sum", "gelu5", "silu_c", "mod_vec", "p_yrs",
                 "ctx_in", "mod_gain", "normed", "wide_taken", "csq", "csum", "crms", "crinv", "cnormed",
                 "kv_part", "q_out", "rot", "roped", "mla_s", "mla_mx", "mla_p", "mla_pn", "mla_t", "mla_pt",
                 "mla_o", "mla_om", "lb_d", "lb_e", "lb_v", "hg_ready", "sig_ready", "f_ready", "lf_ready",
                 "scan_r", "exp_r", "kw_ready", "d1_ready", "e1_ready", "e2_ready", "qk_ready", "kwt", "kwt_out",
                 "s0_sum", "s_ready", "at_sum", "kd_sum", "at_out", "kd_out", "su_sum", "h_out", "h_sq", "h_sum",
                 "h_rms", "h_y"]
        S = {n: sem(n) for n in names}
        w_loaded = [sem(f"w_loaded{i}") for i in range(RING)]
        block = ctx.enter_context(nc.Block())

        @block.sync
        def _(sp):
            sp.dma_start(VEC[:, :], vec).then_inc(S["const_in"], 16)
            sp.dma_start(CST[:, :], cst).then_inc(S["const_in"], 16)
            sp.dma_start(XT[:, :, :], xin).then_inc(S["x_in"], 16)
            for u in range(RING):
                sp.dma_start(raw[:, u, :], wst[u]).then_inc(w_loaded[u], 16)

            def load(u0, j, it=None):
                u = u0 + j
                before = u - RING
                step = 0 if it is None else it * RING
                if MOD0 <= before < MOD0 + MODN:
                    sp.wait_ge(S["w_used"], before + 1 + step)
                else:
                    sp.wait_ge(S["w_lo"], split_index(before) + 1 + step)
                    if before in RAW_USED:
                        sp.wait_ge(S["w_used"], before + 1)
                src = wst[u] if it is None else wst[bass.ds(u + step, 1)].squeeze(0)
                sp.dma_start(raw[:, u % RING, :], src).then_inc(w_loaded[u % RING], 16)

            def loads(u0, u1):
                n = (u1 - u0) // RING if not any(u0 <= u + RING < u1 for u in RAW_USED) else 0
                if n > 1:
                    with sp.Fori(0, n) as it:
                        for j in range(RING):
                            load(u0, j, it)
                    u0 += n * RING
                for u in range(u0, u1):
                    load(u, 0)

            cuts = [RING, MOD0 + RING, MOD0 + MODN + RING, IN0 + RING, IN0 + RING + 12, UNITS + 1]
            for a, b in zip(cuts, cuts[1:]):
                loads(a, b)
            sp.wait_ge(S["normed"], 2 * KT)
            sp.dma_start(out, XT[:, :, :]).then_inc(S["x_in"], 16)
            sp.wait_ge(S["x_in"], 32)

        def limit(u):
            return MOD0 if u < MOD0 else split_index(UNITS)

        @block.scalar
        def _(act):
            t = Tally()

            def split_hi(s, it=None):
                u, r = unit_of(s), s % RING
                step = 0 if it is None else it
                act.wait_ge(w_loaded[u % RING], 16 * (u // RING + 1) + 16 * step)
                if s >= RING:
                    act.wait_ge(S["w_used"], unit_of(s - RING) + 1 + RING * step)
                act.activation(whi[:, r, :], raw[:, u % RING, :], ACT.Copy).then_inc(S["w_hi"], 1)

            def ahead(u):
                while t.s < limit(u) and t.s <= split_index(u) + 2:
                    split_hi(t.s)
                    t.s += 1

            def used(u, step=0):
                act.wait_ge(S["w_used"], u + 1 + step)

            def squares(ready, src=XT):
                for mp in range(4):
                    ready(mp)
                    act.activation(SQ[:, 2 * mp:2 * mp + 2, :], src[:, 2 * mp:2 * mp + 2, :], ACT.Square)\
                        .then_inc(S["sq_ready"], 1)

            def rms():
                act.wait_ge(S["norm_sum"], t.norm + 1)
                act.activation(RMS, PS[:, 6, 0:T], ACT.Sqrt, bias=vcol("eps", 0), scale=1.0 / D)\
                    .then_inc(S["rms_ready"], 1)
                t.norm += 1

            def norm(shift=None, at=0):
                rms()
                for k in range(KT):
                    act.wait_ge(S["xn_ready"], t.xn + 1)
                    t.xn += 1
                    if shift is None:
                        act.activation(XH[:, k, at:at + T], XN[:, k, :], ACT.Copy).then_inc(S["op_hi"], 1)
                    else:
                        sh = MODV[:, shift[0] + k, shift[1]:shift[1] + 1]
                        act.activation(XH[:, k, at:at + T], XN[:, k, :], ACT.Identity, bias=sh)\
                            .then_inc(S["op_hi"], 1)
                t.op += KT

            def norm_stream():
                rms()
                def ready(mp):
                    act.wait_ge(S["normed"], t.normed + 2 * mp + 2)
                squares(ready)
                t.normed += KT

            def residual():
                def ready(mp):
                    ahead(t.u)
                    act.wait_ge(S["pp_taken"], t.pp + 1)
                    t.pp += 1
                    t.u += 1
                squares(ready)

            def ffn(layer, conv=True, aside=None):
                u0, q0, up0, hid0 = t.u, t.pp, t.up, t.hid

                def up(j, it=None):
                    k = 0 if it is None else it
                    u = u0 + 2 + 3 * (j // 2 - 1) + j % 2 if j >= 2 else u0 + j
                    act.wait_ge(S["w_used"], u + 1 + 3 * k)
                    if conv:
                        for i in range(2):
                            c = VC["conv"] + (layer * FT + j) * 8 + 4 * i
                            w2 = VEC[:, c + 2:c + 3] if it is None else VEC[:, bass.ds(it * 16 + c + 2, 1)]
                            cb = VEC[:, c + 3:c + 4] if it is None else VEC[:, bass.ds(it * 16 + c + 3, 1)]
                            a = act.activation(CA[:, j % 2, i, :], PS[:, 4 + (q0 + j) % 2, i * T:(i + 1) * T],
                                               ACT.Identity, bias=cb, scale=w2)
                        a.then_inc(S["conv0"], 1)
                        act.wait_ge(S["pp_taken"], q0 + j + 1 + 2 * k)
                        act.activation(SG[:, j % 2, :], CA[:, j % 2, 1, :], ACT.Silu).then_inc(S["silu_ready"], 1)
                    else:
                        act.activation(SG[:, j % 2, :], PS[:, 4 + (q0 + j) % 2, T:2 * T], ACT.Silu)\
                            .then_inc(S["silu_ready"], 1)

                def hidden(h, it=None):
                    k = 0 if it is None else it
                    act.wait_ge(S["hid_ready"] if conv else S["pp_taken"], (up0 if conv else q0) + 2 * h + 2 + 2 * k)
                    if h > 0:
                        act.wait_ge(S["w_used"], u0 + 2 + 3 * h + 3 * k)
                    act.activation(HH[:, :, :], HID, ACT.Copy).then_inc(S["hh_ready"], 1)

                if not conv:
                    act.preload_act_table(ACT.Silu)
                for j in range(2):
                    ahead(u0 + j)
                    up(j)
                hidden(0)
                if aside:
                    aside()
                n = FT // 2 - 1
                s1 = t.s
                with act.Fori(0, n) as it:
                    for j in range(2):
                        split_hi(s1 + j, it)
                        up(2 + j, it)
                    split_hi(s1 + 2, it)
                    hidden(1, it)
                t.s += 3 * n
                t.u = u0 + 2 + 3 * n
                ahead(t.u)

                def ready(mp):
                    act.wait_ge(S["acc_taken"], t.acc + 1)
                    t.acc += 1
                squares(ready)
                t.u += 1
                t.pp += FT
                t.up += FT
                t.hid += FT // 2

            def attention():
                for n in range(8):
                    ahead(t.u)
                    used(t.u)
                    act.activation(QK[:, 2 * n:2 * n + 2, :],
                                   PS[:, 4 + t.pp % 2, :].rearrange("p (a b) -> p a b", a=2), ACT.Copy,
                                   scale=0.125 if n < 4 else 1.0).then_inc(S["pp_taken"], 1)
                    t.u += 1
                    t.pp += 1
                for n in range(4):
                    ahead(t.u)
                    used(t.u)
                    act.activation(V[:, :, 256 * n:256 * n + 256],
                                   PS[:, 4 + t.pp % 2, :].rearrange("p (a b) -> p a b", a=2), ACT.Copy)\
                        .then_inc(S["pp_taken"], 1)
                    t.u += 1
                    t.pp += 1
                act.preload_act_table_set("natural_log_exp_and_others")
                n0 = t.att
                for p in range(10):
                    if p < 8:
                        act.wait_ge(S["zc_ready"], n0 + p + 1)
                        act.activation(EX[:, p % 2, :], ZC[:, p % 2, :], ACT.Exp).then_inc(S["ex_ready"], 1)
                        act.wait_ge(S["ex_ready"], n0 + p + 1)
                        act.activation(LN[:, p % 2, :], EX[:, p % 2, :], ACT.Ln, bias=1.0)\
                            .then_inc(S["ln_ready"], 1)
                    if 1 <= p < 9:
                        r = (p - 1) % 3
                        act.wait_ge(S["c_ready"], n0 + p)
                        act.activation(WB[:, (p - 1) % 2, :].rearrange("p (a b) -> p a b", a=2),
                                       PS[:, 2 * r:2 * r + 2, 0:384], ACT.Exp).then_inc(S["wb_ready"], 1)
                    if p >= 2:
                        act.wait_ge(S["o_ready"], n0 + p - 1)
                        act.activation(XH[:, p - 2, 0:T], PS[:, 6 + p % 2, 0:T], ACT.Copy)\
                            .then_inc(S["op_hi"], 1)
                t.att += 8
                t.op += KT
                residual()

            def gating():
                for n in range(4):
                    ahead(t.u)
                    used(t.u)
                    act.activation(GV[:, :, 256 * n:256 * n + 256],
                                   PS[:, 4 + t.pp % 2, :].rearrange("p (a b) -> p a b", a=2),
                                   ACT.Gelu_apprx_tanh).then_inc(S["pp_taken"], 1)
                    t.u += 1
                    t.pp += 1
                act.wait_ge(S["gss_ready"], 2)
                act.activation(SM[:, 2:4], SM[:, 0:2], ACT.Sqrt, bias=vcol("eps", 0), scale=1.0 / D)\
                    .then_inc(S["grms_ready"], 1)
                for n in range(4):
                    ahead(t.u)
                    used(t.u)
                    act.activation(GU[:, 2 * n:2 * n + 2, :],
                                   PS[:, 4 + t.pp % 2, :].rearrange("p (a b) -> p a b", a=2),
                                   ACT.Gelu_apprx_tanh).then_inc(S["pp_taken"], 1)
                    t.u += 1
                    t.pp += 1
                for n in range(4):
                    act.wait_ge(S["gy_ready"], n + 1)
                    act.activation(XH[:, 2 * n:2 * n + 2, 0:T], GU[:, 2 * n:2 * n + 2, :], ACT.Copy)\
                        .then_inc(S["op_hi"], 1)
                    t.op += 1
                residual()

            def state_space():
                act.activation(DT, VEC[:, VC["log_dt"]:VC["log_dt"] + 32], ACT.Exp).then_inc(S["s5_dt"], 1)
                for n in range(4):
                    ahead(t.u)
                    used(t.u)
                    act.activation(U5[:, 2 * n:2 * n + 2, :],
                                   PS[:, 4 + t.pp % 2, :].rearrange("p (a b) -> p a b", a=2), ACT.Copy)\
                        .then_inc(S["pp_taken"], 1)
                    t.u += 1
                    t.pp += 1
                    for i, tab in enumerate((TS, TC) if n == 0 else ()):
                        act.wait_ge(S["s5_angle"], i + 1)
                        act.activation(tab, tab, ACT.Sin, scale=6.283185).then_inc(S["s5_table"], 1)
                t.u += MODN
                for c in range(4):
                    act.wait_ge(S["y5_sum"], c + 1)
                    y = U5[:, :, 64 * c:64 * c + 64]
                    act.activation(y, y, ACT.Gelu_apprx_tanh).then_inc(S["gelu5"], 1)
                    act.wait_ge(S["gelu5"], c + 1)
                    act.activation(XH[:, :, 64 * c:64 * c + 64], y, ACT.Copy).then_inc(S["op_hi"], 1)
                t.op += 4

                def ready(mp):
                    for j in (2 * mp, 2 * mp + 1):
                        ahead(t.u)
                        used(t.u)
                        act.activation(SG[:, j % 2, :], PS[:, 4 + t.pp % 2, T:2 * T], ACT.Sigmoid)\
                            .then_inc(S["glu_sig"], 1)
                        t.u += 1
                        t.pp += 1
                    act.wait_ge(S["glu_mul"], 2 * mp + 2)
                ahead(t.u)
                squares(ready)

            def last_mixer():
                def wide(n):
                    return 4 + 2 * (n % 2)

                def taken(dst, src, **kw):
                    act.activation(dst, src, ACT.Copy, **kw).then_inc(S["wide_taken"], 1)
                    t.wide += 1

                def step():
                    ahead(t.u)
                    used(t.u)
                    t.u += 1

                act.wait_ge(S["lb_d"], 1)
                act.activation(LBD, LBD, ACT.Exp).then_inc(S["lb_e"], 1)
                for i, (c, n) in enumerate(((CKV, 512), (CQ, T))):
                    step()
                    b = wide(t.wide)
                    if i == 0:
                        taken(c, PS[:, b:b + 2, :])
                    else:
                        taken(c, PS[:, b, :].rearrange("p (a b) -> p a b", a=2))
                    act.wait_ge(S["wide_taken"], t.wide)
                    if i == 1:
                        act.wait_ge(S["csum"], 1)
                    act.activation(CSQ[:, :, 0:n], c, ACT.Square).then_inc(S["csq"], 1)
                act.activation(RC, PS[:, 0, :], ACT.Sqrt, bias=vcol("eps", 0), scale=1.0 / 256)\
                    .then_inc(S["crms"], 1)
                for i in range(2):
                    step()
                    b = wide(t.wide)
                    taken(HV[:, :, 256 * i:256 * i + 256], PS[:, b:b + 2, :].rearrange("p a (c f) -> p (a c) f", c=2))
                    if i == 0:
                        act.wait_ge(S["csum"], 2)
                        act.activation(RQ, PS[:, 1, 0:T], ACT.Sqrt, bias=vcol("eps", 0), scale=1.0 / 256)\
                            .then_inc(S["crms"], 1)
                step()
                taken(KPE[0:64], PS[0:64, wide(t.wide), :])
                scale = float(NOPE + ROPE) ** -0.5
                act.activation(QN, PS[:, 0:2, :].rearrange("p a (b c) -> p (a b) c", b=2), ACT.Copy, scale=scale)\
                    .then_inc(S["q_out"], 1)
                act.activation(QR[0:64], PS[0:64, 2:4, :].rearrange("p a (b c) -> p (a b) c", b=2), ACT.Copy,
                               scale=scale).then_inc(S["q_out"], 1)
                ahead(t.u)
                for i in range(4):
                    if i < 3:
                        act.wait_ge(S["kv_part"], i + 1)
                    else:
                        used(t.u)
                    b = wide(t.wide)
                    dst = KN if i < 2 else V2
                    taken(dst[:, 2 * (i % 2):2 * (i % 2) + 2, :], PS[:, b:b + 2, :])
                t.u += 1

                def item(i):
                    act.wait_ge(S["mla_mx"], i + 1)
                    if i >= 2:
                        act.wait_ge(S["mla_t"], i - 1)
                    act.activation(PB[:, i % 2, :], PS[:, i % 2, :], ACT.Exp, bias=NMX[:, i:i + 1],
                                   accum_out=PSM[:, i:i + 1]).then_inc(S["mla_p"], 1)

                n = 0
                for i in range(6):
                    step()
                    b = wide(t.wide)
                    if i < 4:
                        dst = HQ if i < 2 else HG
                        taken(dst[:, 2 * (i % 2):2 * (i % 2) + 2, :], PS[:, b, :].rearrange("p (a b) -> p a b", a=2))
                    else:
                        for s in range(2):
                            a = act.activation(GK[0][:, s, 2 * (i % 2):2 * (i % 2) + 2, :],
                                               PS[:, b:b + 2, s * T:(s + 1) * T], ACT.Copy)
                        a.then_inc(S["wide_taken"], 1)
                        t.wide += 1
                    for _ in range(2 if i < 4 else 0):
                        item(n)
                        n += 1
                act.wait_ge(S["mla_om"], 8)
                for i in range(2):
                    step()
                    b = wide(t.wide)
                    for s in range(2):
                        a = act.activation(GK[1][:, s, 2 * i:2 * i + 2, :], PS[:, b:b + 2, s * T:(s + 1) * T], ACT.Copy)
                    a.then_inc(S["wide_taken"], 1)
                    t.wide += 1
                act.activation(HG, HG, ACT.Silu).then_inc(S["hg_ready"], 1)
                for k in range(4):
                    a = act.activation(XH[:, k, 0:T], QN[:, k, :], ACT.Copy)
                a.then_inc(S["op_hi"], 1)
                act.wait_ge(S["wide_taken"], t.wide)
                for d in range(2):
                    act.activation(GK[d], GK[d], ACT.Sigmoid).then_inc(S["sig_ready"], 1)
                act.preload_act_table_set("natural_log_exp_and_others")
                for d in range(2):
                    act.wait_ge(S["f_ready"], d + 1)
                    act.activation(GL[d], GK[d], ACT.Ln).then_inc(S["lf_ready"], 1)
                for d in range(2):
                    act.wait_ge(S["scan_r"], d + 1)
                    act.activation(W1, W1, ACT.Exp).then_inc(S["exp_r"], 1)
                    act.wait_ge(S["d1_ready"], d + 1)
                    act.activation(QA[d].rearrange("p h t -> p (h t)"), W2, ACT.Exp).then_inc(S["e1_ready"], 1)
                    act.activation(EQ[d].rearrange("p h t -> p (h t)"), W1, ACT.Exp).then_inc(S["e1_ready"], 1)
                    last = 0 if d else CH - 1
                    act.activation(EL[d], W1.rearrange("p (h c t) -> p h c t", h=4, c=4)[:, :, :, last], ACT.Exp)\
                        .then_inc(S["e1_ready"], 1)
                    act.wait_ge(S["e1_ready"], 4 * d + 3)
                    act.activation(W2, W2, ACT.Exp, scale=-1.0).then_inc(S["e1_ready"], 1)
                    act.activation(W3, W3, ACT.Exp, scale=-1.0).then_inc(S["e2_ready"], 1)
                act.wait_ge(S["h_out"], 1)
                act.activation(W2, PS[:, 0:2, :].rearrange("p a b -> p (a b)"), ACT.Square).then_inc(S["h_sq"], 1)
                act.wait_ge(S["h_sum"], 1)
                act.activation(W3, PS[:, 2:4, :].rearrange("p a b -> p (a b)"), ACT.Sqrt, bias=vcol("eps", 0),
                               scale=1.0 / P).then_inc(S["h_rms"], 1)
                act.wait_ge(S["h_y"], 3)
                act.activation(XH[:, 4:8, 0:T], W1.rearrange("p (h t) -> p h t", h=4), ACT.Copy)\
                    .then_inc(S["op_hi"], 1)
                t.op += 2

                residual()

            act.wait_ge(S["const_in"], 32)
            act.activation(SCV[:, :], VEC[:, VC["c"]:VC["c"] + 2 * KT], ACT.Silu).then_inc(S["silu_c"], 1)
            ahead(0)
            act.wait_ge(S["x_in"], 16)
            squares(lambda mp: None)
            norm()
            attention()
            norm()
            ffn(0)
            norm()
            act.dma_start(GW, sgw).then_inc(S["sg_in"], 16)
            act.dma_start(GB, sgb).then_inc(S["sg_in"], 16)
            gating()
            norm()
            ffn(1)
            act.dma_start(SBC, sbc).then_inc(S["s5_in"], 16)
            norm()
            state_space()
            norm()
            ffn(2)
            norm()
            attention()
            norm()
            act.dma_start(CT, ctxin).then_inc(S["ctx_in"], 16)
            act.dma_start(RP[0:64], ropes).then_inc(S["ctx_in"], 16)

            def context():
                act.wait_ge(S["ctx_in"], 32)
                squares(lambda mp: None, CT)
                norm((0, 1), T)
            ffn(3, aside=context)
            norm_stream()
            norm((0, 0))
            last_mixer()
            norm((3 * KT, 0))
            ffn(0, conv=False)
            rms()

        @block.vector
        def _(dve):
            t = Tally()

            def split_lo(s, it=None):
                u, r = unit_of(s), s % RING
                step = 0 if it is None else it
                dve.wait_ge(S["w_hi"], s + 1 + RING * step)
                dve.tensor_tensor(wlo[:, r, :], raw[:, u % RING, :], whi[:, r, :].bitcast(F32), ALU.subtract)\
                    .then_inc(S["w_lo"], 1)

            def ahead(u):
                while t.s < limit(u) and t.s <= split_index(u) + 2:
                    split_lo(t.s)
                    t.s += 1

            def used(u):
                dve.wait_ge(S["w_used"], u + 1)

            def low(dst, src, hi, n):
                dve.wait_ge(S["op_hi"], n)
                dve.tensor_tensor(dst, src, hi.bitcast(F32), ALU.subtract).then_inc(S["op_lo"], 1)

            def rstd():
                dve.wait_ge(S["rms_ready"], t.norm + 1)
                dve.reciprocal(RSTD, RMS).then_inc(S["rstd_ready"], 1)
                dve.wait_ge(S["rstd_ready"], t.norm + 1)
                t.norm += 1

            def norm(g, src=XT, shift=None, at=0):
                rstd()
                for k in range(KT + 1):
                    if k < KT:
                        dve.scalar_tensor_tensor(XN[:, k, :], src[:, k, :], g(k), RSTD,
                                                 ALU.mult, ALU.mult).then_inc(S["xn_ready"], 1)
                    if k >= 1:
                        m = k - 1
                        if shift is None:
                            low(XL[:, m, at:at + T], XN[:, m, :], XH[:, m, at:at + T], t.op + k)
                        else:
                            dve.wait_ge(S["op_hi"], t.op + k)
                            sh = MODV[:, shift[0] + m, shift[1]:shift[1] + 1]
                            dve.scalar_tensor_tensor(XL[:, m, at:at + T], XN[:, m, :], sh,
                                                     XH[:, m, at:at + T].bitcast(F32), ALU.add, ALU.subtract)\
                                .then_inc(S["op_lo"], 1)
                t.op += KT

            def norm_stream(name):
                rstd()
                for k in range(KT):
                    dve.scalar_tensor_tensor(XT[:, k, :], XT[:, k, :], vcol(name, k), RSTD, ALU.mult, ALU.mult)\
                        .then_inc(S["normed"], 1)
                t.normed += KT

            def gain(i):
                return lambda k: vcol("norm_g", i * KT + k)

            def mod_gain(i, s):
                return lambda k: MODG[:, i, k, s:s + 1]

            def residual():
                for mp in range(4):
                    ahead(t.u)
                    used(t.u)
                    x = XT[:, 2 * mp:2 * mp + 2, :]
                    dve.tensor_tensor(x, PS[:, 4 + t.pp % 2, :].rearrange("p (a b) -> p a b", a=2), x, ALU.add)\
                        .then_inc(S["pp_taken"], 1)
                    t.u += 1
                    t.pp += 1

            def ffn(layer, conv=True, aside=None):
                u0, q0, up0, hid0 = t.u, t.pp, t.up, t.hid

                def up(j, it=None):
                    k = 0 if it is None else it
                    bank = PS[:, 4 + (q0 + j) % 2, :].rearrange("p (a b) -> p a b", a=2)
                    if conv:
                        dve.wait_ge(S["conv0"], up0 + j + 1 + 2 * k)
                        for back in (1, 2):
                            for i in range(2):
                                c = VC["conv"] + (layer * FT + j) * 8 + 4 * i + 2 - back
                                w = VEC[:, c:c + 1] if it is None else VEC[:, bass.ds(it * 16 + c, 1)]
                                y = CA[:, j % 2, i, back:T]
                                ins = dve.scalar_tensor_tensor(y, bank[:, i, 0:T - back], w, y, ALU.mult, ALU.add)
                            if back == 1:
                                ins.then_inc(S["conv1"], 1)
                                dve.wait_ge(S["conv1"], up0 + j + 1 + 2 * k)
                            else:
                                ins.then_inc(S["pp_taken"], 1)
                        dve.wait_ge(S["silu_ready"], up0 + j + 1 + 2 * k)
                        dve.tensor_tensor(HID[:, j % 2, :], CA[:, j % 2, 0, :], SG[:, j % 2, :], ALU.mult)\
                            .then_inc(S["hid_ready"], 1)
                    else:
                        if j == 2:
                            dve.wait_ge(S["hl_ready"], hid0 + 1 + k)
                        dve.wait_ge(S["silu_ready"], up0 + j + 1 + 2 * k)
                        dve.tensor_tensor(HID[:, j % 2, :], bank[:, 0, :], SG[:, j % 2, :], ALU.mult)\
                            .then_inc(S["pp_taken"], 1)

                def hidden(h, it=None):
                    k = 0 if it is None else it
                    dve.wait_ge(S["hh_ready"], hid0 + h + 1 + k)
                    dve.tensor_tensor(HL[:, :, :], HID, HH[:, :, :].bitcast(F32), ALU.subtract)\
                        .then_inc(S["hl_ready"], 1)

                for j in range(2):
                    ahead(u0 + j)
                    up(j)
                hidden(0)
                if aside:
                    aside()
                n = FT // 2 - 1
                s1 = t.s
                with dve.Fori(0, n) as it:
                    for j in range(2):
                        split_lo(s1 + j, it)
                        up(2 + j, it)
                    split_lo(s1 + 2, it)
                    hidden(1, it)
                t.s += 3 * n
                t.u = u0 + 2 + 3 * n
                ahead(t.u)
                used(t.u)
                for mp in range(4):
                    if conv:
                        x = XT[:, 2 * mp:2 * mp + 2, :]
                        ins = dve.tensor_tensor(x, PS[:, mp, :].rearrange("p (a b) -> p a b", a=2), x, ALU.add)
                    else:
                        for m in (2 * mp, 2 * mp + 1):
                            ins = dve.scalar_tensor_tensor(XT[:, m, :], PS[:, mp, (m % 2) * T:(m % 2 + 1) * T],
                                                           MODV[:, 5 * KT + m, 0:1], XT[:, m, :],
                                                           ALU.mult, ALU.add)
                    ins.then_inc(S["acc_taken"], 1)
                t.acc += 4
                t.u += 1
                t.pp += FT
                t.up += FT
                t.hid += FT // 2

            def attention():
                for n in range(12):
                    ahead(t.u)
                    t.u += 1
                    t.pp += 1
                n0 = t.att
                for p in range(10):
                    r = p % 3
                    if p < 8:
                        dve.wait_ge(S["sc_ready"], n0 + p + 1)
                        z = PS[:, 2 * r:2 * r + 2, 0:384]
                        dve.tensor_scalar(ZC[:, p % 2, :].rearrange("p (a b) -> p a b", a=2), z, 40.0, None,
                                          ALU.min).then_inc(S["zc_ready"], 1)
                        dve.wait_ge(S["ln_ready"], n0 + p + 1)
                        dve.tensor_tensor(SP[:, p % 2, :].rearrange("p (a b) -> p a b", a=2), z,
                                          LN[:, p % 2, :].rearrange("p (a b) -> p a b", a=2), ALU.max)\
                            .then_inc(S["sp_ready"], 1)
                    if p >= 2:
                        low(XL[:, p - 2, 0:T], PS[:, 6 + p % 2, 0:T], XH[:, p - 2, 0:T], t.op + p - 1)
                t.att += 8
                t.op += KT
                residual()

            def gating():
                for n in range(4):
                    ahead(t.u)
                    t.u += 1
                    t.pp += 1
                dve.wait_ge(S["pp_taken"], t.pp)
                dve.wait_ge(S["sg_in"], 32)
                for g in range(8):
                    dve.tensor_tensor(GW[:, g, :], GW[:, g, :], tril, ALU.mult).then_inc(S["gtril"], 1)
                for c in range(2):
                    dve.tensor_tensor_reduce(GJ[:, c, :], GV[:, c, :], GV[:, c, :], 1.0, 0.0, ALU.mult, ALU.add,
                                             SM[:, c:c + 1]).then_inc(S["gss_ready"], 1)
                dve.wait_ge(S["grms_ready"], 1)
                dve.reciprocal(SM[:, 4:6], SM[:, 2:4]).then_inc(S["grstd_ready"], 1)
                dve.wait_ge(S["grstd_ready"], 1)
                for c in range(2):
                    dve.tensor_scalar(GV[:, c, :], GV[:, c, :], SM[:, 4 + c:5 + c], None, ALU.mult)\
                        .then_inc(S["gvn_ready"], 1)
                for n in range(2):
                    ahead(t.u + n)
                for g in range(8):
                    if g % 2 == 0:
                        dve.wait_ge(S["mix_ready"], g // 2 + 1)
                    dve.scalar_tensor_tensor(
                        GS[:, g, :].rearrange("p (c t) -> p c t", c=2),
                        PS[:, g // 2, (g % 2) * T:(g % 2 + 1) * T].rearrange("p (c t) -> p c t", c=2),
                        vcol("sg_norm_g", g), GB[:, g, :].unsqueeze(1).broadcast_to([P, 2, P]),
                        ALU.mult, ALU.add).then_inc(S["gs_ready"], 1)
                for n in range(4):
                    if n >= 2:
                        ahead(t.u)
                    dve.wait_ge(S["pp_taken"], t.pp + 1)
                    dve.wait_ge(S["gs_ready"], 8)
                    gu = GU[:, 2 * n:2 * n + 2, :]
                    dve.tensor_tensor(gu, gu, GS[:, 2 * n:2 * n + 2, :], ALU.mult).then_inc(S["gy_ready"], 1)
                    t.u += 1
                    t.pp += 1
                    if n >= 1:
                        m = 2 * n - 2
                        low(XL[:, m:m + 2, 0:T], GU[:, m:m + 2, :], XH[:, m:m + 2, 0:T], t.op + n)
                low(XL[:, 6:8, 0:T], GU[:, 6:8, :], XH[:, 6:8, 0:T], t.op + 4)
                t.op += 4
                residual()

            links = [0]

            def link(ins):
                links[0] += 1
                ins.then_inc(S["s5_link"], 1)
                dve.wait_ge(S["s5_link"], links[0])

            def discretize():
                big = 12582912.0
                li = VEC[:, VC["lam_im"]:VC["lam_im"] + 32]

                def b64(v):
                    return v.unsqueeze(2).broadcast_to([P, 32, 64])

                def b16(v):
                    return v.unsqueeze(2).broadcast_to([P, 32, 16])
                link(dve.tensor_scalar(LR, VEC[:, VC["lam_re"]:VC["lam_re"] + 32], -1e-4, None, ALU.min))
                dve.wait_ge(S["s5_dt"], 1)
                link(dve.scalar_tensor_tensor(PH, DT, 1.0 / (2 * np.pi), li, ALU.mult, ALU.mult))
                link(dve.tensor_scalar(NN, PH, big, None, ALU.add))
                link(dve.tensor_scalar(NN, NN, big, None, ALU.subtract))
                link(dve.tensor_tensor(PH, PH, NN, ALU.subtract))
                link(dve.tensor_tensor(PHT, b64(PH), rt.unsqueeze(1).broadcast_to([P, 32, 64]), ALU.mult))
                for i, (tab, quarter) in enumerate(((TS, 0.0), (TC, 0.25))):
                    link(dve.tensor_scalar(PHN, PHT, quarter, big, ALU.add, ALU.add))
                    link(dve.tensor_scalar(PHN, PHN, big, None, ALU.subtract))
                    dve.scalar_tensor_tensor(tab, PHT, quarter, PHN, ALU.add, ALU.subtract)\
                        .then_inc(S["s5_angle"], 1)
                    dve.wait_ge(S["s5_angle"], i + 1)
                link(dve.tensor_tensor(Z5, DT, LR, ALU.mult))
                link(dve.tensor_scalar(Z5, Z5, -87.0, 1.0 / 256, ALU.max, ALU.mult))
                link(dve.tensor_scalar(E5, Z5, 1.0 / 7, 1.0, ALU.mult, ALU.add))
                for n in range(6, 1, -1):
                    link(dve.scalar_tensor_tensor(E5, E5, 1.0 / n, Z5, ALU.mult, ALU.mult))
                    link(dve.tensor_scalar(E5, E5, 1.0, None, ALU.add))
                link(dve.tensor_tensor(E5, E5, Z5, ALU.mult))
                for _ in range(8):
                    link(dve.scalar_tensor_tensor(E5, E5, 2.0, E5, ALU.add, ALU.mult))
                link(dve.tensor_scalar(MAG, E5, 1.0, None, ALU.add))
                link(dve.tensor_copy(MG, b64(MAG)))
                link(dve.memset(MG[:, :, 0:1], 0.0))
                dve.wait_ge(S["s5_table"], 2)
                link(dve.tensor_tensor(ARE, MAG, TC[:, :, 1], ALU.mult))
                link(dve.tensor_tensor(AIM, MAG, TS[:, :, 1], ALU.mult))
                link(dve.tensor_tensor(DEN, LR, LR, ALU.mult))
                link(dve.tensor_tensor(T0, li, li, ALU.mult))
                link(dve.tensor_tensor(DEN, DEN, T0, ALU.add))
                link(dve.reciprocal(DEN, DEN))
                link(dve.scalar_tensor_tensor(T0, ARE, -1.0, LR, ALU.add, ALU.mult))
                link(dve.tensor_tensor(T1, AIM, li, ALU.mult))
                link(dve.tensor_tensor(T0, T0, T1, ALU.add))
                link(dve.tensor_tensor(CFR, T0, DEN, ALU.mult))
                link(dve.scalar_tensor_tensor(T0, ARE, -1.0, li, ALU.add, ALU.mult))
                link(dve.tensor_tensor(T1, AIM, LR, ALU.mult))
                link(dve.tensor_tensor(T0, T1, T0, ALU.subtract))
                link(dve.tensor_tensor(CFI, T0, DEN, ALU.mult))
                dve.wait_ge(S["s5_in"], 16)
                link(dve.memset(AR[:, 0:2048], 0.0))
                link(dve.memset(AR[:, B0 + 8192:B0 + 12288], 0.0))
                bre, bim, cre, cim = (SBC[:, :, 16 * i:16 * i + 16] for i in range(4))
                link(dve.tensor_tensor(BT[0], b16(CFR), bre, ALU.mult))
                link(dve.tensor_tensor(BT[1], b16(CFI), bim, ALU.mult))
                link(dve.tensor_tensor(BT[2], b16(CFR), bim, ALU.mult))
                link(dve.tensor_tensor(BT[3], b16(CFI), bre, ALU.mult))
                for g in range(2):
                    r = slice(64 * g, 64 * g + 64)
                    h = slice(16 * g, 16 * g + 16)
                    dve.tensor_tensor(XBR[r, :, h], BT[0][r], BT[1][r], ALU.subtract).then_inc(S["s5_xb"], 1)
                    dve.tensor_tensor(XBI[r, :, h], BT[2][r], BT[3][r], ALU.add).then_inc(S["s5_xb"], 1)
                    link(dve.tensor_copy(CRE[r, :, h], cre[r]))
                    link(dve.tensor_scalar(CIM[r, :, h], cim[r], -1.0, None, ALU.mult))
                link(dve.memset(AR[:, B0 + 12288:B0 + 14336], 0.0))
                link(dve.memset(SM[:, 448:512], 0.0))

            def turned():
                dve.wait_ge(S["s5_turned"], 1)
                for i, b in enumerate((BRE, BIM)):
                    for q in range(4):
                        r = slice(32 * q, 32 * q + 32)
                        dve.tensor_copy(b[r, :, q % 2, :],
                                        PS[r, 2 * i:2 * i + 2, :].rearrange("p a (k n) -> p (a k) n", n=P))\
                            .then_inc(S["s5_b"], 1)

            def state_space():
                for n in range(4):
                    ahead(t.u)
                    if n == 0:
                        discretize()
                    t.u += 1
                    t.pp += 1
                turned()
                t.u += MODN

                def halves(v):
                    return v.rearrange("p (a b) -> p a b", a=2)
                for st in range(18):
                    if st >= 2 and st < 14:
                        s = st - 2
                        qd, wk = s % 4, W5[s % 2]
                        dve.wait_ge(S["x5_ready"], s + 1)
                        xr, xi = (v.rearrange("p (a b) -> p a b", b=64)[:, :, 63] for v in (wk[0], wk[4]))
                        c8 = slice(8 * qd, 8 * qd + 8)
                        link(dve.tensor_tensor(T0[:, c8], ARE[:, c8], xr, ALU.mult))
                        link(dve.tensor_tensor(T1[:, c8], AIM[:, c8], xi, ALU.mult))
                        link(dve.tensor_tensor(JRE[:, c8], T0[:, c8], T1[:, c8], ALU.subtract))
                        link(dve.tensor_tensor(T0[:, c8], ARE[:, c8], xi, ALU.mult))
                        link(dve.tensor_tensor(T1[:, c8], AIM[:, c8], xr, ALU.mult))
                        link(dve.tensor_tensor(JIM[:, c8], T0[:, c8], T1[:, c8], ALU.add))
                    if st < 16:
                        qd, wk, b = st % 4, W5[st % 2], 2 * (st % 2)
                        tc = AR[:, B0 + 512 * qd:B0 + 512 * qd + 512]
                        ts = AR[:, B0 + 2048 + 512 * qd:B0 + 2048 + 512 * qd + 512]
                        dve.wait_ge(S["bu_ready"], st + 1)
                        if st >= 2:
                            dve.wait_ge(S["y5_ready"], st - 1)
                        re, im = PS[:, b:b + 2, 0:T], PS[:, b:b + 2, T:2 * T]
                        dve.tensor_tensor(halves(wk[0]), re, halves(tc), ALU.mult)
                        dve.tensor_tensor(halves(wk[1]), im, halves(ts), ALU.mult)
                        dve.tensor_tensor(halves(wk[2]), im, halves(tc), ALU.mult)
                        dve.tensor_tensor(halves(wk[3]), re, halves(ts), ALU.mult).then_inc(S["bu_mult"], 1)
                    if 1 <= st < 17:
                        s = st - 1
                        qd, wk = s % 4, W5[s % 2]
                        tc = AR[:, B0 + 512 * qd:B0 + 512 * qd + 512]
                        ts = AR[:, B0 + 2048 + 512 * qd:B0 + 2048 + 512 * qd + 512]
                        mg = AR[:, B0 + 4096 + 512 * qd:B0 + 4096 + 512 * qd + 512]
                        dve.wait_ge(S["v_ready"], s + 1)
                        for v, j in ((wk[0], JRE), (wk[2], JIM)):
                            v0 = v.rearrange("p (a b) -> p a b", b=64)[:, :, 0]
                            link(dve.tensor_tensor(v0, v0, j[:, 8 * qd:8 * qd + 8], ALU.add))
                        dve.tensor_tensor_scan(wk[1], mg, wk[0], 0.0, ALU.mult, ALU.add)
                        dve.tensor_tensor_scan(wk[3], mg, wk[2], 0.0, ALU.mult, ALU.add)\
                            .then_inc(S["scan_ready"], 1)
                        dve.wait_ge(S["scan_ready"], s + 1)
                        dve.tensor_tensor(wk[0], wk[1], tc, ALU.mult)
                        dve.tensor_tensor(wk[2], wk[3], ts, ALU.mult).then_inc(S["rot_ready"], 1)
                    if st >= 5 and st % 4 == 1:
                        c = st // 4 - 1
                        tok = slice(64 * c, 64 * c + 64)
                        dve.wait_ge(S["y5_ready"], 4 * c + 4)
                        for k in range(KT):
                            ins = dve.scalar_tensor_tensor(U5[:, k, tok], U5[:, k, tok], vcol("ssm_d", k),
                                                           PS[:, 4 + c % 2, 64 * k:64 * k + 64], ALU.mult, ALU.add)
                        ins.then_inc(S["y5_sum"], 1)
                        low(XL[:, :, tok], U5[:, :, tok], XH[:, :, tok], t.op + c + 1)
                t.op += 4
                dve.wait_ge(S["w_used"], MOD0 + MODN)
                dve.tensor_tensor(MODV[:, :, :], PS[:, 7, 0:96].rearrange("p (a b) -> p a b", b=2),
                                  VEC[:, VC["b_mod"]:VC["b_mod"] + 48].unsqueeze(2).broadcast_to([P, 48, 2]),
                                  ALU.add).then_inc(S["mod_vec"], 1)
                dve.wait_ge(S["mod_vec"], 1)
                for i, name in enumerate(("g_mix", "g_ffn")):
                    sc = MODV[:, (3 * i + 1) * KT:(3 * i + 2) * KT, :]
                    g = VEC[:, VC[name]:VC[name] + KT].unsqueeze(2).broadcast_to([P, KT, 2])
                    dve.scalar_tensor_tensor(MODG[:, i], sc, 1.0, g, ALU.add, ALU.mult).then_inc(S["mod_gain"], 1)
                ahead(t.u)
                for j in range(KT):
                    ahead(t.u)
                    dve.wait_ge(S["glu_sig"], j + 1)
                    dve.tensor_tensor(CA[:, j % 2, 0, :], PS[:, 4 + t.pp % 2, 0:T], SG[:, j % 2, :], ALU.mult)\
                        .then_inc(S["pp_taken"], 1)
                    dve.wait_ge(S["pp_taken"], t.pp + 1)
                    dve.tensor_tensor(XT[:, j, :], XT[:, j, :], CA[:, j % 2, 0, :], ALU.add)\
                        .then_inc(S["glu_mul"], 1)
                    t.u += 1
                    t.pp += 1

            def last_mixer():
                raw_lb = VEC[:, VC["lb_fwd"]:VC["lb_fwd"] + 16].rearrange("p (d h r) -> p d h r", d=2, h=4)
                link(dve.tensor_tensor(LBM, raw_lb[:, :, :, 0], raw_lb[:, :, :, 1], ALU.max))
                link(dve.tensor_tensor(LBD[:, :, :, 0], raw_lb[:, :, :, 0], LBM, ALU.subtract))
                dve.tensor_tensor(LBD[:, :, :, 1], raw_lb[:, :, :, 1], LBM, ALU.subtract).then_inc(S["lb_d"], 1)
                dve.wait_ge(S["lb_e"], 1)
                link(dve.tensor_tensor(LBS, LBD[:, :, :, 0], LBD[:, :, :, 1], ALU.add))
                link(dve.reciprocal(LBS, LBS))
                link(dve.tensor_tensor(LBV, LBD[:, :, :, 0], LBS, ALU.mult))
                link(dve.tensor_scalar(OML, LBV, -1.0, 1.0, ALU.mult, ALU.add))

                for _ in range(2):
                    ahead(t.u)
                    t.u += 1
                for i, (c, r, g) in enumerate(((CKV, RC, "g_kv"), (CQ, RQ, "g_q"))):
                    ahead(t.u)
                    t.u += 1
                    dve.wait_ge(S["crms"], i + 1)
                    dve.reciprocal(r, r).then_inc(S["crinv"], 1)
                    dve.wait_ge(S["crinv"], i + 1)
                    for k in range(2):
                        dve.scalar_tensor_tensor(c[:, k, :], c[:, k, :], vcol(g, k), r, ALU.mult, ALU.mult)\
                            .then_inc(S["cnormed"], 1)
                ahead(t.u)
                t.u += 1
                ahead(t.u)
                t.u += 1
                cos, sin = RP[0:64, 0, :], RP[0:64, 1, :]

                def b4(v):
                    return v.unsqueeze(1).broadcast_to([64, 4, T])
                for i, (x, rot, cc, ss) in enumerate((
                        (KPE[0:64, 0:T], PS[0:64, 2, 0:T], cos, sin),
                        (QR[0:64], PS[0:64, 0:2, :].rearrange("p a (b c) -> p (a b) c", b=2), b4(cos), b4(sin)))):
                    dve.wait_ge(S["rot"], i + 1)
                    ta, tb = (v[:, 0:T] if i == 0 else v.rearrange("p (a b) -> p a b", a=4) for v in RT)
                    link(dve.tensor_tensor(ta, x, cc, ALU.mult))
                    link(dve.tensor_tensor(tb, rot, ss, ALU.mult))
                    dve.tensor_tensor(x, ta, tb, ALU.add).then_inc(S["roped"], 1)
                    dve.wait_ge(S["roped"], i + 1)

                def item(i):
                    if i < 8:
                        dve.wait_ge(S["mla_s"], i + 1)
                        link(dve.reduce_max(MX[:, i:i + 1], PS[:, i % 2, :], AX.X))
                        dve.tensor_scalar(NMX[:, i:i + 1], MX[:, i:i + 1], -1.0, None, ALU.mult)\
                            .then_inc(S["mla_mx"], 1)
                    if 1 <= i < 9:
                        j = i - 1
                        dve.wait_ge(S["mla_p"], j + 1)
                        link(dve.reciprocal(PRS[:, j:j + 1], PSM[:, j:j + 1]))
                        dve.tensor_scalar(PB[:, j % 2, :], PB[:, j % 2, :], PRS[:, j:j + 1], None, ALU.mult)\
                            .then_inc(S["mla_pn"], 1)
                        dve.wait_ge(S["mla_t"], j + 1)
                        dve.tensor_copy(PT[:, j % 2, :], PS[:, 2, :]).then_inc(S["mla_pt"], 1)
                    if i >= 2:
                        j = i - 2
                        dve.wait_ge(S["mla_o"], j + 1)
                        dve.tensor_copy(QN[:, j // 2, (j % 2) * P:(j % 2 + 1) * P], PS[:, 3, 0:P])\
                            .then_inc(S["mla_om"], 1)

                n = 0
                for i in range(6):
                    ahead(t.u)
                    t.u += 1
                    for _ in range(2 if i < 4 else 1):
                        item(n)
                        n += 1
                for i in range(2):
                    ahead(t.u)
                    t.u += 1
                dve.wait_ge(S["op_hi"], t.op + 1)
                dve.wait_ge(S["mla_om"], 8)
                for k in range(4):
                    ins = dve.tensor_tensor(XL[:, k, 0:T], QN[:, k, :], XH[:, k, 0:T].bitcast(F32), ALU.subtract)
                ins.then_inc(S["op_lo"], 1)
                link(dve.memset(M64, 1.0))
                link(dve.memset(M64.rearrange("p (a b) -> p a b", b=CH)[:, :, 0:1], 0.0))
                for d in range(2):
                    dve.wait_ge(S["sig_ready"], d + 1)
                    for h in range(4):
                        g = GK[d][:, :, h, :]
                        ins = dve.tensor_scalar(g, g, OML[:, d, h:h + 1], LBV[:, d, h:h + 1], ALU.mult, ALU.add)
                    ins.then_inc(S["f_ready"], 1)
                for d in range(2):
                    dve.wait_ge(S["lf_ready"], d + 1)
                    link(dve.tensor_scalar(GK[d], GK[d], -1.0, 1.0, ALU.mult, ALU.add))
                    t1 = W1.rearrange("p (h t) -> p h t", h=4)
                    for h in range(4):
                        for half in range(2):
                            lo = P * ((1 - half) if d == 0 else half)
                            first = lo + P - 1 if d == 0 else lo
                            before = first + 1 if d == 0 else first - 1
                            init = t1[:, h, before:before + 1] if half else 0.0
                            g, o = GL[d][:, 1, h, lo:lo + P], t1[:, h, lo:lo + P]
                            if d == 0:
                                g, o = g[:, ::-1], o[:, ::-1]
                            link(dve.tensor_tensor_scan(o, ones, g, init, ALU.mult, ALU.add))
                    dve.tensor_tensor(t1, t1, GL[d][:, 1], ALU.subtract).then_inc(S["scan_r"], 1)
                    dve.wait_ge(S["exp_r"], d + 1)
                    dve.tensor_tensor(GK[d][:, 1], GK[d][:, 1], t1, ALU.mult).then_inc(S["kw_ready"], 1)
                    dve.wait_ge(S["kw_ready"], d + 1)
                    g = GL[d][:, 0].rearrange("p h t -> p (h t)")
                    if d == 0:
                        link(dve.tensor_tensor_scan(W1, M64, g, 0.0, ALU.mult, ALU.add))
                    else:
                        link(dve.tensor_tensor_scan(W1[:, ::-1], M64, g[:, ::-1], 0.0, ALU.mult, ALU.add))
                    b = W1.rearrange("p (c t) -> p c t", t=CH)
                    mid, end = (CH // 2, 0) if d else (CH // 2 - 1, CH - 1)
                    for tt, at in ((W2, mid), (W3, end)):
                        ins = dve.tensor_tensor(tt.rearrange("p (c t) -> p c t", t=CH), b,
                                                b[:, :, at:at + 1].broadcast_to([P, 16, CH]), ALU.subtract)
                        if at == mid:
                            link(ins)
                    ins.then_inc(S["d1_ready"], 1)
                    dve.wait_ge(S["e1_ready"], 4 * d + 4)
                    dve.wait_ge(S["e2_ready"], d + 1)
                    link(dve.tensor_tensor(QA[d], QA[d], HQ, ALU.mult))
                    link(dve.tensor_tensor(EQ[d], EQ[d], HQ, ALU.mult))
                    link(dve.tensor_tensor(KA[d], W2.rearrange("p (h t) -> p h t", h=4), GK[d][:, 0], ALU.mult))
                    dve.tensor_tensor(GK[d][:, 0], W3.rearrange("p (h t) -> p h t", h=4), GK[d][:, 0], ALU.mult)\
                        .then_inc(S["qk_ready"], 1)
                    dve.wait_ge(S["qk_ready"], d + 1)
                kwt = W1, W2
                for d in range(2):
                    dve.wait_ge(S["kwt"], d + 1)
                    dve.tensor_copy(kwt[d], PS[:, 4 + 2 * d:6 + 2 * d, :].rearrange("p a b -> p (a b)"))\
                        .then_inc(S["kwt_out"], 1)
                for d in range(2):
                    dve.wait_ge(S["s0_sum"], d + 1)
                    dve.tensor_copy(ST[:, d].rearrange("p h v -> p (h v)"), PS[:, 2 + d, :])\
                        .then_inc(S["s_ready"], 1)
                link(dve.memset(ATS, 0.0))
                n = 0
                for i in range(4):
                    for d in range(2):
                        c = 3 - i if d else i
                        r = slice(64 * (c % 2), 64 * (c % 2) + 64)
                        n += 1
                        mask = CST[r, CTB:CTB + CH] if d else tril[r, r]
                        dve.wait_ge(S["at_sum"], n)
                        a4 = lambda v: v.rearrange("p (h t) -> p h t", h=4)
                        for rows, cols in quarters(d):
                            rr = slice(r.start + rows.start, r.start + rows.stop)
                            w = cols.stop - cols.start
                            ins = dve.tensor_tensor(a4(ATS[rr, d, c % 2, :])[:, :, cols], a4(PS[rr, 2 + d, 0:256])[:, :, cols],
                                                    mask[rows, cols].unsqueeze(1).broadcast_to([CH // 2, 4, w]),
                                                    ALU.mult)
                        ins.then_inc(S["at_out"], 1)
                        if i < 3:
                            dve.wait_ge(S["kd_sum"], n)
                            dve.tensor_copy(KDS[r, d, :], PS[r, 4 + d, :]).then_inc(S["kd_out"], 1)
                    for d in range(2):
                        c = 3 - i if d else i
                        if i < 3:
                            dve.wait_ge(S["su_sum"], 2 * i + d + 1)
                            for h in range(4):
                                ins = dve.scalar_tensor_tensor(
                                    ST[:, d, h, :], ST[:, d, h, :], EL[d][:, h, c:c + 1],
                                    PS[:, 6 + d, h * P:(h + 1) * P], ALU.mult, ALU.add)
                            ins.then_inc(S["s_ready"], 1)
                dve.wait_ge(S["h_rms"], 1)
                link(dve.reciprocal(W3, W3))
                for b in range(2):
                    dve.scalar_tensor_tensor(W1[:, 512 * b:512 * b + 512], PS[:, b, :], vcol("g_on", 0),
                                             W3[:, 512 * b:512 * b + 512], ALU.mult, ALU.mult)\
                        .then_inc(S["h_y"], 1)
                dve.wait_ge(S["h_y"], 2)
                dve.wait_ge(S["hg_ready"], 1)
                dve.tensor_tensor(W1, W1, HG.rearrange("p h t -> p (h t)"), ALU.mult).then_inc(S["h_y"], 1)
                dve.wait_ge(S["h_y"], 3)
                low(XL[:, 4:8, 0:T], W1.rearrange("p (h t) -> p h t", h=4), XH[:, 4:8, 0:T], t.op + 2)
                t.op += 2
                for mp in range(4):
                    ahead(t.u)
                    used(t.u)
                    for m in (2 * mp, 2 * mp + 1):
                        b = PS[:, 4 + t.pp % 2, (m % 2) * T:(m % 2 + 1) * T]
                        ins = dve.scalar_tensor_tensor(XT[:, m, :], b, MODV[:, 2 * KT + m, 0:1], XT[:, m, :],
                                                       ALU.mult, ALU.add)
                    ins.then_inc(S["pp_taken"], 1)
                    t.u += 1
                    t.pp += 1

            dve.memset(ZB[:, :], 0.0).then_inc(S["setup"], 1)
            dve.wait_ge(S["const_in"], 32)
            dve.tensor_copy(IDB[:, :], ident).then_inc(S["setup"], 1)
            dve.tensor_copy(MKB[:, :], CST[:, CMK:CMK + P]).then_inc(S["setup"], 1)
            ahead(0)
            norm(gain(0))
            attention()
            norm(gain(1))
            ffn(0)
            norm(gain(2))
            gating()
            norm(gain(3))
            ffn(1)
            norm(gain(4))
            state_space()
            norm(gain(5))
            ffn(2)
            norm(gain(6))
            attention()
            norm(gain(7))

            def context():
                dve.wait_ge(S["ctx_in"], 32)
                norm(mod_gain(0, 1), CT, (0, 1), T)
            ffn(3, aside=context)
            norm_stream("final_norm_g")
            norm(mod_gain(0, 0), XT, (0, 0))
            last_mixer()
            norm(mod_gain(1, 0), XT, (3 * KT, 0))
            ffn(0, conv=False)
            norm_stream("g_final")

        @block.tensor
        def _(pe):
            t = Tally()

            def product(dst, stat, mov, first, last, **kw):
                (sh, sl), (mh, ml) = stat, mov
                pe.matmul(dst, sh, mh, start=first, stop=False, **kw)
                pe.matmul(dst, sh, ml, start=False, stop=False, **kw)
                return pe.matmul(dst, sl, mh, start=False, stop=last, **kw)

            def w(slot, a, b):
                return whi[:, slot, a:b], wlo[:, slot, a:b]

            def x(k, a=0, b=T):
                return XH[:, k, a:b], XL[:, k, a:b]

            def fresh_bank():
                if t.pp >= 2:
                    pe.wait_ge(S["pp_taken"], t.pp - 1)
                t.pp += 1
                return 4 + (t.pp - 1) % 2

            def operand(first, k, per=1):
                if first and k % per == 0:
                    pe.wait_ge(S["op_lo"], t.op + k // per + 1)

            def unit_ready(u):
                pe.wait_ge(S["w_lo"], split_index(u) + 1)
                return split_index(u) % RING

            def features(first=False, per=1):
                b = fresh_bank()
                slot = unit_ready(t.u)
                for m in range(2):
                    for k in range(KT):
                        operand(first and m == 0, k, per)
                        mm = product(PS[:, b, m * T:(m + 1) * T], w(slot, k * 256 + m * P, k * 256 + m * P + P),
                                     x(k), k == 0, k == KT - 1)
                mm.then_inc(S["w_used"], 1)
                t.u += 1

            def tokens(first=False):
                b = fresh_bank()
                slot = unit_ready(t.u)
                for c in range(2):
                    for k in range(KT):
                        operand(first and c == 0, k)
                        mm = product(PS[:, b, c * 256:(c + 1) * 256], x(k, c * P, (c + 1) * P),
                                     w(slot, k * 256, (k + 1) * 256), k == 0, k == KT - 1)
                mm.then_inc(S["w_used"], 1)
                t.u += 1

            def sums(mp):
                pe.wait_ge(S["sq_ready"], 4 * t.norm + mp + 1)
                for k in (2 * mp, 2 * mp + 1):
                    mm = pe.matmul(PS[:, 6, 0:T], ones, SQ[:, k, :], start=(k == 0), stop=(k == KT - 1))
                if mp == 3:
                    mm.then_inc(S["norm_sum"], 1)
                    t.norm += 1

            def residual(per):
                for mp in range(4):
                    features(mp == 0, per)
                    if mp >= 1:
                        sums(mp - 1)
                sums(3)
                t.op += KT // per

            def ffn(aside=None):
                u0, q0, hid0 = t.u, t.pp, t.hid

                def up(j, it=None):
                    k = 0 if it is None else it
                    u = u0 + 2 + 3 * (j // 2 - 1) + j % 2 if j >= 2 else u0 + j
                    if q0 + j >= 2:
                        pe.wait_ge(S["pp_taken"], q0 + j - 1 + 2 * k)
                    pe.wait_ge(S["w_lo"], split_index(u) + 1 + 3 * k)
                    slot = split_index(u) % RING
                    for m in range(2):
                        for kt in range(KT):
                            operand(it is None and j == 0 and m == 0, kt)
                            mm = product(PS[:, 4 + (q0 + j) % 2, m * T:(m + 1) * T],
                                         w(slot, kt * 256 + m * P, kt * 256 + m * P + P),
                                         x(kt), kt == 0, kt == KT - 1)
                    mm.then_inc(S["w_used"], 1)

                def down(h, it=None, last=False):
                    k = 0 if it is None else it
                    u = u0 + 4 + 3 * h
                    if last:
                        u = u0 + 3 * FT // 2 - 1
                    pe.wait_ge(S["hl_ready"], hid0 + h + 1 + k)
                    pe.wait_ge(S["w_lo"], split_index(u) + 1 + 3 * k)
                    slot = split_index(u) % RING
                    for m in range(KT):
                        for i in range(2):
                            mm = product(PS[:, m // 2, (m % 2) * T:(m % 2 + 1) * T],
                                         w(slot, i * D + m * P, i * D + m * P + P),
                                         (HH[:, i, :], HL[:, i, :]), False, last and i == 1,
                                         skip_group_check=True)
                    mm.then_inc(S["w_used"], 1)

                if t.acc:
                    pe.wait_ge(S["acc_taken"], t.acc)
                for b in range(4):
                    pe.matmul(PS[:, b, :], ZB[:, 0:P], ZB[:, :], start=True, stop=False, skip_group_check=True)
                up(0)
                up(1)
                if aside:
                    aside()
                n = FT // 2 - 1
                with pe.Fori(0, n) as it:
                    up(2, it)
                    up(3, it)
                    down(0, it)
                down(n, last=True)
                t.u += 3 * FT // 2
                t.op += KT
                t.pp += FT
                t.hid += FT // 2
                t.acc += 4
                for mp in range(4):
                    sums(mp)

            def attention():
                for n in range(8):
                    features(n == 0)
                for n in range(4):
                    tokens()
                t.op += KT
                pe.wait_ge(S["pp_taken"], t.pp)
                n0 = t.att
                kw = dict(skip_group_check=True)
                for p in range(10):
                    if p < 8:
                        r = p % 3
                        if p >= 3:
                            pe.wait_ge(S["wb_ready"], n0 + p - 2)
                        for i in range(2):
                            rows = slice(64 * i, 64 * i + 64)
                            b = PS[:, 2 * r + i, :]
                            q, k = QK[rows, p, :], QK[rows, KT + p, :]
                            pe.matmul(b[:, 0:P], IDB[:, :], MKB[:, :], start=True, stop=False, **kw)
                            pe.matmul(b[:, 2 * P:3 * P], IDB[:, :], MKB[:, :], start=False, stop=False, **kw)
                            pe.matmul(b[:, 0:T], k[:, 0:P], q, start=False, stop=True, **kw)
                            mm = pe.matmul(b[:, T:T + P], k[:, P:T], q[:, P:T], start=False, stop=True, **kw)
                        mm.then_inc(S["sc_ready"], 1)
                    if 1 <= p < 9:
                        r = (p - 1) % 3
                        pe.wait_ge(S["sp_ready"], n0 + p)
                        for i in range(2):
                            b = PS[:, 2 * r + i, :]
                            s = SP[:, (p - 1) % 2, 384 * i:384 * i + 384]
                            pe.matmul(b[:, 0:T], negU, s[:, 0:T], start=False, stop=True, **kw)
                            pe.matmul(b[:, P:T], negones, s[:, T:T + P], start=False, stop=True, **kw)
                            mm = pe.matmul(b[:, T:T + P], negU, s[:, T:T + P], start=False, stop=True, **kw)
                        mm.then_inc(S["c_ready"], 1)
                    if p >= 2:
                        h = p - 2
                        pe.wait_ge(S["wb_ready"], n0 + h + 1)
                        if h >= 2:
                            pe.wait_ge(S["op_lo"], t.op + h - 1)
                        for i in range(2):
                            o = PS[64 * i:64 * i + 64, 6 + p % 2, :]
                            f = (2 * h + i) * 64
                            wt = WB[:, h % 2, 384 * i:384 * i + 384]
                            pe.matmul(o[:, 0:T], V[:, 0, f:f + 64], wt[:, 0:T], start=True, stop=False, **kw)
                            mm = pe.matmul(o[:, P:T], V[:, 1, f:f + 64], wt[:, T:T + P], start=False, stop=True,
                                           **kw)
                        mm.then_inc(S["o_ready"], 1)
                t.att += 8
                residual(1)

            def gating():
                for n in range(4):
                    tokens(n == 0)
                for n in range(2):
                    features()
                pe.wait_ge(S["gvn_ready"], 2)
                pe.wait_ge(S["gtril"], 8)
                for g in range(8):
                    for c in range(2):
                        o = (g % 2) * T + c * P
                        mm = pe.matmul(PS[:, g // 2, o:o + P], GV[:, c, g * P:(g + 1) * P], GW[:, g, :],
                                       start=True, stop=True)
                    if g % 2:
                        mm.then_inc(S["mix_ready"], 1)
                for n in range(2):
                    features()
                t.op += KT
                residual(2)

            def last_mixer():
                def pair():
                    if t.wide == 0:
                        pe.wait_ge(S["pp_taken"], t.pp)
                    if t.wide >= 2:
                        pe.wait_ge(S["wide_taken"], t.wide - 1)
                    t.wide += 1
                    return 4 + 2 * ((t.wide - 1) % 2)

                def unit(kind, first=False):
                    b = pair()
                    slot = unit_ready(t.u)
                    if kind == "tokens":
                        for blk in range(4):
                            for k in range(KT):
                                mm = product(PS[:, b + blk // 2, (blk % 2) * 256:(blk % 2) * 256 + 256],
                                             x(k, blk * P, (blk + 1) * P), w(slot, k * 256, (k + 1) * 256),
                                             k == 0, k == KT - 1)
                    else:
                        n = 2 * T if kind == "both" else T
                        for m in range(2):
                            dst = PS[:, b + m, :] if kind == "both" else PS[:, b, m * T:(m + 1) * T]
                            for k in range(KT):
                                operand(first and m == 0, k)
                                mm = product(dst, w(slot, k * 256 + m * P, k * 256 + m * P + P), x(k, 0, n),
                                             k == 0, k == KT - 1)
                    mm.then_inc(S["w_used"], 1)
                    t.u += 1

                def csum(i, n):
                    pe.wait_ge(S["csq"], i + 1)
                    for k in range(2):
                        mm = pe.matmul(PS[:, i, 0:n], ones, CSQ[:, k, 0:n], start=(k == 0), stop=(k == 1))
                    mm.then_inc(S["csum"], 1)

                unit("both", True)
                t.op += KT
                csum(0, 512)
                unit("one")
                unit("tokens")
                csum(1, T)
                unit("tokens")
                b = pair()
                slot = unit_ready(t.u)
                for k in range(KT):
                    product(PS[0:64, b, :], w(slot, 64 * k, 64 * k + 64), x(k, 0, 512), k == 0, k == KT - 1)
                pe.wait_ge(S["cnormed"], 4)
                pe.wait_ge(S["crms"], 2)
                rw = raw[:, t.u % RING, :]
                for h in range(QHEADS):
                    for part, rows in ((0, P), (1, 64)):
                        for k in range(2):
                            c = 512 + 768 * k + (P * h if part == 0 else 512 + 64 * h)
                            mm = pe.matmul(PS[0:rows, 2 * part + h // 2, (h % 2) * T:(h % 2 + 1) * T],
                                           rw[:, c:c + rows], CQ[:, k, :], start=(k == 0), stop=(k == 1))
                mm.then_inc(S["w_used"], 1)
                t.u += 1
                pe.wait_ge(w_loaded[t.u % RING], 16 * (t.u // RING + 1))
                rw = raw[:, t.u % RING, :]
                for i in range(4):
                    b = pair()
                    for j in range(2):
                        for k in range(2):
                            if i < 2:
                                h = 2 * i + j
                                lhs, rhs = rw[:, D * k + P * h:D * k + P * h + P], CKV[:, k, :]
                            else:
                                blk = 2 * (i - 2) + j
                                lhs, rhs = CKV[:, k, P * blk:P * blk + P], rw[:, D * k + 512:D * k + D]
                            mm = pe.matmul(PS[:, b + j, :], lhs, rhs, start=(k == 0), stop=(k == 1))
                    mm.then_inc(S["kv_part"] if i < 3 else S["w_used"], 1)
                t.u += 1
                pe.wait_ge(S["q_out"], 2)
                pe.wait_ge(S["wide_taken"], 5)
                swap = CST[0:64, CRO:CRO + 64]
                pe.matmul(PS[0:64, 2, 0:T], swap, KPE[0:64, 0:T], start=True, stop=True).then_inc(S["rot"], 1)
                for i in range(2):
                    mm = pe.matmul(PS[0:64, i, :], swap, QR[0:64, 2 * i:2 * i + 2, :], start=True, stop=True)
                mm.then_inc(S["rot"], 1)

                def item(i):
                    if i < 8:
                        h, q = i // 2, slice((i % 2) * P, (i % 2 + 1) * P)
                        if i == 0:
                            pe.wait_ge(S["roped"], 2)
                            pe.wait_ge(S["wide_taken"], 9)
                        if i >= 2:
                            pe.wait_ge(S["mla_p"], i - 1)
                        pe.matmul(PS[:, i % 2, :], QN[:, h, q], KN[:, h, :], start=True, stop=False)
                        pe.matmul(PS[:, i % 2, :], QR[0:64, h, q], KPE[0:64, :], start=False, stop=True)\
                            .then_inc(S["mla_s"], 1)
                    if 1 <= i < 9:
                        j = i - 1
                        pe.wait_ge(S["mla_pn"], j + 1)
                        if j >= 1:
                            pe.wait_ge(S["mla_pt"], j)
                        for k in range(4):
                            mm = pe.transpose(PS[:, 2, k * P:(k + 1) * P], PB[:, j % 2, k * P:(k + 1) * P], ident)
                        mm.then_inc(S["mla_t"], 1)
                    if i >= 2:
                        j = i - 2
                        h = j // 2
                        pe.wait_ge(S["mla_pt"], j + 1)
                        if j >= 1:
                            pe.wait_ge(S["mla_om"], j)
                        for k in range(4):
                            mm = pe.matmul(PS[:, 3, 0:P], V2[:, k, h * P:(h + 1) * P],
                                           PT[:, j % 2, k * P:(k + 1) * P], start=(k == 0), stop=(k == 3))
                        mm.then_inc(S["mla_o"], 1)

                n = 0
                for i in range(6):
                    unit("one" if i < 4 else "both")
                    for _ in range(2 if i < 4 else 1):
                        item(n)
                        n += 1
                for i in range(2):
                    unit("both")

                pe.wait_ge(S["wide_taken"], t.wide)
                for d in range(2):
                    pe.wait_ge(S["kw_ready"], d + 1)
                    for blk in range(2):
                        for h in range(4):
                            mm = pe.transpose(PS[:, 4 + 2 * d + blk, h * P:(h + 1) * P],
                                              GK[d][:, 1, h, blk * P:(blk + 1) * P], ident)
                    mm.then_inc(S["kwt"], 1)
                kwt = W1, W2
                for d in range(2):
                    pe.wait_ge(S["kwt_out"], d + 1)
                    for h in range(4):
                        for blk in range(2):
                            mm = pe.matmul(PS[:, 2 + d, h * P:(h + 1) * P],
                                           kwt[d][:, blk * 512 + h * P:blk * 512 + (h + 1) * P],
                                           HV[:, 2 + blk, h * P:(h + 1) * P], start=(blk == 0), stop=(blk == 1))
                    mm.then_inc(S["s0_sum"], 1)
                kw = dict(skip_group_check=True)
                for b in range(2):
                    pe.matmul(PS[:, b, :], ZB[:, 0:P], ZB[:, :], start=True, stop=False, **kw)
                for i in range(4):
                    for d in range(2):
                        c = 3 - i if d else i
                        r = slice(64 * (c % 2), 64 * (c % 2) + 64)
                        tok = slice(CH * c, CH * c + CH)
                        if i == 0:
                            pe.wait_ge(S["s_ready"], 2)
                        for h in range(4):
                            for rows, cols in quarters(d):
                                key = slice(tok.start + rows.start, tok.start + rows.stop)
                                query = slice(tok.start + cols.start, tok.start + cols.stop)
                                mm = pe.matmul(
                                    PS[r.start + rows.start:r.start + rows.stop, 2 + d,
                                       h * CH + cols.start:h * CH + cols.stop],
                                    KA[d][:, h, key], QA[d][:, h, query], start=True, stop=True)
                        mm.then_inc(S["at_sum"], 1)
                        if i < 3:
                            for h in range(4):
                                mm = pe.matmul(PS[r, 4 + d, h * P:(h + 1) * P], GK[d][:, 0, h, tok], ident,
                                               start=True, stop=True)
                            mm.then_inc(S["kd_sum"], 1)
                    for d in range(2):
                        c = 3 - i if d else i
                        r = slice(64 * (c % 2), 64 * (c % 2) + 64)
                        tok = slice(CH * c, CH * c + CH)
                        n = 2 * i + d + 1
                        pe.wait_ge(S["at_out"], n)
                        pe.wait_ge(S["s_ready"], n)
                        for h in range(4):
                            o = PS[:, h // 2, (h % 2) * T + CH * c:(h % 2) * T + CH * c + CH]
                            pe.matmul(o, ST[:, d, h, :], EQ[d][:, h, tok], start=False, stop=False, **kw)
                            mm = pe.matmul(o, HV[:, c // 2, h * P:(h + 1) * P], ATS[:, d, c % 2, h * CH:(h + 1) * CH],
                                           start=False, stop=(i == 3), **kw)
                        if i == 3 and d == 1:
                            mm.then_inc(S["h_out"], 1)
                        if i < 3:
                            pe.wait_ge(S["kd_out"], n)
                            for h in range(4):
                                mm = pe.matmul(PS[:, 6 + d, h * P:(h + 1) * P], KDS[r, d, h * P:(h + 1) * P],
                                               HV[r, c // 2, h * P:(h + 1) * P], start=True, stop=True)
                            mm.then_inc(S["su_sum"], 1)
                pe.wait_ge(S["h_sq"], 1)
                for b in range(2):
                    mm = pe.matmul(PS[:, 2 + b, :], ones, W2[:, 512 * b:512 * b + 512], start=True, stop=True)
                mm.then_inc(S["h_sum"], 1)
                residual(4)

            def modulation():
                u = t.u
                pe.wait_ge(w_loaded[u % RING], 16 * (u // RING + 1))
                for m in range(2):
                    f = 2 * (u - MOD0) + m
                    for k in range(KT):
                        mm = pe.matmul(PS[:, 7, 2 * f:2 * f + 2],
                                       raw[:, u % RING, k * 256 + m * P:k * 256 + m * P + P],
                                       SCV[:, 2 * k:2 * k + 2], start=(k == 0), stop=(k == KT - 1))
                mm.then_inc(S["w_used"], 1)
                t.u += 1

            def state_space():
                for n in range(4):
                    features(n == 0)
                t.op += KT
                pe.wait_ge(S["s5_xb"], 4)
                for i, xb in enumerate((XBR, XBI)):
                    for k in range(KT):
                        for j in range(2):
                            pos = 8 * (k // 2) + 4 * j + 2 * (k % 2)
                            src = xb[:, pos:pos + 2, :].rearrange("p r n -> p (r n)")
                            mm = pe.matmul(PS[64 * j:64 * j + 64, 2 * i + k // 4, (k % 4) * P:(k % 4 + 1) * P],
                                           src, ident, start=True, stop=True)
                mm.then_inc(S["s5_turned"], 1)
                pe.wait_ge(S["s5_b"], 8)
                pe.wait_ge(S["pp_taken"], t.pp)
                for st in range(17):
                    if st < 16:
                        c, qd, b = st // 4, st % 4, 2 * (st % 2)
                        if st >= 2:
                            pe.wait_ge(S["bu_mult"], st - 1)
                        for j in range(2):
                            rows = slice(64 * j, 64 * j + 64)
                            for kk in range(2):
                                k = 2 * qd + kk
                                for e in range(2):
                                    o = (2 * kk + e) * 64
                                    for ri, bm in ((0, BRE), (T, BIM)):
                                        mm = pe.matmul(PS[:, b + j, ri + o:ri + o + 64], bm[rows, k, e, :],
                                                       U5[rows, k, 64 * c:64 * c + 64], start=True, stop=True)
                        mm.then_inc(S["bu_ready"], 1)
                    for _ in range(2):
                        if t.u < MOD0 + MODN:
                            modulation()
                    if st >= 1:
                        s = st - 1
                        c, qd, wk = s // 4, s % 4, W5[s % 2]
                        pe.wait_ge(S["x5_ready"], s + 1)
                        if c >= 2 and qd == 0:
                            pe.wait_ge(S["y5_sum"], c - 1)
                        for pos in range(8):
                            k, q = 2 * qd + (pos // 2) % 2, 2 * (pos // 4) + pos % 2
                            dst = PS[32 * q:32 * q + 32, 4 + c % 2, 64 * k:64 * k + 64]
                            col = slice(64 * pos, 64 * pos + 64)
                            pe.matmul(dst, CRE[:, 8 * qd + pos, :], wk[0][:, col], start=True, stop=False)
                            mm = pe.matmul(dst, CIM[:, 8 * qd + pos, :], wk[4][:, col], start=False, stop=True)
                        mm.then_inc(S["y5_ready"], 1)
                for c in range(4):
                    pe.wait_ge(S["op_lo"], t.op + c + 1)
                for mp in range(4):
                    features()
                    features()
                    if mp >= 1:
                        sums(mp - 1)
                sums(3)
                t.op += 4

            pe.wait_ge(S["setup"], 3)
            pe.wait_ge(S["silu_c"], 1)
            for mp in range(4):
                sums(mp)
            attention()
            ffn()
            gating()
            ffn()
            state_space()
            ffn()
            attention()

            def context():
                for mp in range(4):
                    sums(mp)
                t.op += KT
            ffn(context)
            for mp in range(4):
                sums(mp)
            last_mixer()
            ffn()

        @block.gpsimd
        def _(pool):
            for st in range(17):
                if st < 16:
                    wk = W5[st % 2]
                    pool.wait_ge(S["bu_mult"], st + 1)
                    pool.tensor_tensor(wk[0], wk[0], wk[1], ALU.add)
                    pool.tensor_tensor(wk[2], wk[2], wk[3], ALU.subtract).then_inc(S["v_ready"], 1)
                if st >= 1:
                    s = st - 1
                    qd, wk = s % 4, W5[s % 2]
                    tc = AR[:, B0 + 512 * qd:B0 + 512 * qd + 512]
                    ts = AR[:, B0 + 2048 + 512 * qd:B0 + 2048 + 512 * qd + 512]
                    pool.wait_ge(S["scan_ready"], s + 1)
                    pool.tensor_tensor(wk[4], wk[1], ts, ALU.mult).then_inc(S["p_yrs"], 1)
                    pool.wait_ge(S["rot_ready"], s + 1)
                    pool.tensor_tensor(wk[3], wk[3], tc, ALU.mult).then_inc(S["p_yrs"], 1)
                    pool.tensor_tensor(wk[0], wk[0], wk[2], ALU.subtract)
                    pool.wait_ge(S["p_yrs"], 2 * s + 2)
                    pool.tensor_tensor(wk[4], wk[4], wk[3], ALU.add).then_inc(S["x5_ready"], 1)


def unit_pairs(w, pairs=None):
    k, n = w.shape
    return w.reshape(k // P, P, n // 256, 256).transpose(2, 1, 0, 3).reshape(n // 256, P, -1)


def unit_ffn(w_a, w_g, w_down):
    both = np.stack([w_a.reshape(D, FT, P), w_g.reshape(D, FT, P)], axis=2).reshape(D, FT * 2 * P)
    up, down = unit_pairs(both), w_down.reshape(FT // 2, 2, P, D).transpose(0, 2, 1, 3).reshape(FT // 2, P, -1)
    order = [up[0:2]]
    for h in range(1, FT // 2):
        order += [up[2 * h:2 * h + 2], down[h - 1:h]]
    return np.concatenate(order + [down[-1:]])


def fm(v):
    return v.reshape(-1, P).T


def kernel(**inputs):
    import numpy as _np
    import concourse.bacc as _bacc
    from concourse import mybir as _mybir
    from concourse.bass_utils import run_bass_kernel_spmd as _run

    a = {k: _np.asarray(v) for k, v in inputs.items()}
    ffn = [unit_ffn(a["ffn_w_up"][i][:, :FF], a["ffn_w_up"][i][:, FF:], a["ffn_w_down"][i]) for i in range(4)]
    glu = _np.stack([a["ssm_w_glu"][0][:, :D].reshape(D, KT, P), a["ssm_w_glu"][0][:, D:].reshape(D, KT, P)],
                    axis=2).reshape(D, 2 * D)
    sg = a["sg_w_in"][0]
    stream = [unit_pairs(a["sb_w_qkv"][0]), unit_pairs(a["sb_w_o"][0]), ffn[0],
              unit_pairs(sg[:, D:]), unit_pairs(sg[:, :D]), unit_pairs(a["sg_w_o"][0]), ffn[1],
              unit_pairs(a["ssm_w_in"][0]), unit_pairs(a["w_mod_2"][0]), unit_pairs(glu), ffn[2],
              unit_pairs(a["sb_w_qkv"][1]), unit_pairs(a["sb_w_o"][1]), ffn[3]]
    win, wuq, wukv = a["w_in_2"][0], a["w_uq_2"][0], a["w_ukv_2"][0]
    col = lambda i, n: unit_pairs(win[:, i:i + n])
    rows = lambda w: w.reshape(-1, P, w.shape[1]).transpose(1, 0, 2).reshape(P, -1)
    uq = wuq.reshape(256, 4, 192)
    uq = _np.concatenate([uq[:, :, :NOPE].reshape(256, -1), uq[:, :, NOPE:].reshape(256, -1)], axis=1)
    ukv = wukv.reshape(256, 4, 2, P).transpose(0, 2, 1, 3).reshape(256, D)
    stream += [col(256, 256), col(0, 256), col(1088, 512),
               _np.concatenate([rows(win[:, 512:576]), rows(uq)], axis=1)[None], rows(ukv)[None],
               col(576, 512), col(1600, 512), col(2112, 512), col(2624, 512),
               unit_pairs(a["w_out_2"][0]), unit_ffn(a["w_up_2"][0], a["w_gate_2"][0], a["w_down_2"][0])]
    stream.append(_np.zeros((1, P, UNIT), _np.float32))
    stream = _np.concatenate(stream)
    cw, cb = a["ffn_conv_w"], a["ffn_conv_b"]
    taps = _np.concatenate([cw, cb[:, None]], axis=1).reshape(4, 4, 2, FT, P)
    taps = taps.transpose(4, 0, 3, 2, 1).reshape(P, -1)
    lb = lambda v: v.reshape(2, 4, P).transpose(2, 1, 0).reshape(P, 8)
    order = _np.array([4 * (2 * qd + kk) + 2 * j + e for qd in range(4) for j in range(2)
                       for kk in range(2) for e in range(2)])
    pairs = lambda v: v.reshape(32, P)[order].T
    vec = _np.concatenate([
        fm(a["norm_g"].reshape(-1)), fm(a["final_norm_g"]), fm(a["sg_norm_g"][0]), fm(a["ssm_d"][0]), taps,
        fm(a["b_mod_2"][0]), fm(a["g_norm_mix_2"][0]), fm(a["g_norm_ffn_2"][0]), fm(a["g_q_norm_2"][0]),
        fm(a["g_kv_norm_2"][0]), lb(a["lb_fwd_2"]), lb(a["lb_bwd_2"]), fm(a["g_hgrn_norm_2"][0]),
        fm(a["g_final_2"]),
        _np.stack([fm(a["c_2"][0]), fm(a["c_ctx_2"])], axis=2).reshape(P, 2 * KT),
        _np.full((P, 1), EPS, _np.float32),
        pairs(a["ssm_lam_re"][0].reshape(-1)), pairs(a["ssm_lam_im"][0].reshape(-1)),
        pairs(_np.repeat(a["ssm_log_dt"][0], 64))], axis=1)
    assert vec.shape[1] == NVEC
    i = _np.arange(P)
    swap = _np.zeros((P, 64))
    for m in range(64):
        swap[m + 16 if m % 32 < 16 else m - 16, m] = -1.0 if m % 32 < 16 else 1.0
    inv = (1.0 / 10000.0 ** (_np.arange(0, 32, 2, dtype=_np.float32) / 32)).astype(_np.float32)
    row, colm = _np.arange(T) // 64, _np.arange(T) % 64
    ang = _np.concatenate([inv[:, None] * row[None, :].astype(_np.float32)] * 2
                          + [inv[:, None] * colm[None, :].astype(_np.float32)] * 2)
    ropes = _np.stack([_np.cos(ang), _np.sin(ang)], axis=1).astype(_np.float32)
    tri = 1.0 * (i[:, None] <= i[None, :])
    cst = _np.concatenate([
        _np.eye(P), -1.0 * (i[:, None] >= i[None, :]), -_np.ones((P, P)), _np.ones((P, P)),
        _np.where(i[:, None] < i[None, :], 0.0, -1e30), tri,
        _np.broadcast_to(_np.arange(64), (P, 64)), 1.0 * (i[:, None] % 64 >= _np.arange(64)[None, :]),
        swap], axis=1).astype(_np.float32)
    arrays = {
        "wst": stream, "vec": vec, "cst": cst,
        "x_in": a["x"][0].T.reshape(KT, P, T).transpose(1, 0, 2),
        "sgw": a["sg_w_s"][0].transpose(2, 0, 1),
        "sgb": _np.broadcast_to(a["sg_b"][0], (P, 8, P)),
        "sbc": _np.concatenate([a["ssm_b_re"][0].reshape(32, P, 16), a["ssm_b_im"][0].reshape(32, P, 16),
                                a["ssm_c_re"][0].transpose(0, 2, 1).reshape(32, P, 16),
                                a["ssm_c_im"][0].transpose(0, 2, 1).reshape(32, P, 16)], axis=2)[order].transpose(1, 0, 2),
        "ctxin": a["ctx_2"][0].T.reshape(KT, P, T).transpose(1, 0, 2),
        "ropes": ropes,
    }
    nc = _bacc.Bacc("TRN2", target_bir_lowering=False, num_devices=1)
    arrays = {k: _np.ascontiguousarray(v) for k, v in arrays.items()}
    args = [nc.dram_tensor(k, v.shape, _mybir.dt.from_np(v.dtype), kind="ExternalInput").ap()
            for k, v in arrays.items()]
    args.append(nc.dram_tensor("y_out", (P, KT, T), _mybir.dt.float32, kind="ExternalOutput").ap())
    program(nc, *args)
    r = _run(nc, [arrays], core_ids=[0])
    y = r.results[0]["y_out"]
    return _np.ascontiguousarray(y.transpose(2, 1, 0).reshape(1, T, D))
```

```python
from contextlib import ExitStack

import numpy as np

import concourse.bass as bass
from concourse import mybir

F32 = mybir.dt.float32
R32 = mybir.dt.float32r
BF16 = mybir.dt.bfloat16
ALU = mybir.AluOpType
ACT = mybir.ActivationFunctionType
AX = mybir.AxisListType

P = 128
T = 256
D = 1024
KT = D // P
EPS = 1e-6
UNIT = 2048
RING = 3
FF = 2816
FT = FF // P
HEADS = 16

PLAN = [("qkv", 12), ("wo", 4), ("ffn", 33), ("sg", 8), ("wo", 4), ("ffn", 33), ("ssm", 4),
        ("mod", 8), ("glu", 8), ("ffn", 33), ("qkv", 12), ("wo", 4), ("ffn", 33),
        ("in2", 14), ("mod", 16), ("wo", 4), ("ffn", 33)]
STARTS = [sum(n for _, n in PLAN[:i]) for i in range(len(PLAN) + 1)]
UNITS = STARTS[-1]
MODS = (STARTS[7], 8), (STARTS[14], 16)


def split_index(u):
    return u - sum(min(max(u - m, 0), n) for m, n in MODS)


def unit_of(s):
    for m, n in MODS:
        if s >= m:
            s += n
    return s


def is_mod(u):
    return any(m <= u < m + n for m, n in MODS)


def step5(s):
    return 2 * (s // 8) + s % 2, s // 2 % 4


def quarters(d):
    first, second, whole = slice(0, CH // 2), slice(CH // 2, CH), slice(0, CH)
    return ((first, whole), (second, second)) if d == 0 else ((first, first), (second, whole))


def vector_columns():
    at, n = {}, 0
    for name, k in (("norm_g", 4 * 2 * KT), ("final_norm_g", KT), ("sg_norm_g", KT), ("ssm_d", KT),
                    ("conv", 4 * 2 * FT * 4), ("b_mod", 6 * KT), ("g_mix", KT), ("g_ffn", KT),
                    ("g_q", 2), ("g_kv", 2), ("lb_fwd", 8), ("lb_bwd", 8), ("g_on", 1),
                    ("g_final", KT), ("c", 2 * KT), ("eps", 1),
                    ("lam_re", 32), ("lam_im", 32), ("log_dt", 32)):
        at[name] = n
        n += k
    return at, n


VC, NVEC = vector_columns()
CI, CNU, CNO, CON, CMK, CTR, CRT, CTB, CRO = 0, 128, 256, 384, 512, 640, 768, 832, 896
NCST = 960
QHEADS = 4
NOPE, ROPE = 128, 64
CH = 64
IN0 = STARTS[13]
RAW_USED = (IN0 + 4, IN0 + 5)


class Tally:

    def __init__(self):
        self.u = 0
        self.s = 0
        self.pp = 0
        self.norm = 0
        self.op = 0
        self.up = 0
        self.hid = 0
        self.conv = 0
        self.acc = 0
        self.att = 0
        self.xn = 0
        self.normed = 0
        self.wide = 0


def program(nc, wst, vec, cst, xin, sgw, sgb, sbc, ctxin, ropes, out):
    with ExitStack() as ctx:
        def sb(name, shape, dt=F32):
            return ctx.enter_context(nc.sbuf_tensor(name, shape, dt))

        def sem(name):
            return ctx.enter_context(nc.semaphore(name))

        raw = sb("raw", [P, RING, UNIT])
        whi = sb("whi", [P, RING, UNIT], R32)
        wlo = sb("wlo", [P, RING, UNIT], R32)
        XH = sb("XH", [P, KT, 2 * T], R32)
        XL = sb("XL", [P, KT, 2 * T], R32)
        HH = sb("HH", [P, 2, T], R32)
        HL = sb("HL", [P, 2, T], R32)
        XT = sb("XT", [P, KT, T])
        AR = sb("AR", [P, 20480])
        VEC = sb("VEC", [P, NVEC])
        CST = sb("CST", [P, NCST])
        MKB = sb("MKB", [P, P], BF16)
        IDB = sb("IDB", [P, P], BF16)
        ZB = sb("ZB", [P, 512], BF16)
        MODV = sb("MODV", [P, 6 * KT, 2])
        MODG = sb("MODG", [P, 2, KT, 2])
        SM = sb("SM", [P, 512])
        PS = ctx.enter_context(nc.psum_tensor("PS", [P, 8, 512], F32))

        def ar(off, *shape):
            n = int(np.prod(shape))
            v = AR[:, off:off + n]
            if len(shape) == 2:
                return v.rearrange("p (a b) -> p a b", b=shape[1])
            if len(shape) == 3:
                return v.rearrange("p (a b c) -> p a b c", b=shape[1], c=shape[2])
            return v

        ident, negU, negones, ones = (CST[:, o:o + P] for o in (CI, CNU, CNO, CON))
        tril = CST[:, CTR:CTR + P]
        rt = CST[:, CRT:CRT + 64]

        def vcol(name, i):
            return VEC[:, VC[name] + i:VC[name] + i + 1]

        SCP = SM[:, 256:512].rearrange("p (k s) -> p k s", s=32)
        MROW = AR[:, 2048:2560], AR[:, 4096:4608], AR[:, 4096:4608]
        XN = ar(0, KT, T)
        SQ = ar(2048, KT, T)
        CA = ar(4096, 2, 2, T)
        SG = ar(5120, 2, T)
        HID = ar(5632, 2, T)
        RMS = SM[:, 0:T]
        RSTD = SM[:, T:2 * T]
        B0 = 6144
        QK = ar(B0, 2 * KT, T)
        V = ar(B0 + 4096, 2, D)
        ZC = ar(B0 + 6144, 2, 768)
        EX = ar(B0 + 7680, 2, 768)
        LN = ar(B0 + 9216, 2, 768)
        SP = ar(B0 + 10752, 2, 768)
        WB = ar(B0 + 12288, 2, 768)
        GV = ar(B0, 2, D)
        GU = ar(B0 + 2048, KT, T)
        GS = ar(B0 + 4096, KT, T)
        GW = ar(B0 + 6144, 8, P)
        GB = ar(B0 + 7168, 8, P)
        GJ = ar(B0 + 8192, 2, D)

        TC = ar(B0, 32, 64)
        TS = ar(B0 + 2048, 32, 64)
        MG = ar(B0 + 4096, 32, 64)
        U5 = ar(B0 + 6144, KT, T)
        CRE = ar(B0 + 8192, 32, 32)
        CIM = ar(B0 + 9216, 32, 32)
        BRE = ar(B0 + 10240, KT, 2, P)
        BIM = ar(B0 + 12288, KT, 2, P)
        SBC = ar(B0 + 12288, 32, 64)
        PHT = ar(0, 32, 64)
        PHN = ar(2048, 32, 64)
        XBR, XBI = ar(4096, 32, 32), ar(5120, 32, 32)
        BT = [ar(B0 + 10240 + 512 * i, 32, 16) for i in range(4)]
        W5 = [[AR[:, 2048 * a + 512 * i:2048 * a + 512 * i + 512] for i in range(4)] for a in range(3)]

        def s5(i):
            return AR[:, B0 + 6144 + 32 * i:B0 + 6176 + 32 * i]
        Z5, E5, MAG, PH, NN, ARE, AIM, CFR, CFI, T0, T1, AER, AEI = (s5(i) for i in range(13))
        DEN, DENI = (MODV[:, 16 * i:16 * i + 16, :].rearrange("p a b -> p (a b)") for i in range(2))
        LR = VEC[:, VC["lam_re"]:VC["lam_re"] + 32]
        LI = VEC[:, VC["lam_im"]:VC["lam_im"] + 32]
        DT = VEC[:, VC["log_dt"]:VC["log_dt"] + 32]
        AR64, AI64, JRE, JIM, JA, JB, JC, JD = (SM[:, 32 * i:32 * i + 32] for i in range(8))

        V2 = ar(0, 4, 512)
        KN = ar(2048, QHEADS, 512)
        CKV = ar(4096, 2, 512)
        CQ = ar(5120, 2, T)
        KPE = ar(5632, 512)
        QN = ar(6144, QHEADS, T)
        QR = ar(7168, QHEADS, T)
        GK = [ar(8192 + 4096 * d, 2, 4, T) for d in range(2)]
        GL = [ar(10240 + 4096 * d, 2, 4, T) for d in range(2)]
        HV = ar(16384, 4, 512)
        HQ = ar(18432, 4, T)
        HG = ar(19456, 4, T)
        CT = ar(8192, KT, T)
        MW = 12288
        CSQ = ar(MW, 2, 512)
        RC = ar(MW + 1024, 512)
        RQ = ar(MW + 1536, T)
        PB = ar(MW, 2, 512)
        PT = ar(MW + 1024, 2, 512)
        RP = ar(MW + 2048, 2, T)
        RT = [AR[0:64, MW + 2560:MW + 3584], AR[0:64, 4096:5120]]
        EQ = [ar(1024 * d, 4, T) for d in range(2)]
        W1, W2, W3 = (AR[:, 2048 + 1024 * i:3072 + 1024 * i] for i in range(3))
        M64 = ar(5120, 1024)
        ST = ar(7168, 2, 4, P)
        ATS = ar(2048, 2, 2, 256)
        KDS = ar(3072, 2, 512)
        QA = [GL[d][:, 1] for d in range(2)]
        KA = [GL[d][:, 0] for d in range(2)]
        MX, NMX, PSM, PRS = (SM[:, 8 * i:8 * i + 8] for i in range(4))
        LBD = SM[:, 32:48].rearrange("p (d h r) -> p d h r", d=2, h=4)
        LBM, LBS, LBV, OML = (SM[:, 48 + 8 * i:56 + 8 * i].rearrange("p (d h) -> p d h", d=2) for i in range(4))
        EL = [SM[:, 80 + 16 * d:96 + 16 * d].rearrange("p (h c) -> p h c", c=4) for d in range(2)]

        names = ["const_in", "vec_in", "x_in", "sg_in", "s5_in", "w_hi", "w_lo", "w_used", "pp_taken", "sq_ready",
                 "norm_sum", "rms_ready", "rstd_ready", "xn_ready", "op_hi", "op_lo", "conv0", "conv1",
                 "silu_ready", "hid_ready", "hh_ready", "hl_ready", "acc_taken", "acc_ready", "setup", "zc_ready",
                 "ex_ready", "ln_ready", "sp_ready", "wb_ready", "sc_ready", "c_ready", "o_ready",
                 "qkv_ready", "gv_ready", "gss_ready", "grms_ready", "grstd_ready", "gvn_ready", "mix_ready",
                 "gs_ready", "gu_ready", "gtril", "gy_ready", "glu_sig", "glu_mul", "link", "s5_step", "s5_dt", "s5_den", "s5_bt", "s5_moved", "s5_clear",
                 "s5_angle", "s5_table", "s5_xb", "s5_turned", "s5_b", "bu_ready", "bu_mult", "v_ready", "scan_ready",
                 "rot_ready", "x5_ready", "jump", "jump_parts", "y5_ready", "y5_sum", "gelu5", "silu_c", "scp_nil", "mod_rows", "mod_sum", "mod_vec",
                 "ctx_in", "mod_gain", "normed", "wide_taken", "csq", "csum", "crms", "crinv", "cnormed",
                 "kv_part", "q_out", "rot", "roped", "mla_s", "mla_mx", "mla_p", "mla_pn", "mla_t", "mla_pt",
                 "mla_o", "mla_om", "lb_d", "lb_e", "lb_v", "hg_ready", "sig_ready", "f_ready", "lf_ready",
                 "scan_r", "exp_r", "kw_ready", "d1_ready", "e1_ready", "e2_ready", "qk_ready", "kwt", "kwt_out",
                 "s0_sum", "s_ready", "at_sum", "kd_sum", "at_out", "kd_out", "su_sum", "h_out", "h_sq", "h_sum",
                 "h_rms", "h_y"]
        S = {n: sem(n) for n in names}
        w_loaded = [sem(f"w_loaded{i}") for i in range(RING)]
        block = ctx.enter_context(nc.Block())

        @block.sync
        def _(sp):
            sp.dma_start(XT[:, :, :], xin).then_inc(S["x_in"], 16)
            sp.dma_start(CST[:, :], cst).then_inc(S["const_in"], 16)
            sp.dma_start(raw[:, 0, :], wst[0]).then_inc(w_loaded[0], 16)
            sp.dma_start(VEC[:, :], vec).then_inc(S["vec_in"], 16)
            for u in range(1, RING):
                sp.dma_start(raw[:, u, :], wst[u]).then_inc(w_loaded[u], 16)

            def load(u0, j, it=None):
                u = u0 + j
                before = u - RING
                step = 0 if it is None else it * RING
                if is_mod(before):
                    sp.wait_ge(S["w_used"], before + 1 + step)
                else:
                    sp.wait_ge(S["w_lo"], split_index(before) + 1 + step)
                    if before in RAW_USED:
                        sp.wait_ge(S["w_used"], before + 1)
                src = wst[u] if it is None else wst[bass.ds(u + step, 1)].squeeze(0)
                sp.dma_start(raw[:, u % RING, :], src).then_inc(w_loaded[u % RING], 16)

            def loads(u0, u1):
                n = (u1 - u0) // RING if not any(u0 <= u + RING < u1 for u in RAW_USED) else 0
                if n > 1:
                    with sp.Fori(0, n) as it:
                        for j in range(RING):
                            load(u0, j, it)
                    u0 += n * RING
                for u in range(u0, u1):
                    load(u, 0)

            cuts = [RING] + sorted([m + RING for m, _ in MODS] + [m + n + RING for m, n in MODS] + [IN0 + RING])\
                + [UNITS + 1]
            for a, b in zip(cuts, cuts[1:]):
                loads(a, b)
            sp.wait_ge(S["normed"], 2 * KT)
            sp.dma_start(out, XT[:, :, :]).then_inc(S["x_in"], 16)
            sp.wait_ge(S["x_in"], 32)

        def limit(u):
            return next((split_index(m) for m, _ in MODS if u < m), split_index(UNITS))

        @block.scalar
        def _(act):
            t = Tally()

            def split_hi(s, it=None):
                u, r = unit_of(s), s % RING
                step = 0 if it is None else it
                act.wait_ge(w_loaded[u % RING], 16 * (u // RING + 1) + 16 * step)
                if s >= RING:
                    act.wait_ge(S["w_used"], unit_of(s - RING) + 1 + RING * step)
                act.activation(whi[:, r, :], raw[:, u % RING, :], ACT.Copy).then_inc(S["w_hi"], 1)

            def ahead(u):
                while t.s < limit(u) and t.s <= split_index(u) + 2:
                    split_hi(t.s)
                    t.s += 1

            def used(u, step=0):
                act.wait_ge(S["w_used"], u + 1 + step)

            def squares(ready, src=XT):
                for mp in range(4):
                    ready(mp)
                    act.activation(SQ[:, 2 * mp:2 * mp + 2, :], src[:, 2 * mp:2 * mp + 2, :], ACT.Square)\
                        .then_inc(S["sq_ready"], 1)

            def rms():
                act.wait_ge(S["norm_sum"], t.norm + 1)
                act.activation(RMS, PS[:, 6, 0:T], ACT.Sqrt, bias=vcol("eps", 0), scale=1.0 / D)\
                    .then_inc(S["rms_ready"], 1)
                t.norm += 1

            def norm(shift=None, at=0):
                rms()
                for k in range(KT):
                    act.wait_ge(S["xn_ready"], t.xn + 1)
                    t.xn += 1
                    if shift is None:
                        act.activation(XH[:, k, at:at + T], XN[:, k, :], ACT.Copy).then_inc(S["op_hi"], 1)
                    else:
                        sh = MODV[:, shift[0] + k, shift[1]:shift[1] + 1]
                        act.activation(XH[:, k, at:at + T], XN[:, k, :], ACT.Identity, bias=sh)\
                            .then_inc(S["op_hi"], 1)
                t.op += KT

            def norm_stream():
                rms()
                def ready(mp):
                    act.wait_ge(S["normed"], t.normed + 2 * mp + 2)
                squares(ready)
                t.normed += KT

            def residual():
                def ready(mp):
                    ahead(t.u)
                    act.wait_ge(S["pp_taken"], t.pp + 1)
                    t.pp += 1
                    t.u += 1
                squares(ready)

            def ffn(layer, conv=True, aside=None, tail=None):
                u0, q0, up0, hid0 = t.u, t.pp, t.up, t.hid

                def up(j, it=None):
                    k = 0 if it is None else it
                    u = u0 + 2 + 3 * (j // 2 - 1) + j % 2 if j >= 2 else u0 + j
                    act.wait_ge(S["w_used"], u + 1 + 3 * k)
                    if conv:
                        for i in range(2):
                            c = VC["conv"] + (layer * FT + j) * 8 + 4 * i
                            w2 = VEC[:, c + 2:c + 3] if it is None else VEC[:, bass.ds(it * 16 + c + 2, 1)]
                            cb = VEC[:, c + 3:c + 4] if it is None else VEC[:, bass.ds(it * 16 + c + 3, 1)]
                            a = act.activation(CA[:, j % 2, i, :], PS[:, 4 + (q0 + j) % 2, i * T:(i + 1) * T],
                                               ACT.Identity, bias=cb, scale=w2)
                        a.then_inc(S["conv0"], 1)
                        act.wait_ge(S["pp_taken"], q0 + j + 1 + 2 * k)
                        act.activation(SG[:, j % 2, :], CA[:, j % 2, 1, :], ACT.Silu).then_inc(S["silu_ready"], 1)
                    else:
                        act.activation(SG[:, j % 2, :], PS[:, 4 + (q0 + j) % 2, T:2 * T], ACT.Silu)\
                            .then_inc(S["silu_ready"], 1)

                def hidden(h, it=None):
                    k = 0 if it is None else it
                    act.wait_ge(S["hid_ready"] if conv else S["pp_taken"], (up0 if conv else q0) + 2 * h + 2 + 2 * k)
                    if h > 0:
                        act.wait_ge(S["w_used"], u0 + 2 + 3 * h + 3 * k)
                    act.activation(HH[:, :, :], HID, ACT.Copy).then_inc(S["hh_ready"], 1)

                if not conv:
                    act.preload_act_table(ACT.Silu)
                for j in range(2):
                    ahead(u0 + j)
                    up(j)
                hidden(0)
                if aside:
                    aside()
                n = FT // 2 - 1
                s1 = t.s
                with act.Fori(0, n) as it:
                    for j in range(2):
                        split_hi(s1 + j, it)
                        up(2 + j, it)
                    split_hi(s1 + 2, it)
                    hidden(1, it)
                t.s += 3 * n
                t.u = u0 + 2 + 3 * n
                ahead(t.u)
                if tail:
                    tail()

                def ready(mp):
                    act.wait_ge(S["acc_taken"], t.acc + 1)
                    t.acc += 1
                squares(ready)
                t.u += 1
                t.pp += FT
                t.up += FT
                t.hid += FT // 2

            def attention():
                for n in range(8):
                    ahead(t.u)
                    used(t.u)
                    act.activation(QK[:, 2 * n:2 * n + 2, :],
                                   PS[:, 4 + t.pp % 2, :].rearrange("p (a b) -> p a b", a=2), ACT.Copy,
                                   scale=0.125 if n < 4 else 1.0).then_inc(S["pp_taken"], 1)
                    t.u += 1
                    t.pp += 1
                for n in range(4):
                    ahead(t.u)
                    used(t.u)
                    act.activation(V[:, :, 256 * n:256 * n + 256],
                                   PS[:, 4 + t.pp % 2, :].rearrange("p (a b) -> p a b", a=2), ACT.Copy)\
                        .then_inc(S["pp_taken"], 1)
                    t.u += 1
                    t.pp += 1
                act.preload_act_table_set("natural_log_exp_and_others")
                n0 = t.att
                for p in range(10):
                    if p < 8:
                        act.wait_ge(S["zc_ready"], n0 + p + 1)
                        act.activation(EX[:, p % 2, :], ZC[:, p % 2, :], ACT.Exp).then_inc(S["ex_ready"], 1)
                        act.wait_ge(S["ex_ready"], n0 + p + 1)
                        act.activation(LN[:, p % 2, :], EX[:, p % 2, :], ACT.Ln, bias=1.0)\
                            .then_inc(S["ln_ready"], 1)
                    if 1 <= p < 9:
                        r = (p - 1) % 3
                        act.wait_ge(S["c_ready"], n0 + p)
                        act.activation(WB[:, (p - 1) % 2, :].rearrange("p (a b) -> p a b", a=2),
                                       PS[:, 2 * r:2 * r + 2, 0:384], ACT.Exp).then_inc(S["wb_ready"], 1)
                    if p >= 2:
                        act.wait_ge(S["o_ready"], n0 + p - 1)
                        act.activation(XH[:, p - 2, 0:T], PS[:, 6 + p % 2, 0:T], ACT.Copy)\
                            .then_inc(S["op_hi"], 1)
                t.att += 8
                t.op += KT
                residual()

            def gating():
                for n in range(4):
                    ahead(t.u)
                    used(t.u)
                    act.activation(GV[:, :, 256 * n:256 * n + 256],
                                   PS[:, 4 + t.pp % 2, :].rearrange("p (a b) -> p a b", a=2),
                                   ACT.Gelu_apprx_tanh).then_inc(S["pp_taken"], 1)
                    t.u += 1
                    t.pp += 1
                act.wait_ge(S["gss_ready"], 2)
                act.activation(SM[:, 2:4], SM[:, 0:2], ACT.Sqrt, bias=vcol("eps", 0), scale=1.0 / D)\
                    .then_inc(S["grms_ready"], 1)
                for n in range(4):
                    ahead(t.u)
                    used(t.u)
                    act.activation(GU[:, 2 * n:2 * n + 2, :],
                                   PS[:, 4 + t.pp % 2, :].rearrange("p (a b) -> p a b", a=2),
                                   ACT.Gelu_apprx_tanh).then_inc(S["pp_taken"], 1)
                    t.u += 1
                    t.pp += 1
                for n in range(4):
                    act.wait_ge(S["gy_ready"], n + 1)
                    act.activation(XH[:, 2 * n:2 * n + 2, 0:T], GU[:, 2 * n:2 * n + 2, :], ACT.Copy)\
                        .then_inc(S["op_hi"], 1)
                    t.op += 1
                residual()

            def silu_c(n):
                act.wait_ge(S["scp_nil"], n)
                act.activation(SCP[:, :, 0:2], VEC[:, VC["c"]:VC["c"] + 2 * KT].rearrange("p (k s) -> p k s", s=2),
                               ACT.Silu).then_inc(S["silu_c"], 1)

            def sines():
                for i, tab in enumerate((TS, TC)):
                    act.wait_ge(S["s5_angle"], i + 1)
                    act.activation(tab, tab, ACT.Sin, scale=6.283185).then_inc(S["s5_table"], 1)

            def state_space():
                for n in range(4):
                    ahead(t.u)
                    used(t.u)
                    if n == 0:
                        act.wait_ge(S["s5_moved"], 1)
                    act.activation(U5[:, 2 * n:2 * n + 2, :],
                                   PS[:, 4 + t.pp % 2, :].rearrange("p (a b) -> p a b", a=2), ACT.Copy)\
                        .then_inc(S["pp_taken"], 1)
                    t.u += 1
                    t.pp += 1
                silu_c(1)
                t.u += MODS[0][1]
                for c in range(4):
                    act.wait_ge(S["y5_sum"], c + 1)
                    y = U5[:, :, 64 * c:64 * c + 64]
                    act.activation(y, y, ACT.Gelu_apprx_tanh).then_inc(S["gelu5"], 1)
                    act.wait_ge(S["gelu5"], c + 1)
                    act.activation(XH[:, :, 64 * c:64 * c + 64], y, ACT.Copy).then_inc(S["op_hi"], 1)
                t.op += 4

                def ready(mp):
                    for j in (2 * mp, 2 * mp + 1):
                        ahead(t.u)
                        used(t.u)
                        act.activation(SG[:, j % 2, :], PS[:, 4 + t.pp % 2, T:2 * T], ACT.Sigmoid)\
                            .then_inc(S["glu_sig"], 1)
                        t.u += 1
                        t.pp += 1
                    act.wait_ge(S["glu_mul"], 2 * mp + 2)
                ahead(t.u)
                squares(ready)

            def last_mixer():
                def wide(n):
                    return 4 + 2 * (n % 2)

                def taken(dst, src, **kw):
                    act.activation(dst, src, ACT.Copy, **kw).then_inc(S["wide_taken"], 1)
                    t.wide += 1

                def step():
                    ahead(t.u)
                    used(t.u)
                    t.u += 1

                act.wait_ge(S["lb_d"], 1)
                act.activation(LBD, LBD, ACT.Exp).then_inc(S["lb_e"], 1)
                for i, (c, n) in enumerate(((CKV, 512), (CQ, T))):
                    step()
                    b = wide(t.wide)
                    if i == 0:
                        taken(c, PS[:, b:b + 2, :])
                    else:
                        taken(c, PS[:, b, :].rearrange("p (a b) -> p a b", a=2))
                    act.wait_ge(S["wide_taken"], t.wide)
                    if i == 1:
                        act.wait_ge(S["csum"], 1)
                    act.activation(CSQ[:, :, 0:n], c, ACT.Square).then_inc(S["csq"], 1)
                act.activation(RC, PS[:, 0, :], ACT.Sqrt, bias=vcol("eps", 0), scale=1.0 / 256)\
                    .then_inc(S["crms"], 1)
                for i in range(2):
                    step()
                    b = wide(t.wide)
                    taken(HV[:, :, 256 * i:256 * i + 256], PS[:, b:b + 2, :].rearrange("p a (c f) -> p (a c) f", c=2))
                    if i == 0:
                        act.wait_ge(S["csum"], 2)
                        act.activation(RQ, PS[:, 1, 0:T], ACT.Sqrt, bias=vcol("eps", 0), scale=1.0 / 256)\
                            .then_inc(S["crms"], 1)
                step()
                taken(KPE[0:64], PS[0:64, wide(t.wide), :])
                scale = float(NOPE + ROPE) ** -0.5
                act.activation(QN, PS[:, 0:2, :].rearrange("p a (b c) -> p (a b) c", b=2), ACT.Copy, scale=scale)\
                    .then_inc(S["q_out"], 1)
                act.activation(QR[0:64], PS[0:64, 2:4, :].rearrange("p a (b c) -> p (a b) c", b=2), ACT.Copy,
                               scale=scale).then_inc(S["q_out"], 1)
                ahead(t.u)
                for i in range(4):
                    if i < 3:
                        act.wait_ge(S["kv_part"], i + 1)
                    else:
                        used(t.u)
                    b = wide(t.wide)
                    dst = KN if i < 2 else V2
                    taken(dst[:, 2 * (i % 2):2 * (i % 2) + 2, :], PS[:, b:b + 2, :])
                t.u += 1

                def item(i):
                    act.wait_ge(S["mla_mx"], i + 1)
                    if i >= 2:
                        act.wait_ge(S["mla_t"], i - 1)
                    act.activation(PB[:, i % 2, :], PS[:, i % 2, :], ACT.Exp, bias=NMX[:, i:i + 1],
                                   accum_out=PSM[:, i:i + 1]).then_inc(S["mla_p"], 1)

                n = 0
                for i in range(6):
                    step()
                    b = wide(t.wide)
                    if i < 4:
                        dst = HQ if i < 2 else HG
                        taken(dst[:, 2 * (i % 2):2 * (i % 2) + 2, :], PS[:, b, :].rearrange("p (a b) -> p a b", a=2))
                    else:
                        for s in range(2):
                            a = act.activation(GK[0][:, s, 2 * (i % 2):2 * (i % 2) + 2, :],
                                               PS[:, b:b + 2, s * T:(s + 1) * T], ACT.Copy)
                        a.then_inc(S["wide_taken"], 1)
                        t.wide += 1
                    for _ in range(2 if i < 4 else 0):
                        item(n)
                        n += 1
                act.wait_ge(S["mla_om"], 8)
                for i in range(2):
                    step()
                    b = wide(t.wide)
                    for s in range(2):
                        a = act.activation(GK[1][:, s, 2 * i:2 * i + 2, :], PS[:, b:b + 2, s * T:(s + 1) * T], ACT.Copy)
                    a.then_inc(S["wide_taken"], 1)
                    t.wide += 1
                act.activation(HG, HG, ACT.Silu).then_inc(S["hg_ready"], 1)
                silu_c(2)
                for k in range(4):
                    a = act.activation(XH[:, k, 0:T], QN[:, k, :], ACT.Copy)
                a.then_inc(S["op_hi"], 1)
                act.wait_ge(S["wide_taken"], t.wide)
                for d in range(2):
                    act.activation(GK[d], GK[d], ACT.Sigmoid).then_inc(S["sig_ready"], 1)
                act.preload_act_table_set("natural_log_exp_and_others")
                for d in range(2):
                    act.wait_ge(S["f_ready"], d + 1)
                    act.activation(GL[d], GK[d], ACT.Ln).then_inc(S["lf_ready"], 1)
                for d in range(2):
                    act.wait_ge(S["scan_r"], d + 1)
                    act.activation(W1, W1, ACT.Exp).then_inc(S["exp_r"], 1)
                    act.wait_ge(S["d1_ready"], d + 1)
                    act.activation(QA[d].rearrange("p h t -> p (h t)"), W2, ACT.Exp).then_inc(S["e1_ready"], 1)
                    act.activation(EQ[d].rearrange("p h t -> p (h t)"), W1, ACT.Exp).then_inc(S["e1_ready"], 1)
                    last = 0 if d else CH - 1
                    act.activation(EL[d], W1.rearrange("p (h c t) -> p h c t", h=4, c=4)[:, :, :, last], ACT.Exp)\
                        .then_inc(S["e1_ready"], 1)
                    act.wait_ge(S["e1_ready"], 4 * d + 3)
                    act.activation(W2, W2, ACT.Exp, scale=-1.0).then_inc(S["e1_ready"], 1)
                    act.activation(W3, W3, ACT.Exp, scale=-1.0).then_inc(S["e2_ready"], 1)
                t.u = sum(MODS[1])
                ahead(t.u)
                act.wait_ge(S["h_out"], 1)
                act.activation(W2, PS[:, 0:2, :].rearrange("p a b -> p (a b)"), ACT.Square).then_inc(S["h_sq"], 1)
                act.wait_ge(S["h_sum"], 1)
                act.activation(W3, PS[:, 2:4, :].rearrange("p a b -> p (a b)"), ACT.Sqrt, bias=vcol("eps", 0),
                               scale=1.0 / P).then_inc(S["h_rms"], 1)
                act.wait_ge(S["h_y"], 3)
                act.activation(XH[:, 4:8, 0:T], W1.rearrange("p (h t) -> p h t", h=4), ACT.Copy)\
                    .then_inc(S["op_hi"], 1)
                t.op += 2

                residual()

            act.wait_ge(S["x_in"], 16)
            squares(lambda mp: None)
            split_hi(0)
            t.s += 1
            act.wait_ge(S["vec_in"], 16)
            norm()
            act.activation(DT, DT, ACT.Exp).then_inc(S["s5_dt"], 1)
            attention()
            norm()
            ffn(0)
            norm()
            act.dma_start(GW, sgw).then_inc(S["sg_in"], 16)
            act.dma_start(GB, sgb).then_inc(S["sg_in"], 16)
            gating()
            norm()
            act.dma_start(SBC, sbc).then_inc(S["s5_in"], 16)
            ffn(1, tail=sines)
            norm()
            state_space()
            norm()
            ffn(2)
            norm()
            attention()
            norm()
            act.dma_start(CT, ctxin).then_inc(S["ctx_in"], 16)
            act.dma_start(RP[0:64], ropes).then_inc(S["ctx_in"], 16)

            def context():
                act.wait_ge(S["ctx_in"], 32)
                squares(lambda mp: None, CT)
                norm((0, 1), T)
            ffn(3, aside=context)
            norm_stream()
            norm((0, 0))
            last_mixer()
            norm((3 * KT, 0))
            ffn(0, conv=False)
            rms()

        @block.vector
        def _(dve):
            t = Tally()

            def split_lo(s, it=None):
                u, r = unit_of(s), s % RING
                step = 0 if it is None else it
                dve.wait_ge(S["w_hi"], s + 1 + RING * step)
                dve.tensor_tensor(wlo[:, r, :], raw[:, u % RING, :], whi[:, r, :].bitcast(F32), ALU.subtract)\
                    .then_inc(S["w_lo"], 1)

            def ahead(u):
                while t.s < limit(u) and t.s <= split_index(u) + 2:
                    split_lo(t.s)
                    t.s += 1

            def used(u):
                dve.wait_ge(S["w_used"], u + 1)

            def low(dst, src, hi, n):
                dve.wait_ge(S["op_hi"], n)
                dve.tensor_tensor(dst, src, hi.bitcast(F32), ALU.subtract).then_inc(S["op_lo"], 1)

            def rstd():
                dve.wait_ge(S["rms_ready"], t.norm + 1)
                dve.reciprocal(RSTD, RMS).then_inc(S["rstd_ready"], 1)
                dve.wait_ge(S["rstd_ready"], t.norm + 1)
                t.norm += 1

            def norm(g, src=XT, shift=None, at=0):
                rstd()
                for k in range(KT + 1):
                    if k < KT:
                        dve.scalar_tensor_tensor(XN[:, k, :], src[:, k, :], g(k), RSTD,
                                                 ALU.mult, ALU.mult).then_inc(S["xn_ready"], 1)
                    if k >= 1:
                        m = k - 1
                        if shift is None:
                            low(XL[:, m, at:at + T], XN[:, m, :], XH[:, m, at:at + T], t.op + k)
                        else:
                            dve.wait_ge(S["op_hi"], t.op + k)
                            sh = MODV[:, shift[0] + m, shift[1]:shift[1] + 1]
                            dve.scalar_tensor_tensor(XL[:, m, at:at + T], XN[:, m, :], sh,
                                                     XH[:, m, at:at + T].bitcast(F32), ALU.add, ALU.subtract)\
                                .then_inc(S["op_lo"], 1)
                t.op += KT

            def norm_stream(name):
                rstd()
                for k in range(KT):
                    dve.scalar_tensor_tensor(XT[:, k, :], XT[:, k, :], vcol(name, k), RSTD, ALU.mult, ALU.mult)\
                        .then_inc(S["normed"], 1)
                t.normed += KT

            def modulation_rows(n, bank):
                if n:
                    dve.wait_ge(S["mod_sum"], n)
                dve.tensor_copy(MROW[n], PS[:, bank, :]).then_inc(S["mod_rows"], 1)

            def modulated(n, bank):
                dve.wait_ge(S["mod_sum"], n + 1)
                dve.tensor_tensor(MODV[:, 16 * n:16 * n + 16, :].rearrange("p (q c) r -> p q c r", c=4),
                                  PS[:, bank, 0:32].rearrange("p (c q r) -> p q c r", q=4, r=2),
                                  VEC[:, VC["b_mod"] + 16 * n:VC["b_mod"] + 16 * n + 16]
                                  .rearrange("p (q c) -> p q c", c=4).unsqueeze(3).broadcast_to([P, 4, 4, 2]),
                                  ALU.add).then_inc(S["mod_vec"], 1)

            def modulated_gain(i):
                sc = MODV[:, (3 * i + 1) * KT:(3 * i + 2) * KT, :]
                name = ("g_mix", "g_ffn")[i]
                g = VEC[:, VC[name]:VC[name] + KT].unsqueeze(2).broadcast_to([P, KT, 2])
                dve.scalar_tensor_tensor(MODG[:, i], sc, 1.0, g, ALU.add, ALU.mult).then_inc(S["mod_gain"], 1)

            def gain(i):
                return lambda k: vcol("norm_g", i * KT + k)

            def mod_gain(i, s):
                return lambda k: MODG[:, i, k, s:s + 1]

            def residual():
                for mp in range(4):
                    ahead(t.u)
                    used(t.u)
                    x = XT[:, 2 * mp:2 * mp + 2, :]
                    dve.tensor_tensor(x, PS[:, 4 + t.pp % 2, :].rearrange("p (a b) -> p a b", a=2), x, ALU.add)\
                        .then_inc(S["pp_taken"], 1)
                    t.u += 1
                    t.pp += 1

            def ffn(layer, conv=True, aside=None):
                u0, q0, up0, hid0 = t.u, t.pp, t.up, t.hid

                def up(j, it=None):
                    k = 0 if it is None else it
                    bank = PS[:, 4 + (q0 + j) % 2, :].rearrange("p (a b) -> p a b", a=2)
                    if conv:
                        dve.wait_ge(S["conv0"], up0 + j + 1 + 2 * k)
                        for back in (1, 2):
                            for i in range(2):
                                c = VC["conv"] + (layer * FT + j) * 8 + 4 * i + 2 - back
                                w = VEC[:, c:c + 1] if it is None else VEC[:, bass.ds(it * 16 + c, 1)]
                                y = CA[:, j % 2, i, back:T]
                                ins = dve.scalar_tensor_tensor(y, bank[:, i, 0:T - back], w, y, ALU.mult, ALU.add)
                            if back == 1:
                                ins.then_inc(S["conv1"], 1)
                                dve.wait_ge(S["conv1"], up0 + j + 1 + 2 * k)
                            else:
                                ins.then_inc(S["pp_taken"], 1)
                        dve.wait_ge(S["silu_ready"], up0 + j + 1 + 2 * k)
                        dve.tensor_tensor(HID[:, j % 2, :], CA[:, j % 2, 0, :], SG[:, j % 2, :], ALU.mult)\
                            .then_inc(S["hid_ready"], 1)
                    else:
                        if j == 2:
                            dve.wait_ge(S["hl_ready"], hid0 + 1 + k)
                        dve.wait_ge(S["silu_ready"], up0 + j + 1 + 2 * k)
                        dve.tensor_tensor(HID[:, j % 2, :], bank[:, 0, :], SG[:, j % 2, :], ALU.mult)\
                            .then_inc(S["pp_taken"], 1)

                def hidden(h, it=None):
                    k = 0 if it is None else it
                    dve.wait_ge(S["hh_ready"], hid0 + h + 1 + k)
                    dve.tensor_tensor(HL[:, :, :], HID, HH[:, :, :].bitcast(F32), ALU.subtract)\
                        .then_inc(S["hl_ready"], 1)

                for j in range(2):
                    ahead(u0 + j)
                    up(j)
                hidden(0)
                if aside:
                    aside()
                n = FT // 2 - 1
                s1 = t.s
                with dve.Fori(0, n) as it:
                    for j in range(2):
                        split_lo(s1 + j, it)
                        up(2 + j, it)
                    split_lo(s1 + 2, it)
                    hidden(1, it)
                t.s += 3 * n
                t.u = u0 + 2 + 3 * n
                ahead(t.u)
                for mp in range(4):
                    if mp < 3:
                        dve.wait_ge(S["acc_ready"], 3 * (t.acc // 4) + mp + 1)
                    else:
                        used(t.u)
                    if conv:
                        x = XT[:, 2 * mp:2 * mp + 2, :]
                        ins = dve.tensor_tensor(x, PS[:, mp, :].rearrange("p (a b) -> p a b", a=2), x, ALU.add)
                    else:
                        for m in (2 * mp, 2 * mp + 1):
                            ins = dve.scalar_tensor_tensor(XT[:, m, :], PS[:, mp, (m % 2) * T:(m % 2 + 1) * T],
                                                           MODV[:, 5 * KT + m, 0:1], XT[:, m, :],
                                                           ALU.mult, ALU.add)
                    ins.then_inc(S["acc_taken"], 1)
                t.acc += 4
                t.u += 1
                t.pp += FT
                t.up += FT
                t.hid += FT // 2

            def attention():
                for n in range(12):
                    ahead(t.u)
                    t.u += 1
                    t.pp += 1
                n0 = t.att
                for p in range(10):
                    r = p % 3
                    if p < 8:
                        dve.wait_ge(S["sc_ready"], n0 + p + 1)
                        z = PS[:, 2 * r:2 * r + 2, 0:384]
                        dve.tensor_scalar(ZC[:, p % 2, :].rearrange("p (a b) -> p a b", a=2), z, 40.0, None,
                                          ALU.min).then_inc(S["zc_ready"], 1)
                        dve.wait_ge(S["ln_ready"], n0 + p + 1)
                        dve.tensor_tensor(SP[:, p % 2, :].rearrange("p (a b) -> p a b", a=2), z,
                                          LN[:, p % 2, :].rearrange("p (a b) -> p a b", a=2), ALU.max)\
                            .then_inc(S["sp_ready"], 1)
                    if p >= 2:
                        low(XL[:, p - 2, 0:T], PS[:, 6 + p % 2, 0:T], XH[:, p - 2, 0:T], t.op + p - 1)
                t.att += 8
                t.op += KT
                residual()

            def gating():
                for n in range(4):
                    ahead(t.u)
                    t.u += 1
                    t.pp += 1
                dve.wait_ge(S["pp_taken"], t.pp)
                dve.wait_ge(S["sg_in"], 32)
                for g in range(8):
                    dve.tensor_tensor(GW[:, g, :], GW[:, g, :], tril, ALU.mult).then_inc(S["gtril"], 1)
                for c in range(2):
                    dve.tensor_tensor_reduce(GJ[:, c, :], GV[:, c, :], GV[:, c, :], 1.0, 0.0, ALU.mult, ALU.add,
                                             SM[:, c:c + 1]).then_inc(S["gss_ready"], 1)
                dve.wait_ge(S["grms_ready"], 1)
                dve.reciprocal(SM[:, 4:6], SM[:, 2:4]).then_inc(S["grstd_ready"], 1)
                dve.wait_ge(S["grstd_ready"], 1)
                for c in range(2):
                    dve.tensor_scalar(GV[:, c, :], GV[:, c, :], SM[:, 4 + c:5 + c], None, ALU.mult)\
                        .then_inc(S["gvn_ready"], 1)
                for n in range(2):
                    ahead(t.u + n)
                for g in range(8):
                    if g % 2 == 0:
                        dve.wait_ge(S["mix_ready"], g // 2 + 1)
                    dve.scalar_tensor_tensor(
                        GS[:, g, :].rearrange("p (c t) -> p c t", c=2),
                        PS[:, g // 2, (g % 2) * T:(g % 2 + 1) * T].rearrange("p (c t) -> p c t", c=2),
                        vcol("sg_norm_g", g), GB[:, g, :].unsqueeze(1).broadcast_to([P, 2, P]),
                        ALU.mult, ALU.add).then_inc(S["gs_ready"], 1)
                for n in range(4):
                    if n >= 2:
                        ahead(t.u)
                    dve.wait_ge(S["pp_taken"], t.pp + 1)
                    dve.wait_ge(S["gs_ready"], 8)
                    gu = GU[:, 2 * n:2 * n + 2, :]
                    dve.tensor_tensor(gu, gu, GS[:, 2 * n:2 * n + 2, :], ALU.mult).then_inc(S["gy_ready"], 1)
                    t.u += 1
                    t.pp += 1
                    if n >= 1:
                        m = 2 * n - 2
                        low(XL[:, m:m + 2, 0:T], GU[:, m:m + 2, :], XH[:, m:m + 2, 0:T], t.op + n)
                low(XL[:, 6:8, 0:T], GU[:, 6:8, :], XH[:, 6:8, 0:T], t.op + 4)
                t.op += 4
                residual()

            links = [0]

            def link(ins):
                links[0] += 1
                ins.then_inc(S["link"], 1)
                dve.wait_ge(S["link"], links[0])

            def turned():
                dve.wait_ge(S["s5_turned"], 1)
                dve.wait_ge(S["s5_clear"], 1)
                for i, b in enumerate((BRE, BIM)):
                    for q in range(4):
                        r = slice(32 * q, 32 * q + 32)
                        dve.tensor_copy(b[r, :, q % 2, :],
                                        PS[r, 2 * i:2 * i + 2, :].rearrange("p a (k n) -> p (a k) n", n=P))\
                            .then_inc(S["s5_b"], 1)

            def state_space():
                for n in range(4):
                    ahead(t.u)
                    if n == 0:
                        dve.memset(SCP, 0.0).then_inc(S["scp_nil"], 1)
                        dve.wait_ge(S["s5_bt"], 4)
                        dve.tensor_copy(AR64, AER)
                        dve.tensor_copy(AI64, AEI).then_inc(S["s5_moved"], 1)
                        link(dve.memset(SM[:, 64:128], 0.0))
                    if n == 2:
                        turned()
                    t.u += 1
                    t.pp += 1
                dve.wait_ge(S["s5_moved"], 1)
                t.u += MODS[0][1]

                def tables(s):
                    _, qd = step5(s)
                    return (AR[:, B0 + 2048 * i + 512 * qd:B0 + 2048 * i + 512 * qd + 512] for i in range(3))

                def jumps(s):
                    return 2 * (s + 1 if s < 8 else 9 + (s - 8) // 2)

                def pairs(v):
                    return v.rearrange("p (a b) -> p a b", a=8)

                def products(s):
                    wk = W5[s % 3]
                    tc, ts, _ = tables(s)
                    dve.wait_ge(S["bu_ready"], s // 2 + 1)
                    if s >= 3:
                        dve.wait_ge(S["y5_ready"], s - 2)
                    re, im = (PS[:, b:b + 2, :].rearrange("p a (n t) -> p (a n) t", t=128)[:, :, 64 * (s % 2):64 * (s % 2) + 64]
                              for b in (0, 2))
                    dve.tensor_tensor(pairs(wk[0]), re, pairs(tc), ALU.mult)
                    dve.tensor_tensor(pairs(wk[1]), im, pairs(ts), ALU.mult)
                    dve.tensor_tensor(pairs(wk[2]), im, pairs(tc), ALU.mult)
                    dve.tensor_tensor(pairs(wk[3]), re, pairs(ts), ALU.mult).then_inc(S["bu_mult"], 1)

                def scans(s):
                    wk = W5[s % 3]
                    tc, ts, mg = tables(s)
                    c, qd = step5(s)
                    c8 = slice(8 * qd, 8 * qd + 8)
                    dve.wait_ge(S["v_ready"], s + 1)
                    if c:
                        dve.wait_ge(S["jump"], jumps(s - 1 if c % 2 else s - 7))
                        for v, j in ((wk[0], JRE), (wk[2], JIM)):
                            v0 = v.rearrange("p (a b) -> p a b", b=64)[:, :, 0]
                            ins = dve.tensor_tensor(v0, v0, j[:, c8], ALU.add)
                        link(ins)
                    dve.tensor_tensor_scan(wk[1], mg, wk[0], 0.0, ALU.mult, ALU.add)
                    dve.tensor_tensor_scan(wk[3], mg, wk[2], 0.0, ALU.mult, ALU.add)\
                        .then_inc(S["scan_ready"], 1)
                    dve.wait_ge(S["scan_ready"], s + 1)
                    dve.tensor_tensor(wk[0], wk[1], tc, ALU.mult)
                    dve.scalar_tensor_tensor(wk[2], wk[3], -1.0, ts, ALU.mult, ALU.mult)\
                        .then_inc(S["rot_ready"], 1)
                    if c < 3:
                        zr, zi = (v.rearrange("p (a b) -> p a b", b=64)[:, :, 63] for v in (wk[1], wk[3]))
                        for o, x, y in ((JA, AR64, zr), (JB, AI64, zi), (JC, AR64, zi), (JD, AI64, zr)):
                            ins = dve.tensor_tensor(o[:, c8], x[:, c8], y, ALU.mult)
                        ins.then_inc(S["jump_parts"], 1)
                        dve.wait_ge(S["jump_parts"], jumps(s) // 2)
                        dve.tensor_tensor(JRE[:, c8], JA[:, c8], JB[:, c8], ALU.subtract).then_inc(S["jump"], 1)
                        dve.tensor_tensor(JIM[:, c8], JC[:, c8], JD[:, c8], ALU.add).then_inc(S["jump"], 1)

                def outputs(c):
                    tok = slice(64 * c, 64 * c + 64)
                    dve.wait_ge(S["y5_ready"], 8 * (c // 2) + 7 + c % 2)
                    for k in range(KT):
                        ins = dve.scalar_tensor_tensor(U5[:, k, tok], U5[:, k, tok], vcol("ssm_d", k),
                                                       PS[:, 4 + c % 2, 64 * k:64 * k + 64], ALU.mult, ALU.add)
                    ins.then_inc(S["y5_sum"], 1)

                def lows(c):
                    tok = slice(64 * c, 64 * c + 64)
                    low(XL[:, :, tok], U5[:, :, tok], XH[:, :, tok], t.op + c + 1)

                for b in range(8):
                    for s in (2 * b, 2 * b + 1):
                        products(s)
                    for s in (2 * b, 2 * b + 1):
                        scans(s)
                        if b == 4:
                            outputs(s % 2)
                        if b == 5:
                            lows(s % 2)
                outputs(2)
                outputs(3)
                lows(2)
                lows(3)
                t.op += 4
                dve.wait_ge(S["w_used"], sum(MODS[0]))
                modulation_rows(0, 7)
                ahead(t.u)
                for j in range(KT):
                    ahead(t.u)
                    if j == 1:
                        modulated(0, 7)
                        dve.wait_ge(S["mod_vec"], 1)
                        modulated_gain(0)
                    dve.wait_ge(S["glu_sig"], j + 1)
                    dve.tensor_tensor(CA[:, j % 2, 0, :], PS[:, 4 + t.pp % 2, 0:T], SG[:, j % 2, :], ALU.mult)\
                        .then_inc(S["pp_taken"], 1)
                    dve.wait_ge(S["pp_taken"], t.pp + 1)
                    dve.tensor_tensor(XT[:, j, :], XT[:, j, :], CA[:, j % 2, 0, :], ALU.add)\
                        .then_inc(S["glu_mul"], 1)
                    t.u += 1
                    t.pp += 1

            def last_mixer():
                dve.memset(SCP, 0.0).then_inc(S["scp_nil"], 1)
                raw_lb = VEC[:, VC["lb_fwd"]:VC["lb_fwd"] + 16].rearrange("p (d h r) -> p d h r", d=2, h=4)
                link(dve.tensor_tensor(LBM, raw_lb[:, :, :, 0], raw_lb[:, :, :, 1], ALU.max))
                link(dve.tensor_tensor(LBD[:, :, :, 0], raw_lb[:, :, :, 0], LBM, ALU.subtract))
                dve.tensor_tensor(LBD[:, :, :, 1], raw_lb[:, :, :, 1], LBM, ALU.subtract).then_inc(S["lb_d"], 1)
                dve.wait_ge(S["lb_e"], 1)
                link(dve.tensor_tensor(LBS, LBD[:, :, :, 0], LBD[:, :, :, 1], ALU.add))
                link(dve.reciprocal(LBS, LBS))
                link(dve.tensor_tensor(LBV, LBD[:, :, :, 0], LBS, ALU.mult))
                link(dve.tensor_scalar(OML, LBV, -1.0, 1.0, ALU.mult, ALU.add))

                for _ in range(2):
                    ahead(t.u)
                    t.u += 1
                for i, (c, r, g) in enumerate(((CKV, RC, "g_kv"), (CQ, RQ, "g_q"))):
                    ahead(t.u)
                    t.u += 1
                    dve.wait_ge(S["crms"], i + 1)
                    dve.reciprocal(r, r).then_inc(S["crinv"], 1)
                    dve.wait_ge(S["crinv"], i + 1)
                    for k in range(2):
                        dve.scalar_tensor_tensor(c[:, k, :], c[:, k, :], vcol(g, k), r, ALU.mult, ALU.mult)\
                            .then_inc(S["cnormed"], 1)
                ahead(t.u)
                t.u += 1
                ahead(t.u)
                t.u += 1
                cos, sin = RP[0:64, 0, :], RP[0:64, 1, :]

                def b4(v):
                    return v.unsqueeze(1).broadcast_to([64, 4, T])
                for i, (x, rot, cc, ss) in enumerate((
                        (KPE[0:64, 0:T], PS[0:64, 2, 0:T], cos, sin),
                        (QR[0:64], PS[0:64, 0:2, :].rearrange("p a (b c) -> p (a b) c", b=2), b4(cos), b4(sin)))):
                    dve.wait_ge(S["rot"], i + 1)
                    ta, tb = (v[:, 0:T] if i == 0 else v.rearrange("p (a b) -> p a b", a=4) for v in RT)
                    link(dve.tensor_tensor(ta, x, cc, ALU.mult))
                    link(dve.tensor_tensor(tb, rot, ss, ALU.mult))
                    dve.tensor_tensor(x, ta, tb, ALU.add).then_inc(S["roped"], 1)
                    dve.wait_ge(S["roped"], i + 1)

                def item(i):
                    if i < 8:
                        dve.wait_ge(S["mla_s"], i + 1)
                        link(dve.reduce_max(MX[:, i:i + 1], PS[:, i % 2, :], AX.X))
                        dve.tensor_scalar(NMX[:, i:i + 1], MX[:, i:i + 1], -1.0, None, ALU.mult)\
                            .then_inc(S["mla_mx"], 1)
                    if 1 <= i < 9:
                        j = i - 1
                        dve.wait_ge(S["mla_p"], j + 1)
                        link(dve.reciprocal(PRS[:, j:j + 1], PSM[:, j:j + 1]))
                        dve.tensor_scalar(PB[:, j % 2, :], PB[:, j % 2, :], PRS[:, j:j + 1], None, ALU.mult)\
                            .then_inc(S["mla_pn"], 1)
                        dve.wait_ge(S["mla_t"], j + 1)
                        dve.tensor_copy(PT[:, j % 2, :], PS[:, 2, :]).then_inc(S["mla_pt"], 1)
                    if i >= 2:
                        j = i - 2
                        dve.wait_ge(S["mla_o"], j + 1)
                        dve.tensor_copy(QN[:, j // 2, (j % 2) * P:(j % 2 + 1) * P], PS[:, 3, 0:P])\
                            .then_inc(S["mla_om"], 1)

                n = 0
                for i in range(6):
                    ahead(t.u)
                    t.u += 1
                    for _ in range(2 if i < 4 else 1):
                        item(n)
                        n += 1
                for i in range(2):
                    ahead(t.u)
                    t.u += 1
                dve.wait_ge(S["op_hi"], t.op + 1)
                dve.wait_ge(S["mla_om"], 8)
                for k in range(4):
                    ins = dve.tensor_tensor(XL[:, k, 0:T], QN[:, k, :], XH[:, k, 0:T].bitcast(F32), ALU.subtract)
                ins.then_inc(S["op_lo"], 1)
                link(dve.memset(M64, 1.0))
                link(dve.memset(M64.rearrange("p (a b) -> p a b", b=CH)[:, :, 0:1], 0.0))
                for d in range(2):
                    dve.wait_ge(S["sig_ready"], d + 1)
                    for h in range(4):
                        g = GK[d][:, :, h, :]
                        ins = dve.tensor_scalar(g, g, OML[:, d, h:h + 1], LBV[:, d, h:h + 1], ALU.mult, ALU.add)
                    ins.then_inc(S["f_ready"], 1)
                for d in range(2):
                    dve.wait_ge(S["lf_ready"], d + 1)
                    link(dve.tensor_scalar(GK[d], GK[d], -1.0, 1.0, ALU.mult, ALU.add))
                    t1 = W1.rearrange("p (h t) -> p h t", h=4)
                    for h in range(4):
                        for half in range(2):
                            lo = P * ((1 - half) if d == 0 else half)
                            first = lo + P - 1 if d == 0 else lo
                            before = first + 1 if d == 0 else first - 1
                            init = t1[:, h, before:before + 1] if half else 0.0
                            g, o = GL[d][:, 1, h, lo:lo + P], t1[:, h, lo:lo + P]
                            if d == 0:
                                g, o = g[:, ::-1], o[:, ::-1]
                            link(dve.tensor_tensor_scan(o, ones, g, init, ALU.mult, ALU.add))
                    dve.tensor_tensor(t1, t1, GL[d][:, 1], ALU.subtract).then_inc(S["scan_r"], 1)
                    dve.wait_ge(S["exp_r"], d + 1)
                    dve.tensor_tensor(GK[d][:, 1], GK[d][:, 1], t1, ALU.mult).then_inc(S["kw_ready"], 1)
                    dve.wait_ge(S["kw_ready"], d + 1)
                    g = GL[d][:, 0].rearrange("p h t -> p (h t)")
                    if d == 0:
                        link(dve.tensor_tensor_scan(W1, M64, g, 0.0, ALU.mult, ALU.add))
                    else:
                        link(dve.tensor_tensor_scan(W1[:, ::-1], M64, g[:, ::-1], 0.0, ALU.mult, ALU.add))
                    b = W1.rearrange("p (c t) -> p c t", t=CH)
                    mid, end = (CH // 2, 0) if d else (CH // 2 - 1, CH - 1)
                    for tt, at in ((W2, mid), (W3, end)):
                        ins = dve.tensor_tensor(tt.rearrange("p (c t) -> p c t", t=CH), b,
                                                b[:, :, at:at + 1].broadcast_to([P, 16, CH]), ALU.subtract)
                        if at == mid:
                            link(ins)
                    ins.then_inc(S["d1_ready"], 1)
                    dve.wait_ge(S["e1_ready"], 4 * d + 4)
                    dve.wait_ge(S["e2_ready"], d + 1)
                    link(dve.tensor_tensor(QA[d], QA[d], HQ, ALU.mult))
                    link(dve.tensor_tensor(EQ[d], EQ[d], HQ, ALU.mult))
                    link(dve.tensor_tensor(KA[d], W2.rearrange("p (h t) -> p h t", h=4), GK[d][:, 0], ALU.mult))
                    dve.tensor_tensor(GK[d][:, 0], W3.rearrange("p (h t) -> p h t", h=4), GK[d][:, 0], ALU.mult)\
                        .then_inc(S["qk_ready"], 1)
                    dve.wait_ge(S["qk_ready"], d + 1)
                kwt = W1, W2
                for d in range(2):
                    dve.wait_ge(S["kwt"], d + 1)
                    dve.tensor_copy(kwt[d], PS[:, 4 + 2 * d:6 + 2 * d, :].rearrange("p a b -> p (a b)"))\
                        .then_inc(S["kwt_out"], 1)
                for d in range(2):
                    dve.wait_ge(S["s0_sum"], d + 1)
                    dve.tensor_copy(ST[:, d].rearrange("p h v -> p (h v)"), PS[:, 2 + d, :])\
                        .then_inc(S["s_ready"], 1)
                for n in (1, 2):
                    dve.wait_ge(S["w_used"], MODS[1][0] + 8 * n)
                    modulation_rows(n, n - 1)
                    modulated(n, 5 + n)
                dve.wait_ge(S["mod_vec"], 3)
                modulated_gain(1)
                t.u = sum(MODS[1])
                ahead(t.u)
                link(dve.memset(ATS, 0.0))
                n = 0
                for i in range(4):
                    for d in range(2):
                        c = 3 - i if d else i
                        r = slice(64 * (c % 2), 64 * (c % 2) + 64)
                        n += 1
                        mask = CST[r, CTB:CTB + CH] if d else tril[r, r]
                        dve.wait_ge(S["at_sum"], n)
                        a4 = lambda v: v.rearrange("p (h t) -> p h t", h=4)
                        for rows, cols in quarters(d):
                            rr = slice(r.start + rows.start, r.start + rows.stop)
                            w = cols.stop - cols.start
                            ins = dve.tensor_tensor(a4(ATS[rr, d, c % 2, :])[:, :, cols], a4(PS[rr, 2 + d, 0:256])[:, :, cols],
                                                    mask[rows, cols].unsqueeze(1).broadcast_to([CH // 2, 4, w]),
                                                    ALU.mult)
                        ins.then_inc(S["at_out"], 1)
                        if i < 3:
                            dve.wait_ge(S["kd_sum"], n)
                            dve.tensor_copy(KDS[r, d, :], PS[r, 4 + d, :]).then_inc(S["kd_out"], 1)
                    for d in range(2):
                        c = 3 - i if d else i
                        if i < 3:
                            dve.wait_ge(S["su_sum"], 2 * i + d + 1)
                            for h in range(4):
                                ins = dve.scalar_tensor_tensor(
                                    ST[:, d, h, :], ST[:, d, h, :], EL[d][:, h, c:c + 1],
                                    PS[:, 6 + d, h * P:(h + 1) * P], ALU.mult, ALU.add)
                            ins.then_inc(S["s_ready"], 1)
                dve.wait_ge(S["h_rms"], 1)
                link(dve.reciprocal(W3, W3))
                for b in range(2):
                    dve.scalar_tensor_tensor(W1[:, 512 * b:512 * b + 512], PS[:, b, :], vcol("g_on", 0),
                                             W3[:, 512 * b:512 * b + 512], ALU.mult, ALU.mult)\
                        .then_inc(S["h_y"], 1)
                dve.wait_ge(S["h_y"], 2)
                dve.wait_ge(S["hg_ready"], 1)
                dve.tensor_tensor(W1, W1, HG.rearrange("p h t -> p (h t)"), ALU.mult).then_inc(S["h_y"], 1)
                dve.wait_ge(S["h_y"], 3)
                low(XL[:, 4:8, 0:T], W1.rearrange("p (h t) -> p h t", h=4), XH[:, 4:8, 0:T], t.op + 2)
                t.op += 2
                for mp in range(4):
                    ahead(t.u)
                    used(t.u)
                    for m in (2 * mp, 2 * mp + 1):
                        b = PS[:, 4 + t.pp % 2, (m % 2) * T:(m % 2 + 1) * T]
                        ins = dve.scalar_tensor_tensor(XT[:, m, :], b, MODV[:, 2 * KT + m, 0:1], XT[:, m, :],
                                                       ALU.mult, ALU.add)
                    ins.then_inc(S["pp_taken"], 1)
                    t.u += 1
                    t.pp += 1

            dve.memset(ZB[:, :], 0.0).then_inc(S["setup"], 1)
            dve.wait_ge(S["const_in"], 16)
            dve.tensor_copy(IDB[:, :], ident).then_inc(S["setup"], 1)
            dve.tensor_copy(MKB[:, :], CST[:, CMK:CMK + P]).then_inc(S["setup"], 1)
            split_lo(0)
            t.s += 1
            dve.wait_ge(S["vec_in"], 16)
            norm(gain(0))
            link(dve.tensor_scalar(LR, LR, -1e-4, None, ALU.min))
            link(dve.tensor_tensor(DEN, LR, LR, ALU.mult))
            link(dve.tensor_tensor(DENI, LI, LI, ALU.mult))
            link(dve.tensor_tensor(DEN, DEN, DENI, ALU.add))
            dve.reciprocal(DEN, DEN).then_inc(S["s5_den"], 1)
            attention()
            norm(gain(1))
            ffn(0)
            norm(gain(2))
            gating()
            norm(gain(3))
            ffn(1)
            norm(gain(4))
            state_space()
            norm(gain(5))
            ffn(2)
            norm(gain(6))
            attention()
            norm(gain(7))

            def context():
                dve.wait_ge(S["ctx_in"], 32)
                norm(mod_gain(0, 1), CT, (0, 1), T)
            ffn(3, aside=context)
            norm_stream("final_norm_g")
            norm(mod_gain(0, 0), XT, (0, 0))
            last_mixer()
            norm(mod_gain(1, 0), XT, (3 * KT, 0))
            ffn(0, conv=False)
            norm_stream("g_final")

        @block.tensor
        def _(pe):
            t = Tally()

            def product(dst, stat, mov, first, last, **kw):
                (sh, sl), (mh, ml) = stat, mov
                pe.matmul(dst, sh, mh, start=first, stop=False, **kw)
                pe.matmul(dst, sh, ml, start=False, stop=False, **kw)
                return pe.matmul(dst, sl, mh, start=False, stop=last, **kw)

            def w(slot, a, b):
                return whi[:, slot, a:b], wlo[:, slot, a:b]

            def x(k, a=0, b=T):
                return XH[:, k, a:b], XL[:, k, a:b]

            def modulation(g, bank):
                pe.wait_ge(w_loaded[t.u % RING], 16 * (t.u // RING + 1))
                for k in range(KT):
                    mm = pe.matmul(PS[32 * (g // 2):32 * (g // 2) + 32, bank, (g % 2) * 256:(g % 2) * 256 + 256],
                                   SCP[:, k, :], raw[:, t.u % RING, k * 256:(k + 1) * 256],
                                   start=(k == 0), stop=(k == KT - 1))
                mm.then_inc(S["w_used"], 1)
                t.u += 1

            def modulation_turned(n, bank):
                pe.wait_ge(S["mod_rows"], n + 1)
                rows = ident.rearrange("p (q r) -> p q r", r=32)[:, :, 0:2]
                for c in range(4):
                    mm = pe.matmul(PS[:, bank, 8 * c:8 * c + 8], MROW[n][:, c * P:(c + 1) * P], rows,
                                   start=True, stop=True)
                mm.then_inc(S["mod_sum"], 1)

            def fresh_bank():
                if t.pp >= 2:
                    pe.wait_ge(S["pp_taken"], t.pp - 1)
                t.pp += 1
                return 4 + (t.pp - 1) % 2

            def operand(first, k, per=1):
                if first and k % per == 0:
                    pe.wait_ge(S["op_lo"], t.op + k // per + 1)

            def unit_ready(u):
                pe.wait_ge(S["w_lo"], split_index(u) + 1)
                return split_index(u) % RING

            def features(first=False, per=1):
                b = fresh_bank()
                slot = unit_ready(t.u)
                for m in range(2):
                    for k in range(KT):
                        operand(first and m == 0, k, per)
                        mm = product(PS[:, b, m * T:(m + 1) * T], w(slot, k * 256 + m * P, k * 256 + m * P + P),
                                     x(k), k == 0, k == KT - 1)
                mm.then_inc(S["w_used"], 1)
                t.u += 1

            def tokens(first=False):
                b = fresh_bank()
                slot = unit_ready(t.u)
                for c in range(2):
                    for k in range(KT):
                        operand(first and c == 0, k)
                        mm = product(PS[:, b, c * 256:(c + 1) * 256], x(k, c * P, (c + 1) * P),
                                     w(slot, k * 256, (k + 1) * 256), k == 0, k == KT - 1)
                mm.then_inc(S["w_used"], 1)
                t.u += 1

            def sums(mp):
                pe.wait_ge(S["sq_ready"], 4 * t.norm + mp + 1)
                for k in (2 * mp, 2 * mp + 1):
                    mm = pe.matmul(PS[:, 6, 0:T], ones, SQ[:, k, :], start=(k == 0), stop=(k == KT - 1))
                if mp == 3:
                    mm.then_inc(S["norm_sum"], 1)
                    t.norm += 1

            def residual(per):
                for mp in range(4):
                    features(mp == 0, per)
                    if mp >= 1:
                        sums(mp - 1)
                sums(3)
                t.op += KT // per

            def ffn(aside=None):
                u0, q0, hid0 = t.u, t.pp, t.hid

                def up(j, it=None):
                    k = 0 if it is None else it
                    u = u0 + 2 + 3 * (j // 2 - 1) + j % 2 if j >= 2 else u0 + j
                    if q0 + j >= 2:
                        pe.wait_ge(S["pp_taken"], q0 + j - 1 + 2 * k)
                    pe.wait_ge(S["w_lo"], split_index(u) + 1 + 3 * k)
                    slot = split_index(u) % RING
                    for m in range(2):
                        for kt in range(KT):
                            operand(it is None and j == 0 and m == 0, kt)
                            mm = product(PS[:, 4 + (q0 + j) % 2, m * T:(m + 1) * T],
                                         w(slot, kt * 256 + m * P, kt * 256 + m * P + P),
                                         x(kt), kt == 0, kt == KT - 1)
                    mm.then_inc(S["w_used"], 1)

                def down(h, it=None, last=False):
                    k = 0 if it is None else it
                    u = u0 + 4 + 3 * h
                    if last:
                        u = u0 + 3 * FT // 2 - 1
                    pe.wait_ge(S["hl_ready"], hid0 + h + 1 + k)
                    pe.wait_ge(S["w_lo"], split_index(u) + 1 + 3 * k)
                    slot = split_index(u) % RING
                    for m in range(KT):
                        for i in range(2):
                            mm = product(PS[:, m // 2, (m % 2) * T:(m % 2 + 1) * T],
                                         w(slot, i * D + m * P, i * D + m * P + P),
                                         (HH[:, i, :], HL[:, i, :]), False, last and i == 1,
                                         skip_group_check=True)
                        if last and m in (1, 3, 5):
                            mm.then_inc(S["acc_ready"], 1)
                    mm.then_inc(S["w_used"], 1)

                if t.acc:
                    pe.wait_ge(S["acc_taken"], t.acc)
                for b in range(4):
                    pe.matmul(PS[:, b, :], ZB[:, 0:P], ZB[:, :], start=True, stop=False, skip_group_check=True)
                up(0)
                up(1)
                if aside:
                    aside()
                n = FT // 2 - 1
                with pe.Fori(0, n) as it:
                    up(2, it)
                    up(3, it)
                    down(0, it)
                down(n, last=True)
                t.u += 3 * FT // 2
                t.op += KT
                t.pp += FT
                t.hid += FT // 2
                t.acc += 4
                for mp in range(4):
                    sums(mp)

            def attention():
                for n in range(8):
                    features(n == 0)
                for n in range(4):
                    tokens()
                t.op += KT
                pe.wait_ge(S["pp_taken"], t.pp)
                n0 = t.att
                kw = dict(skip_group_check=True)
                for p in range(10):
                    if p < 8:
                        r = p % 3
                        if p >= 3:
                            pe.wait_ge(S["wb_ready"], n0 + p - 2)
                        for i in range(2):
                            rows = slice(64 * i, 64 * i + 64)
                            b = PS[:, 2 * r + i, :]
                            q, k = QK[rows, p, :], QK[rows, KT + p, :]
                            pe.matmul(b[:, 0:P], IDB[:, :], MKB[:, :], start=True, stop=False, **kw)
                            pe.matmul(b[:, 2 * P:3 * P], IDB[:, :], MKB[:, :], start=False, stop=False, **kw)
                            pe.matmul(b[:, 0:T], k[:, 0:P], q, start=False, stop=True, **kw)
                            mm = pe.matmul(b[:, T:T + P], k[:, P:T], q[:, P:T], start=False, stop=True, **kw)
                        mm.then_inc(S["sc_ready"], 1)
                    if 1 <= p < 9:
                        r = (p - 1) % 3
                        pe.wait_ge(S["sp_ready"], n0 + p)
                        for i in range(2):
                            b = PS[:, 2 * r + i, :]
                            s = SP[:, (p - 1) % 2, 384 * i:384 * i + 384]
                            pe.matmul(b[:, 0:T], negU, s[:, 0:T], start=False, stop=True, **kw)
                            pe.matmul(b[:, P:T], negones, s[:, T:T + P], start=False, stop=True, **kw)
                            mm = pe.matmul(b[:, T:T + P], negU, s[:, T:T + P], start=False, stop=True, **kw)
                        mm.then_inc(S["c_ready"], 1)
                    if p >= 2:
                        h = p - 2
                        pe.wait_ge(S["wb_ready"], n0 + h + 1)
                        if h >= 2:
                            pe.wait_ge(S["op_lo"], t.op + h - 1)
                        for i in range(2):
                            o = PS[64 * i:64 * i + 64, 6 + p % 2, :]
                            f = (2 * h + i) * 64
                            wt = WB[:, h % 2, 384 * i:384 * i + 384]
                            pe.matmul(o[:, 0:T], V[:, 0, f:f + 64], wt[:, 0:T], start=True, stop=False, **kw)
                            mm = pe.matmul(o[:, P:T], V[:, 1, f:f + 64], wt[:, T:T + P], start=False, stop=True,
                                           **kw)
                        mm.then_inc(S["o_ready"], 1)
                t.att += 8
                residual(1)

            def gating():
                for n in range(4):
                    tokens(n == 0)
                for n in range(2):
                    features()
                pe.wait_ge(S["gvn_ready"], 2)
                pe.wait_ge(S["gtril"], 8)
                for g in range(8):
                    for c in range(2):
                        o = (g % 2) * T + c * P
                        mm = pe.matmul(PS[:, g // 2, o:o + P], GV[:, c, g * P:(g + 1) * P], GW[:, g, :],
                                       start=True, stop=True)
                    if g % 2:
                        mm.then_inc(S["mix_ready"], 1)
                for n in range(2):
                    features()
                t.op += KT
                residual(2)

            def last_mixer():
                def pair():
                    if t.wide == 0:
                        pe.wait_ge(S["pp_taken"], t.pp)
                    if t.wide >= 2:
                        pe.wait_ge(S["wide_taken"], t.wide - 1)
                    t.wide += 1
                    return 4 + 2 * ((t.wide - 1) % 2)

                def unit(kind, first=False):
                    b = pair()
                    slot = unit_ready(t.u)
                    if kind == "tokens":
                        for blk in range(4):
                            for k in range(KT):
                                mm = product(PS[:, b + blk // 2, (blk % 2) * 256:(blk % 2) * 256 + 256],
                                             x(k, blk * P, (blk + 1) * P), w(slot, k * 256, (k + 1) * 256),
                                             k == 0, k == KT - 1)
                    else:
                        n = 2 * T if kind == "both" else T
                        for m in range(2):
                            dst = PS[:, b + m, :] if kind == "both" else PS[:, b, m * T:(m + 1) * T]
                            for k in range(KT):
                                operand(first and m == 0, k)
                                mm = product(dst, w(slot, k * 256 + m * P, k * 256 + m * P + P), x(k, 0, n),
                                             k == 0, k == KT - 1)
                    mm.then_inc(S["w_used"], 1)
                    t.u += 1

                def csum(i, n):
                    pe.wait_ge(S["csq"], i + 1)
                    for k in range(2):
                        mm = pe.matmul(PS[:, i, 0:n], ones, CSQ[:, k, 0:n], start=(k == 0), stop=(k == 1))
                    mm.then_inc(S["csum"], 1)

                unit("both", True)
                t.op += KT
                csum(0, 512)
                unit("one")
                unit("tokens")
                csum(1, T)
                unit("tokens")
                b = pair()
                slot = unit_ready(t.u)
                for k in range(KT):
                    product(PS[0:64, b, :], w(slot, 64 * k, 64 * k + 64), x(k, 0, 512), k == 0, k == KT - 1)
                pe.wait_ge(S["cnormed"], 4)
                pe.wait_ge(S["crms"], 2)
                rw = raw[:, t.u % RING, :]
                for h in range(QHEADS):
                    for part, rows in ((0, P), (1, 64)):
                        for k in range(2):
                            c = 512 + 768 * k + (P * h if part == 0 else 512 + 64 * h)
                            mm = pe.matmul(PS[0:rows, 2 * part + h // 2, (h % 2) * T:(h % 2 + 1) * T],
                                           rw[:, c:c + rows], CQ[:, k, :], start=(k == 0), stop=(k == 1))
                mm.then_inc(S["w_used"], 1)
                t.u += 1
                pe.wait_ge(w_loaded[t.u % RING], 16 * (t.u // RING + 1))
                rw = raw[:, t.u % RING, :]
                for i in range(4):
                    b = pair()
                    for j in range(2):
                        for k in range(2):
                            if i < 2:
                                h = 2 * i + j
                                lhs, rhs = rw[:, D * k + P * h:D * k + P * h + P], CKV[:, k, :]
                            else:
                                blk = 2 * (i - 2) + j
                                lhs, rhs = CKV[:, k, P * blk:P * blk + P], rw[:, D * k + 512:D * k + D]
                            mm = pe.matmul(PS[:, b + j, :], lhs, rhs, start=(k == 0), stop=(k == 1))
                    mm.then_inc(S["kv_part"] if i < 3 else S["w_used"], 1)
                t.u += 1
                pe.wait_ge(S["q_out"], 2)
                pe.wait_ge(S["wide_taken"], 5)
                swap = CST[0:64, CRO:CRO + 64]
                pe.matmul(PS[0:64, 2, 0:T], swap, KPE[0:64, 0:T], start=True, stop=True).then_inc(S["rot"], 1)
                for i in range(2):
                    mm = pe.matmul(PS[0:64, i, :], swap, QR[0:64, 2 * i:2 * i + 2, :], start=True, stop=True)
                mm.then_inc(S["rot"], 1)

                def item(i):
                    if i < 8:
                        h, q = i // 2, slice((i % 2) * P, (i % 2 + 1) * P)
                        if i == 0:
                            pe.wait_ge(S["roped"], 2)
                            pe.wait_ge(S["wide_taken"], 9)
                        if i >= 2:
                            pe.wait_ge(S["mla_p"], i - 1)
                        pe.matmul(PS[:, i % 2, :], QN[:, h, q], KN[:, h, :], start=True, stop=False)
                        pe.matmul(PS[:, i % 2, :], QR[0:64, h, q], KPE[0:64, :], start=False, stop=True)\
                            .then_inc(S["mla_s"], 1)
                    if 1 <= i < 9:
                        j = i - 1
                        pe.wait_ge(S["mla_pn"], j + 1)
                        if j >= 1:
                            pe.wait_ge(S["mla_pt"], j)
                        for k in range(4):
                            mm = pe.transpose(PS[:, 2, k * P:(k + 1) * P], PB[:, j % 2, k * P:(k + 1) * P], ident)
                        mm.then_inc(S["mla_t"], 1)
                    if i >= 2:
                        j = i - 2
                        h = j // 2
                        pe.wait_ge(S["mla_pt"], j + 1)
                        if j >= 1:
                            pe.wait_ge(S["mla_om"], j)
                        for k in range(4):
                            mm = pe.matmul(PS[:, 3, 0:P], V2[:, k, h * P:(h + 1) * P],
                                           PT[:, j % 2, k * P:(k + 1) * P], start=(k == 0), stop=(k == 3))
                        mm.then_inc(S["mla_o"], 1)

                n = 0
                for i in range(6):
                    unit("one" if i < 4 else "both")
                    for _ in range(2 if i < 4 else 1):
                        item(n)
                        n += 1
                for i in range(2):
                    unit("both")

                pe.wait_ge(S["wide_taken"], t.wide)
                pe.wait_ge(S["silu_c"], 2)
                for d in range(2):
                    for g in range(6 * d, 6 * d + 6):
                        modulation(g % 8, g // 8)
                    pe.wait_ge(S["kw_ready"], d + 1)
                    for blk in range(2):
                        for h in range(4):
                            mm = pe.transpose(PS[:, 4 + 2 * d + blk, h * P:(h + 1) * P],
                                              GK[d][:, 1, h, blk * P:(blk + 1) * P], ident)
                    mm.then_inc(S["kwt"], 1)
                for g in range(12, 16):
                    modulation(g % 8, g // 8)
                kwt = W1, W2
                for d in range(2):
                    pe.wait_ge(S["kwt_out"], d + 1)
                    for h in range(4):
                        for blk in range(2):
                            mm = pe.matmul(PS[:, 2 + d, h * P:(h + 1) * P],
                                           kwt[d][:, blk * 512 + h * P:blk * 512 + (h + 1) * P],
                                           HV[:, 2 + blk, h * P:(h + 1) * P], start=(blk == 0), stop=(blk == 1))
                    mm.then_inc(S["s0_sum"], 1)
                for n in (1, 2):
                    modulation_turned(n, 5 + n)
                kw = dict(skip_group_check=True)
                for b in range(2):
                    pe.matmul(PS[:, b, :], ZB[:, 0:P], ZB[:, :], start=True, stop=False, **kw)
                for i in range(4):
                    for d in range(2):
                        c = 3 - i if d else i
                        r = slice(64 * (c % 2), 64 * (c % 2) + 64)
                        tok = slice(CH * c, CH * c + CH)
                        if i == 0:
                            pe.wait_ge(S["s_ready"], 2)
                            pe.wait_ge(S["mod_vec"], 3)
                        for h in range(4):
                            for rows, cols in quarters(d):
                                key = slice(tok.start + rows.start, tok.start + rows.stop)
                                query = slice(tok.start + cols.start, tok.start + cols.stop)
                                mm = pe.matmul(
                                    PS[r.start + rows.start:r.start + rows.stop, 2 + d,
                                       h * CH + cols.start:h * CH + cols.stop],
                                    KA[d][:, h, key], QA[d][:, h, query], start=True, stop=True)
                        mm.then_inc(S["at_sum"], 1)
                        if i < 3:
                            for h in range(4):
                                mm = pe.matmul(PS[r, 4 + d, h * P:(h + 1) * P], GK[d][:, 0, h, tok], ident,
                                               start=True, stop=True)
                            mm.then_inc(S["kd_sum"], 1)
                    for d in range(2):
                        c = 3 - i if d else i
                        r = slice(64 * (c % 2), 64 * (c % 2) + 64)
                        tok = slice(CH * c, CH * c + CH)
                        n = 2 * i + d + 1
                        pe.wait_ge(S["at_out"], n)
                        pe.wait_ge(S["s_ready"], n)
                        for h in range(4):
                            o = PS[:, h // 2, (h % 2) * T + CH * c:(h % 2) * T + CH * c + CH]
                            pe.matmul(o, ST[:, d, h, :], EQ[d][:, h, tok], start=False, stop=False, **kw)
                            mm = pe.matmul(o, HV[:, c // 2, h * P:(h + 1) * P], ATS[:, d, c % 2, h * CH:(h + 1) * CH],
                                           start=False, stop=(i == 3), **kw)
                        if i == 3 and d == 1:
                            mm.then_inc(S["h_out"], 1)
                        if i < 3:
                            pe.wait_ge(S["kd_out"], n)
                            for h in range(4):
                                mm = pe.matmul(PS[:, 6 + d, h * P:(h + 1) * P], KDS[r, d, h * P:(h + 1) * P],
                                               HV[r, c // 2, h * P:(h + 1) * P], start=True, stop=True)
                            mm.then_inc(S["su_sum"], 1)
                pe.wait_ge(S["h_sq"], 1)
                for b in range(2):
                    mm = pe.matmul(PS[:, 2 + b, :], ones, W2[:, 512 * b:512 * b + 512], start=True, stop=True)
                mm.then_inc(S["h_sum"], 1)
                residual(4)

            def turn():
                pe.wait_ge(S["s5_xb"], 4)
                pe.wait_ge(S["acc_taken"], t.acc)
                for i, xb in enumerate((XBR, XBI)):
                    for k in range(KT):
                        for j in range(2):
                            pos = 8 * (k // 2) + 4 * j + 2 * (k % 2)
                            src = xb[:, pos:pos + 2, :].rearrange("p r n -> p (r n)")
                            mm = pe.matmul(PS[64 * j:64 * j + 64, 2 * i + k // 4, (k % 4) * P:(k % 4 + 1) * P],
                                           src, ident, start=True, stop=True)
                mm.then_inc(S["s5_turned"], 1)

            def state_space():
                for n in range(4):
                    features(n == 0)
                    if n == 1:
                        turn()
                t.op += KT
                pe.wait_ge(S["s5_b"], 8)
                pe.wait_ge(S["pp_taken"], t.pp)
                for b in range(9):
                    if b < 8:
                        c, qd = step5(2 * b)
                        if b:
                            pe.wait_ge(S["bu_mult"], 2 * b)
                        for j in range(2):
                            rows = slice(64 * j, 64 * j + 64)
                            for kk in range(2):
                                k = 2 * qd + kk
                                for e in range(2):
                                    o = (2 * kk + e) * 128
                                    for ri, bm in ((0, BRE), (2, BIM)):
                                        mm = pe.matmul(PS[:, ri + j, o:o + 128], bm[rows, k, e, :],
                                                       U5[rows, k, 64 * c:64 * c + 128], start=True, stop=True)
                        mm.then_inc(S["bu_ready"], 1)
                    for s in (2 * b - 2, 2 * b - 1) if b else ():
                        (c, qd), wk = step5(s), W5[s % 3]
                        pe.wait_ge(S["rot_ready"], s + 1)
                        pe.wait_ge(S["x5_ready"], s + 1)
                        if c >= 2 and qd == 0:
                            pe.wait_ge(S["y5_sum"], c - 1)
                        for pos in range(8):
                            k, q = 2 * qd + (pos // 2) % 2, 2 * (pos // 4) + pos % 2
                            dst = PS[32 * q:32 * q + 32, 4 + c % 2, 64 * k:64 * k + 64]
                            col = slice(64 * pos, 64 * pos + 64)
                            for i, (cm, x5) in enumerate(((CRE, 0), (CRE, 2), (CIM, 1), (CIM, 3))):
                                mm = pe.matmul(dst, cm[:, 8 * qd + pos, :], wk[x5][:, col], start=(i == 0),
                                               stop=(i == 3))
                        mm.then_inc(S["y5_ready"], 1)
                    if b < 8:
                        if b == 0:
                            pe.wait_ge(S["silu_c"], 1)
                        modulation(b, 7)
                for c in range(4):
                    pe.wait_ge(S["op_lo"], t.op + c + 1)
                for mp in range(4):
                    features()
                    if mp == 0:
                        modulation_turned(0, 7)
                    features()
                    if mp >= 1:
                        sums(mp - 1)
                sums(3)
                t.op += 4

            pe.wait_ge(S["setup"], 3)
            for mp in range(4):
                sums(mp)
            attention()
            ffn()
            gating()
            ffn()
            state_space()
            ffn()
            attention()

            def context():
                for mp in range(4):
                    sums(mp)
                t.op += KT
            ffn(context)
            for mp in range(4):
                sums(mp)
            last_mixer()
            ffn()

        @block.gpsimd
        def _(pool):
            links = [0]

            def link(ins):
                links[0] += 1
                ins.then_inc(S["s5_step"], 1)
                pool.wait_ge(S["s5_step"], links[0])

            def discretize():
                big = 12582912.0
                pool.wait_ge(S["op_lo"], 5 * KT + 4)

                def b64(v):
                    return v.unsqueeze(2).broadcast_to([P, 32, 64])

                def b16(v):
                    return v.unsqueeze(2).broadcast_to([P, 32, 16])
                pool.wait_ge(S["s5_dt"], 1)
                pool.wait_ge(S["s5_den"], 1)
                link(pool.tensor_scalar(PH, DT, 1.0 / (2 * np.pi), None, ALU.mult))
                link(pool.tensor_tensor(PH, PH, LI, ALU.mult))
                link(pool.tensor_scalar(NN, PH, big, None, ALU.add))
                link(pool.tensor_scalar(NN, NN, big, None, ALU.subtract))
                link(pool.tensor_tensor(PH, PH, NN, ALU.subtract))
                link(pool.tensor_tensor(PHT, b64(PH), rt.unsqueeze(1).broadcast_to([P, 32, 64]), ALU.mult))
                for i, (tab, quarter) in enumerate(((TS, 0.0), (TC, 0.25))):
                    link(pool.tensor_scalar(PHN, PHT, quarter, big, ALU.add, ALU.add))
                    link(pool.tensor_scalar(PHN, PHN, big, None, ALU.subtract))
                    if quarter:
                        link(pool.tensor_scalar(PHT, PHT, quarter, None, ALU.add))
                    pool.tensor_tensor(tab, PHT, PHN, ALU.subtract).then_inc(S["s5_angle"], 1)
                    pool.wait_ge(S["s5_angle"], i + 1)
                link(pool.tensor_tensor(Z5, DT, LR, ALU.mult))
                link(pool.tensor_scalar(Z5, Z5, -87.0, 1.0 / 256, ALU.max, ALU.mult))
                link(pool.tensor_scalar(E5, Z5, 1.0 / 7, 1.0, ALU.mult, ALU.add))
                for n in range(6, 1, -1):
                    link(pool.tensor_tensor(E5, E5, Z5, ALU.mult))
                    link(pool.tensor_scalar(E5, E5, 1.0 / n, 1.0, ALU.mult, ALU.add))
                link(pool.tensor_tensor(E5, E5, Z5, ALU.mult))
                for _ in range(8):
                    link(pool.tensor_scalar(T0, E5, 2.0, None, ALU.add))
                    link(pool.tensor_tensor(E5, E5, T0, ALU.mult))
                link(pool.tensor_scalar(MAG, E5, 1.0, None, ALU.add))
                link(pool.tensor_copy(MG, b64(MAG)))
                link(pool.memset(MG[:, :, 0:1], 0.0))
                pool.wait_ge(S["s5_in"], 16)
                link(pool.memset(AR[:, B0 + 8192:B0 + 10240], 0.0))
                bre, bim, cre, cim = (SBC[:, :, 16 * i:16 * i + 16] for i in range(4))
                for g in range(2):
                    r = slice(64 * g, 64 * g + 64)
                    h = slice(16 * g, 16 * g + 16)
                    pool.tensor_copy(CRE[r, :, h], cre[r])
                    link(pool.tensor_scalar(CIM[r, :, h], cim[r], -1.0, None, ALU.mult))
                pool.wait_ge(S["s5_table"], 2)
                link(pool.tensor_tensor(ARE, MAG, TC[:, :, 1], ALU.mult))
                link(pool.tensor_tensor(AIM, MAG, TS[:, :, 1], ALU.mult))
                link(pool.tensor_tensor(T0, ARE, TC[:, :, 63], ALU.mult))
                link(pool.tensor_tensor(T1, AIM, TS[:, :, 63], ALU.mult))
                link(pool.tensor_tensor(AER, T0, T1, ALU.subtract))
                link(pool.tensor_tensor(T0, ARE, TS[:, :, 63], ALU.mult))
                link(pool.tensor_tensor(T1, AIM, TC[:, :, 63], ALU.mult))
                link(pool.tensor_tensor(AEI, T0, T1, ALU.add))
                link(pool.tensor_scalar(MAG, ARE, -1.0, None, ALU.add))
                link(pool.tensor_tensor(T0, MAG, LR, ALU.mult))
                link(pool.tensor_tensor(T1, AIM, LI, ALU.mult))
                link(pool.tensor_tensor(T0, T0, T1, ALU.add))
                link(pool.tensor_tensor(CFR, T0, DEN, ALU.mult))
                link(pool.tensor_tensor(T0, MAG, LI, ALU.mult))
                link(pool.tensor_tensor(T1, AIM, LR, ALU.mult))
                link(pool.tensor_tensor(T0, T1, T0, ALU.subtract))
                link(pool.tensor_tensor(CFI, T0, DEN, ALU.mult))
                for i, (cf, b) in enumerate(((CFR, bre), (CFI, bim), (CFR, bim), (CFI, bre))):
                    pool.tensor_tensor(BT[i], b16(cf), b, ALU.mult).then_inc(S["s5_bt"], 1)
                pool.wait_ge(S["s5_bt"], 4)
                pool.wait_ge(S["acc_taken"], 8)
                link(pool.memset(AR[:, 4096:6144], 0.0))
                for g in range(2):
                    r = slice(64 * g, 64 * g + 64)
                    h = slice(16 * g, 16 * g + 16)
                    pool.tensor_tensor(XBR[r, :, h], BT[0][r], BT[1][r], ALU.subtract).then_inc(S["s5_xb"], 1)
                    pool.tensor_tensor(XBI[r, :, h], BT[2][r], BT[3][r], ALU.add).then_inc(S["s5_xb"], 1)
                pool.wait_ge(S["s5_xb"], 4)
                pool.memset(AR[:, B0 + 10240:B0 + 14336], 0.0).then_inc(S["s5_clear"], 1)

            discretize()
            for b in range(8):
                for s in (2 * b, 2 * b + 1):
                    wk = W5[s % 3]
                    pool.wait_ge(S["bu_mult"], s + 1)
                    pool.tensor_tensor(wk[0], wk[0], wk[1], ALU.add)
                    pool.tensor_tensor(wk[2], wk[2], wk[3], ALU.subtract).then_inc(S["v_ready"], 1)
                for s in (2 * b, 2 * b + 1):
                    (c, qd), wk = step5(s), W5[s % 3]
                    tc = AR[:, B0 + 512 * qd:B0 + 512 * qd + 512]
                    ts = AR[:, B0 + 2048 + 512 * qd:B0 + 2048 + 512 * qd + 512]
                    pool.wait_ge(S["rot_ready"], s + 1)
                    if c < 3:
                        pool.wait_ge(S["jump_parts"], s + 1 if s < 8 else 9 + (s - 8) // 2)
                    pool.tensor_tensor(wk[1], wk[1], ts, ALU.mult)
                    pool.tensor_tensor(wk[3], wk[3], tc, ALU.mult).then_inc(S["x5_ready"], 1)


def unit_pairs(w, pairs=None):
    k, n = w.shape
    return w.reshape(k // P, P, n // 256, 256).transpose(2, 1, 0, 3).reshape(n // 256, P, -1)


def unit_ffn(w_a, w_g, w_down):
    both = np.stack([w_a.reshape(D, FT, P), w_g.reshape(D, FT, P)], axis=2).reshape(D, FT * 2 * P)
    up, down = unit_pairs(both), w_down.reshape(FT // 2, 2, P, D).transpose(0, 2, 1, 3).reshape(FT // 2, P, -1)
    order = [up[0:2]]
    for h in range(1, FT // 2):
        order += [up[2 * h:2 * h + 2], down[h - 1:h]]
    return np.concatenate(order + [down[-1:]])


def fm(v):
    return v.reshape(-1, P).T


def kernel(**inputs):
    import numpy as _np
    import concourse.bacc as _bacc
    from concourse import mybir as _mybir
    from concourse.bass_utils import run_bass_kernel_spmd as _run

    a = {k: _np.asarray(v) for k, v in inputs.items()}
    ffn = [unit_ffn(a["ffn_w_up"][i][:, :FF], a["ffn_w_up"][i][:, FF:], a["ffn_w_down"][i]) for i in range(4)]
    glu = _np.stack([a["ssm_w_glu"][0][:, :D].reshape(D, KT, P), a["ssm_w_glu"][0][:, D:].reshape(D, KT, P)],
                    axis=2).reshape(D, 2 * D)
    sg = a["sg_w_in"][0]
    mod = unit_pairs(a["w_mod_2"][0])
    stream = [unit_pairs(a["sb_w_qkv"][0]), unit_pairs(a["sb_w_o"][0]), ffn[0],
              unit_pairs(sg[:, D:]), unit_pairs(sg[:, :D]), unit_pairs(a["sg_w_o"][0]), ffn[1],
              unit_pairs(a["ssm_w_in"][0]), mod[:MODS[0][1]], unit_pairs(glu), ffn[2],
              unit_pairs(a["sb_w_qkv"][1]), unit_pairs(a["sb_w_o"][1]), ffn[3]]
    win, wuq, wukv = a["w_in_2"][0], a["w_uq_2"][0], a["w_ukv_2"][0]
    col = lambda i, n: unit_pairs(win[:, i:i + n])
    rows = lambda w: w.reshape(-1, P, w.shape[1]).transpose(1, 0, 2).reshape(P, -1)
    uq = wuq.reshape(256, 4, 192)
    uq = _np.concatenate([uq[:, :, :NOPE].reshape(256, -1), uq[:, :, NOPE:].reshape(256, -1)], axis=1)
    ukv = wukv.reshape(256, 4, 2, P).transpose(0, 2, 1, 3).reshape(256, D)
    stream += [col(256, 256), col(0, 256), col(1088, 512),
               _np.concatenate([rows(win[:, 512:576]), rows(uq)], axis=1)[None], rows(ukv)[None],
               col(576, 512), col(1600, 512), col(2112, 512), col(2624, 512),
               mod[MODS[0][1]:], unit_pairs(a["w_out_2"][0]), unit_ffn(a["w_up_2"][0], a["w_gate_2"][0], a["w_down_2"][0])]
    stream.append(_np.zeros((1, P, UNIT), _np.float32))
    stream = _np.concatenate(stream)
    cw, cb = a["ffn_conv_w"], a["ffn_conv_b"]
    taps = _np.concatenate([cw, cb[:, None]], axis=1).reshape(4, 4, 2, FT, P)
    taps = taps.transpose(4, 0, 3, 2, 1).reshape(P, -1)
    lb = lambda v: v.reshape(2, 4, P).transpose(2, 1, 0).reshape(P, 8)
    order = _np.array([4 * (2 * qd + kk) + 2 * j + e for qd in range(4) for j in range(2)
                       for kk in range(2) for e in range(2)])
    pairs = lambda v: v.reshape(32, P)[order].T
    vec = _np.concatenate([
        fm(a["norm_g"].reshape(-1)), fm(a["final_norm_g"]), fm(a["sg_norm_g"][0]), fm(a["ssm_d"][0]), taps,
        fm(a["b_mod_2"][0]), fm(a["g_norm_mix_2"][0]), fm(a["g_norm_ffn_2"][0]), fm(a["g_q_norm_2"][0]),
        fm(a["g_kv_norm_2"][0]), lb(a["lb_fwd_2"]), lb(a["lb_bwd_2"]), fm(a["g_hgrn_norm_2"][0]),
        fm(a["g_final_2"]),
        _np.stack([fm(a["c_2"][0]), fm(a["c_ctx_2"])], axis=2).reshape(P, 2 * KT),
        _np.full((P, 1), EPS, _np.float32),
        pairs(a["ssm_lam_re"][0].reshape(-1)), pairs(a["ssm_lam_im"][0].reshape(-1)),
        pairs(_np.repeat(a["ssm_log_dt"][0], 64))], axis=1)
    assert vec.shape[1] == NVEC
    i = _np.arange(P)
    swap = _np.zeros((P, 64))
    for m in range(64):
        swap[m + 16 if m % 32 < 16 else m - 16, m] = -1.0 if m % 32 < 16 else 1.0
    inv = (1.0 / 10000.0 ** (_np.arange(0, 32, 2, dtype=_np.float32) / 32)).astype(_np.float32)
    row, colm = _np.arange(T) // 64, _np.arange(T) % 64
    ang = _np.concatenate([inv[:, None] * row[None, :].astype(_np.float32)] * 2
                          + [inv[:, None] * colm[None, :].astype(_np.float32)] * 2)
    ropes = _np.stack([_np.cos(ang), _np.sin(ang)], axis=1).astype(_np.float32)
    tri = 1.0 * (i[:, None] <= i[None, :])
    cst = _np.concatenate([
        _np.eye(P), -1.0 * (i[:, None] >= i[None, :]), -_np.ones((P, P)), _np.ones((P, P)),
        _np.where(i[:, None] < i[None, :], 0.0, -1e30), tri,
        _np.broadcast_to(_np.arange(64), (P, 64)), 1.0 * (i[:, None] % 64 >= _np.arange(64)[None, :]),
        swap], axis=1).astype(_np.float32)
    arrays = {
        "wst": stream, "vec": vec, "cst": cst,
        "x_in": a["x"][0].T.reshape(KT, P, T).transpose(1, 0, 2),
        "sgw": a["sg_w_s"][0].transpose(2, 0, 1),
        "sgb": _np.broadcast_to(a["sg_b"][0], (P, 8, P)),
        "sbc": _np.concatenate([a["ssm_b_re"][0].reshape(32, P, 16), a["ssm_b_im"][0].reshape(32, P, 16),
                                a["ssm_c_re"][0].transpose(0, 2, 1).reshape(32, P, 16),
                                a["ssm_c_im"][0].transpose(0, 2, 1).reshape(32, P, 16)], axis=2)[order].transpose(1, 0, 2),
        "ctxin": a["ctx_2"][0].T.reshape(KT, P, T).transpose(1, 0, 2),
        "ropes": ropes,
    }
    nc = _bacc.Bacc("TRN2", target_bir_lowering=False, num_devices=1)
    arrays = {k: _np.ascontiguousarray(v) for k, v in arrays.items()}
    args = [nc.dram_tensor(k, v.shape, _mybir.dt.from_np(v.dtype), kind="ExternalInput").ap()
            for k, v in arrays.items()]
    args.append(nc.dram_tensor("y_out", (P, KT, T), _mybir.dt.float32, kind="ExternalOutput").ap())
    program(nc, *args)
    r = _run(nc, [arrays], core_ids=[0])
    y = r.results[0]["y_out"]
    return _np.ascontiguousarray(y.transpose(2, 1, 0).reshape(1, T, D))
```
